# Optimizing a Trainium2 kernel written in Bass

```python
import math
import jax, jax.numpy as jnp
from jax import lax
import numpy as np

D_MODEL = 1024
BATCH = 1
SEQ = 512
DEPTH = 2
DEC_BATCH = 1
DEC_SEQ = 256
PAST_LEN = 128

N_MEM = 256
EPS = 1e-6
S5_WIDTH = D_MODEL // 2
S5_GROUP = 16
S5_GROUPS = S5_WIDTH // S5_GROUP
S5_STATE = 64
GLA_HEADS = 4
GLA_DV = (D_MODEL // 2) // GLA_HEADS
GLA_DK = GLA_DV // 2
GLA_RANK = 16
GLA_TAU = 16.0
GLA_CHUNK = 64
GLA_QK = GLA_HEADS * GLA_DK
GLA_V = GLA_HEADS * GLA_DV
EV_COLS = S5_WIDTH + 2 * GLA_QK + 2 * GLA_V + 2 * GLA_RANK
EV_SPLITS = (S5_WIDTH, S5_WIDTH + GLA_QK, S5_WIDTH + 2 * GLA_QK,
             S5_WIDTH + 2 * GLA_QK + GLA_V, S5_WIDTH + 2 * GLA_QK + 2 * GLA_V)
DIFF_HEADS = 8
DIFF_DK = 64
DIFF_DV = 2 * DIFF_DK
Q_BLOCK = 128
X_HEADS = 4
X_DH = D_MODEL // X_HEADS
D_FF = 4 * D_MODEL
N_EVEN = (DEPTH + 1) // 2
N_ODD = DEPTH // 2

kernel_name = "hybrid_s5_gla_diffattn_encoder"

def rms_norm(x, g):
    xf = x.astype(jnp.float32)
    y = xf * lax.rsqrt(jnp.mean(xf * xf, axis=-1, keepdims=True) + EPS)
    return (y * g.astype(jnp.float32)).astype(x.dtype)

def alibi_slopes(n_heads):
    return jnp.asarray(2.0 ** (-8.0 * np.arange(1, n_heads + 1, dtype=np.float32) / n_heads), jnp.float32)

def s5_direction(u, lam_re, lam_im, log_step, b_re, b_im, c_re, c_im, reverse):
    f32 = jnp.float32
    lam = lax.complex(lam_re.astype(f32), lam_im.astype(f32))
    step = jnp.exp(log_step.astype(f32))[:, None]
    lam_bar = jnp.exp(lam * step)
    b = lax.complex(b_re.astype(f32), b_im.astype(f32))
    b_bar = ((lam_bar - 1.0) / lam)[..., None] * b
    c = lax.complex(c_re.astype(f32), c_im.astype(f32))
    bu = jnp.einsum('gpc,blgc->blgp', b_bar, u.astype(jnp.complex64))
    a = jnp.broadcast_to(lam_bar, bu.shape)

    def combine(left, right):
        a_l, b_l = left
        a_r, b_r = right
        return a_r * a_l, a_r * b_l + b_r

    _, states = lax.associative_scan(combine, (a, bu), axis=1, reverse=reverse)
    return jnp.einsum('gcp,blgp->blgc', c, states).real

def s5_mixer(u, lam_re, lam_im, log_step, b_re, b_im, c_re, c_im, d, w_glu):
    bsz, L, _ = u.shape
    ug = u.astype(jnp.float32).reshape(bsz, L, S5_GROUPS, S5_GROUP)
    y = (s5_direction(ug, lam_re[0], lam_im[0], log_step[0], b_re[0], b_im[0], c_re[0], c_im[0], False)
         + s5_direction(ug, lam_re[1], lam_im[1], log_step[1], b_re[1], b_im[1], c_re[1], c_im[1], True)
         + d.astype(jnp.float32) * ug)
    y = jax.nn.gelu(y.reshape(bsz, L, S5_WIDTH))
    y = y * jax.nn.sigmoid(y @ w_glu.astype(jnp.float32))
    return y.astype(u.dtype)

def gla_direction(q, k, v, g):
    bsz, L, H, dk = q.shape
    dv = v.shape[-1]
    C = GLA_CHUNK
    n = L // C
    q = q.reshape(bsz, n, C, H, dk)
    k = k.reshape(bsz, n, C, H, dk)
    v = v.reshape(bsz, n, C, H, dv)
    bcum = jnp.cumsum(g.reshape(bsz, n, C, H, dk), axis=2)
    blast = bcum[:, :, -1:]
    bref = bcum[:, :, C // 2 - 1:C // 2]
    q_rel = q * jnp.exp(bcum - bref)
    k_rel = k * jnp.exp(bref - bcum)
    scores = jnp.einsum('bnihd,bnjhd->bnhij', q_rel, k_rel)
    causal_in_chunk = jnp.tril(jnp.ones((C, C), dtype=bool))
    scores = jnp.where(causal_in_chunk, scores, 0.0)
    o_intra = jnp.einsum('bnhij,bnjhe->bnihe', scores, v)
    k_out = k * jnp.exp(blast - bcum)
    chunk_kv = jnp.einsum('bnjhd,bnjhe->bnhde', k_out, v)
    decay = jnp.exp(blast[:, :, 0])

    def step(S, inp):
        dec, kv = inp
        return dec[..., None] * S + kv, S

    S0 = jnp.zeros((bsz, H, dk, dv), jnp.float32)
    _, S_prev = lax.scan(step, S0, (jnp.moveaxis(decay, 1, 0), jnp.moveaxis(chunk_kv, 1, 0)))
    S_prev = jnp.moveaxis(S_prev, 0, 1)
    o_inter = jnp.einsum('bnihd,bnhde->bnihe', q * jnp.exp(bcum), S_prev)
    return (o_intra + o_inter).reshape(bsz, L, H, dv)

def gla_mixer(q, k, v, og, glr, w_gate, b_gate, norm_g):
    f32 = jnp.float32
    bsz, L, _ = q.shape
    qh = q.astype(f32).reshape(bsz, L, GLA_HEADS, GLA_DK) * (GLA_DK ** -0.5)
    kh = k.astype(f32).reshape(bsz, L, GLA_HEADS, GLA_DK)
    vh = v.astype(f32).reshape(bsz, L, GLA_HEADS, GLA_DV)
    lr = glr.astype(f32).reshape(bsz, L, 2, GLA_RANK)
    logit = jnp.einsum('blzr,zrk->blzk', lr, w_gate.astype(f32)) + b_gate.astype(f32)
    g = (jax.nn.log_sigmoid(logit) / GLA_TAU).reshape(bsz, L, 2, GLA_HEADS, GLA_DK)
    flip = lambda t: jnp.flip(t, axis=1)
    o = (gla_direction(qh, kh, vh, g[:, :, 0])
         + flip(gla_direction(flip(qh), flip(kh), flip(vh), flip(g[:, :, 1]))))
    o = rms_norm(o, norm_g).reshape(bsz, L, GLA_V)
    return (o * jax.nn.silu(og.astype(f32))).astype(q.dtype)

def diff_attention(h, w_in, q_norm, k_norm, lq1, lk1, lq2, lk2, sub_norm, lambda_init):
    f32 = jnp.float32
    bsz, L, _ = h.shape
    proj = (h @ w_in).astype(f32)
    q, k, v = jnp.split(proj, 3, axis=-1)
    q = rms_norm(q.reshape(bsz, L, DIFF_HEADS, 2, DIFF_DK), q_norm) * (DIFF_DK ** -0.5)
    k = rms_norm(k.reshape(bsz, L, DIFF_HEADS, 2, DIFF_DK), k_norm)
    v = v.reshape(bsz, L, DIFF_HEADS, DIFF_DV)
    lam = (jnp.exp(jnp.sum(lq1.astype(f32) * lk1.astype(f32)))
           - jnp.exp(jnp.sum(lq2.astype(f32) * lk2.astype(f32))) + lambda_init)
    slopes = alibi_slopes(DIFF_HEADS)[:, None, None]
    nblk = L // Q_BLOCK
    qb = jnp.moveaxis(q.reshape(bsz, nblk, Q_BLOCK, DIFF_HEADS, 2, DIFF_DK), 1, 0)
    kpos = jnp.arange(L, dtype=f32)

    def block(args):
        qblk, i = args
        qpos = (i * Q_BLOCK + jnp.arange(Q_BLOCK)).astype(f32)
        bias = -slopes * jnp.abs(qpos[:, None] - kpos[None, :])
        s = jnp.einsum('bqhzd,bkhzd->bzhqk', qblk, k) + bias[None, None]
        p = jax.nn.softmax(s, axis=-1)
        attn = p[:, 0] - lam * p[:, 1]
        return jnp.einsum('bhqk,bkhe->bqhe', attn, v)

    o = lax.map(block, (qb, jnp.arange(nblk)))
    o = jnp.moveaxis(o, 0, 1).reshape(bsz, L, DIFF_HEADS, DIFF_DV)
    o = rms_norm(o, sub_norm) * (1.0 - lambda_init)
    return o.reshape(bsz, L, DIFF_HEADS * DIFF_DV).astype(h.dtype)

def cross_attention(h, m, w_q, w_kv, w_o, q_norm, k_norm):
    f32 = jnp.float32
    bsz, L, _ = h.shape
    q = rms_norm((h @ w_q).astype(f32).reshape(bsz, L, X_HEADS, X_DH), q_norm) * (X_DH ** -0.5)
    kv = (m @ w_kv).astype(f32).reshape(bsz, m.shape[1], 2, X_HEADS, X_DH)
    k = rms_norm(kv[:, :, 0], k_norm)
    v = kv[:, :, 1]
    p = jax.nn.softmax(jnp.einsum('bqhd,bmhd->bhqm', q, k), axis=-1)
    o = jnp.einsum('bhqm,bmhd->bqhd', p, v).reshape(bsz, L, D_MODEL)
    return o.astype(h.dtype) @ w_o

def trunk(x, mem, p):
    for layer in range(DEPTH):
        h = rms_norm(x, p['norm_mix'][layer])
        if layer % 2 == 0:
            e = layer // 2
            proj = h @ p['ev_w_in'][e]
            u, q, k, v, og, glr = jnp.split(proj, EV_SPLITS, axis=-1)
            y_s5 = s5_mixer(u, p['s5_lambda_re'][e], p['s5_lambda_im'][e], p['s5_log_step'][e],
                            p['s5_b_re'][e], p['s5_b_im'][e], p['s5_c_re'][e], p['s5_c_im'][e],
                            p['s5_d'][e], p['s5_w_glu'][e])
            y_gla = gla_mixer(q, k, v, og, glr, p['gla_w_gate'][e], p['gla_b_gate'][e], p['gla_norm'][e])
            y = jnp.concatenate([y_s5, y_gla], axis=-1).astype(x.dtype) @ p['ev_w_out'][e]
        else:
            o = layer // 2
            lambda_init = 0.8 - 0.6 * math.exp(-0.3 * layer)
            y = diff_attention(h, p['od_w_in'][o], p['diff_q_norm'][o], p['diff_k_norm'][o],
                               p['diff_lambda_q1'][o], p['diff_lambda_k1'][o],
                               p['diff_lambda_q2'][o], p['diff_lambda_k2'][o],
                               p['diff_norm'][o], lambda_init) @ p['od_w_out'][o]
        x = x + y.astype(x.dtype)
        h = rms_norm(x, p['norm_cross'][layer])
        m = rms_norm(mem, p['norm_mem'][layer])
        x = x + cross_attention(h, m, p['x_w_q'][layer], p['x_w_kv'][layer], p['x_w_o'][layer],
                                p['x_q_norm'][layer], p['x_k_norm'][layer]).astype(x.dtype)
        h = rms_norm(x, p['norm_mlp'][layer])
        x = x + (jnp.square(jax.nn.relu(h @ p['mlp_w1'][layer])) @ p['mlp_w2'][layer]).astype(x.dtype)
    return x

def setup_inputs(seed: int = 0) -> dict:
    key = jax.random.key(seed)
    ks = iter(jax.random.split(key, 64))
    f32 = jnp.float32
    nrm = lambda shape, scale: scale * jax.random.normal(next(ks), shape, f32)
    gain = lambda shape: 1.0 + 0.02 * jax.random.normal(next(ks), shape, f32)
    E, O, G, P = N_EVEN, N_ODD, S5_GROUPS, S5_STATE
    n_idx = jnp.arange(P, dtype=f32)
    return {
        'x_prompt': nrm((BATCH, SEQ, D_MODEL), 1.0),
        'x_sample': nrm((DEC_BATCH, DEC_SEQ, D_MODEL), 1.0),
        'mem_prompt': nrm((BATCH, N_MEM, D_MODEL), 1.0),
        'mem_sample': nrm((DEC_BATCH, N_MEM, D_MODEL), 1.0),
        'norm_mix': gain((DEPTH, D_MODEL)),
        'norm_cross': gain((DEPTH, D_MODEL)),
        'norm_mem': gain((DEPTH, D_MODEL)),
        'norm_mlp': gain((DEPTH, D_MODEL)),
        'ev_w_in': nrm((E, D_MODEL, EV_COLS), D_MODEL ** -0.5),
        'ev_w_out': nrm((E, D_MODEL, D_MODEL), D_MODEL ** -0.5),
        's5_lambda_re': -0.5 + nrm((E, 2, G, P), 0.01),
        's5_lambda_im': math.pi * n_idx + nrm((E, 2, G, P), 0.01),
        's5_log_step': jax.random.uniform(next(ks), (E, 2, G), f32, math.log(1e-3), math.log(1e-1)),
        's5_b_re': nrm((E, 2, G, P, S5_GROUP), (2.0 * S5_GROUP) ** -0.5),
        's5_b_im': nrm((E, 2, G, P, S5_GROUP), (2.0 * S5_GROUP) ** -0.5),
        's5_c_re': nrm((E, 2, G, S5_GROUP, P), (2.0 * P) ** -0.5),
        's5_c_im': nrm((E, 2, G, S5_GROUP, P), (2.0 * P) ** -0.5),
        's5_d': nrm((E, G, S5_GROUP), 1.0),
        's5_w_glu': nrm((E, S5_WIDTH, S5_WIDTH), S5_WIDTH ** -0.5),
        'gla_w_gate': nrm((E, 2, GLA_RANK, GLA_QK), GLA_RANK ** -0.5),
        'gla_b_gate': nrm((E, 2, GLA_QK), 0.1),
        'gla_norm': gain((E, GLA_DV)),
        'od_w_in': nrm((O, D_MODEL, 3 * D_MODEL), D_MODEL ** -0.5),
        'od_w_out': nrm((O, D_MODEL, D_MODEL), D_MODEL ** -0.5),
        'diff_q_norm': gain((O, DIFF_DK)),
        'diff_k_norm': gain((O, DIFF_DK)),
        'diff_lambda_q1': nrm((O, DIFF_DK), 0.1),
        'diff_lambda_k1': nrm((O, DIFF_DK), 0.1),
        'diff_lambda_q2': nrm((O, DIFF_DK), 0.1),
        'diff_lambda_k2': nrm((O, DIFF_DK), 0.1),
        'diff_norm': gain((O, DIFF_DV)),
        'x_w_q': nrm((DEPTH, D_MODEL, D_MODEL), D_MODEL ** -0.5),
        'x_w_kv': nrm((DEPTH, D_MODEL, 2 * D_MODEL), D_MODEL ** -0.5),
        'x_w_o': nrm((DEPTH, D_MODEL, D_MODEL), D_MODEL ** -0.5),
        'x_q_norm': gain((DEPTH, X_DH)),
        'x_k_norm': gain((DEPTH, X_DH)),
        'mlp_w1': nrm((DEPTH, D_MODEL, D_FF), D_MODEL ** -0.5),
        'mlp_w2': nrm((DEPTH, D_FF, D_MODEL), D_FF ** -0.5),
    }

def reference(x_prompt, x_sample, mem_prompt, mem_sample, norm_mix, norm_cross, norm_mem, norm_mlp,
              ev_w_in, ev_w_out, s5_lambda_re, s5_lambda_im, s5_log_step, s5_b_re, s5_b_im,
              s5_c_re, s5_c_im, s5_d, s5_w_glu, gla_w_gate, gla_b_gate, gla_norm,
              od_w_in, od_w_out, diff_q_norm, diff_k_norm, diff_lambda_q1, diff_lambda_k1,
              diff_lambda_q2, diff_lambda_k2, diff_norm, x_w_q, x_w_kv, x_w_o, x_q_norm, x_k_norm,
              mlp_w1, mlp_w2):
    params = dict(norm_mix=norm_mix, norm_cross=norm_cross, norm_mem=norm_mem, norm_mlp=norm_mlp,
                  ev_w_in=ev_w_in, ev_w_out=ev_w_out, s5_lambda_re=s5_lambda_re,
                  s5_lambda_im=s5_lambda_im, s5_log_step=s5_log_step, s5_b_re=s5_b_re, s5_b_im=s5_b_im,
                  s5_c_re=s5_c_re, s5_c_im=s5_c_im, s5_d=s5_d, s5_w_glu=s5_w_glu,
                  gla_w_gate=gla_w_gate, gla_b_gate=gla_b_gate, gla_norm=gla_norm,
                  od_w_in=od_w_in, od_w_out=od_w_out, diff_q_norm=diff_q_norm, diff_k_norm=diff_k_norm,
                  diff_lambda_q1=diff_lambda_q1, diff_lambda_k1=diff_lambda_k1,
                  diff_lambda_q2=diff_lambda_q2, diff_lambda_k2=diff_lambda_k2, diff_norm=diff_norm,
                  x_w_q=x_w_q, x_w_kv=x_w_kv, x_w_o=x_w_o, x_q_norm=x_q_norm, x_k_norm=x_k_norm,
                  mlp_w1=mlp_w1, mlp_w2=mlp_w2)
    y_prompt = trunk(x_prompt, mem_prompt, params)
    y_sample = trunk(x_sample, mem_sample, params)
    return (y_prompt, y_sample)


_drawn_inputs = setup_inputs


def setup_inputs(seed=0):
    import zlib

    import numpy as np

    out = dict(_drawn_inputs(seed))
    spreads = {}
    factors = {'norm_cross': 8.0,
     'norm_mem': 8.0,
     's5_lambda_re': 8.0,
     's5_b_re': 3.555,
     's5_b_im': 3.639,
     's5_c_re': 3.57,
     's5_c_im': 3.621,
     'gla_b_gate': 3.125,
     'gla_norm': 6.203,
     'diff_q_norm': 8.0,
     'diff_k_norm': 8.0,
     'diff_lambda_q2': 4.173,
     'diff_norm': 7.661,
     'x_q_norm': 8.0,
     'x_k_norm': 8.0}
    for name, (base, spread) in spreads.items():
        noise = np.random.default_rng([zlib.crc32(name.encode()), seed]).standard_normal(out[name].shape)
        drawn = base * np.exp(spread * noise) if base else spread * noise
        out[name] = __import__('jax').numpy.asarray(drawn.astype(out[name].dtype))
    for name, factor in factors.items():
        out[name] = (out[name] * factor).astype(out[name].dtype)
    return out
```

```python
import math
from contextlib import ExitStack

import numpy as np

import concourse.bass as bass
from concourse import mybir

F32 = mybir.dt.float32
U8 = mybir.dt.uint8
ALU = mybir.AluOpType
ACT = mybir.ActivationFunctionType
AX = mybir.AxisListType

P = 128
D = 1024
KT = D // P
TP, TS = 512, 256
T = TP + TS
TT = T // P
M = 512
UC = 256
RING = 4
DEPTH = 2
FB = 4
EPS = 1e-6
G, NS, GC = 32, 64, 16
SC = 8
NCH = T // SC
GB = 8
NB = G // GB
LAG = 2 * SC - 1
POS = SC + 2
GH, DK, DV, CH = 4, 64, 128, 64
NC12 = T // CH
DH = 8
XH = 4
LAMBDA_INIT = 0.8 - 0.6 * math.exp(-0.3)
DIST = 896
MAGIC = 12582912.0
TWO_PI_HI = 6.28125
TWO_PI_LO = 2 * math.pi - 6.28125


def _param_columns():
    widths = [("mix0", 8), ("mix1", 8), ("cross0", 8), ("cross1", 8), ("mem0", 8), ("mem1", 8), ("mlp0", 8),
              ("mlp1", 8), ("xq0", 2), ("xq1", 2), ("xk0", 2), ("xk1", 2), ("dq", 1), ("dk", 1), ("dnorm", 1),
              ("gnorm", 1), ("lq", 2), ("lk", 2), ("bgate", 4), ("lre", 32), ("lim", 32), ("lstep", 32), ("s5d", 32),
              ("eps", 1), ("one", 1), ("chunkmask", 96), ("ident", 128), ("ones", 128), ("ones64", 128), ("dist", DIST), ("masks", 256)]
    at, out = 0, {}
    for name, w in widths:
        out[name] = (at, w)
        at += w
    return out, at


COLS, NPAR = _param_columns()


class Signal:

    def __init__(self, ctx, nc, name):
        self.sem = ctx.enter_context(nc.semaphore(name))
        self.base = 0

    def at(self, n):
        return self.base + n


class Chain:

    def __init__(self, sig):
        self.sig = sig
        self.n = 0
        self.eng = None
        self.reg = None

    def start(self, eng):
        self.eng, self.n = eng, 0

    def loop(self, reg, per):
        self.reg, self.per, self.in_loop = reg, per, 0

    def end_loop(self, times):
        assert self.in_loop == self.per, (self.in_loop, self.per)
        self.n += self.per * times
        self.reg = None

    def __call__(self, ins):
        ins.then_inc(self.sig.sem, 1)
        if self.reg is None:
            self.n += 1
            self.eng.wait_ge(self.sig.sem, self.sig.base + self.n)
        else:
            self.in_loop += 1
            self.eng.wait_ge(self.sig.sem, self.reg * self.per + (self.sig.base + self.n + self.in_loop))

    def close(self):
        self.sig.base += self.n
        self.n = 0


def build(nc, params, x_in, mem_in, wstream, wglr_in, wglu_in, wgate_in, bc_in, u_dram, y_dram, out):
    ctx = ExitStack()
    with ctx:
        def sb(name, shape, dt=F32, on=ctx):
            return on.enter_context(nc.sbuf_tensor(name, shape, dt))

        def sig(name):
            return Signal(ctx, nc, name)

        par = sb("par", [P, NPAR])
        x = sb("x", [P, KT, T])
        act = sb("act", [P, KT, T])
        b1 = sb("b1", [P, KT, T])
        b2 = sb("b2", [P, KT, T])
        b3 = sb("b3", [P, KT, T])
        ring = sb("ring", [P, RING, KT, UC])
        rstd = sb("rstd", [P, T])
        sq = sb("sq", [P, 2, T])
        gains = sb("gains", [P, 8])
        ps = ctx.enter_context(nc.psum_tensor("ps", [P, 8, 512], F32))

        def pcol(name, lo=0, n=None):
            a, w = COLS[name]
            return par[:, a + lo:a + lo + (w if n is None else n)]

        ident, ones, ones64 = pcol("ident"), pcol("ones"), pcol("ones64")

        def banks(b, n=T):
            return ps[:, b:b + 2, :].rearrange("p b n -> p (b n)")[:, 0:n]

        loaded = sig("loaded")
        w_loaded = [sig(f"w_loaded{s}") for s in range(RING)]
        tile_done = sig("tile_done")
        tile_free = sig("tile_free")
        act_ready = sig("act_ready")
        sq_ready = sig("sq_ready")
        sq_used = sig("sq_used")
        root_ready = sig("root_ready")
        normed = sig("normed")
        hid_free = sig("hid_free")
        hid_ready = sig("hid_ready")
        dchain = sig("dchain")
        achain = sig("achain")
        pchain = sig("pchain")
        dve_chain, act_chain, pool_chain = Chain(dchain), Chain(achain), Chain(pchain)
        ev = {n: sig(n) for n in ("ev0", "ev1", "ev2", "ev3", "ev4", "ev5", "ev6", "ev7", "ev8", "ev9", "ev10",
                                  "ev11", "ev12", "ev13", "ev14", "ev15")}
        dma = {n: sig(n) for n in ("dma0", "dma1", "dma2", "dma3")}
        state = {"G": 0}

        NG = wstream.shape[0] // RING

        def sp_weights(sp, n):
            g0 = state["G"]
            n_load = min(n, NG - 1 - g0)

            def one(g):
                for s in range(RING):
                    sp.wait_ge(tile_done.sem, g * 8 + (tile_done.base + 2 * s + 2))
                    sp.dma_start(ring[:, s, :, :], wstream[bass.ds(g * RING + ((g0 + 1) * RING + s), 1)]
                                 .rearrange("a p n -> p (a n)").rearrange("p (k n) -> p k n", k=KT))\
                        .then_inc(w_loaded[s].sem, 16)
            if n_load > 1:
                with sp.Fori(0, n_load, 1) as g:
                    one(g)
            elif n_load == 1:
                one(0)

        def pe_product(pe, rhs, kind, g=0, first_wait=None, ready=None, ready_at=0, cols=T,
                       free_wait=None):
            for s in range(RING):
                for half in range(2):
                    n = 2 * s + half
                    if half == 0:
                        pe.wait_ge(w_loaded[s].sem, g * 16 + (16 * (state["G"] + 1)))
                    if free_wait is not None:
                        free_wait(n)
                    elif n >= 2 or g > 0 or tile_free.base > 0:
                        pe.wait_ge(tile_free.sem, tile_free.base + g * 8 + n - 1)
                    bank = 2 * half
                    if kind[s] == "f":
                        for k in range(KT):
                            if n == 0 and ready is not None:
                                pe.wait_ge(ready.sem, ready_at + (ready.base + k + 1))
                            lhs = ring[:, s, k, P * half:P * half + P]
                            last = nc.tensor.matmul(ps[:, bank, :], lhs, rhs[:, k, 0:512],
                                                    start=(k == 0), stop=(k == KT - 1))
                            if cols > 512:
                                last = nc.tensor.matmul(ps[:, bank + 1, 0:cols - 512], lhs, rhs[:, k, 512:cols],
                                                        start=(k == 0), stop=(k == KT - 1))
                    else:
                        per = cols // P // 2
                        if n == 0 and ready is not None:
                            pe.wait_ge(ready.sem, ready_at + (ready.base + KT))
                        for j in range(per):
                            tok = (half * per + j) * P
                            dst = banks(bank, 1024)[:, j * UC:(j + 1) * UC]
                            for k in range(KT):
                                last = nc.tensor.matmul(dst, rhs[:, k, tok:tok + P], ring[:, s, k, :],
                                                        start=(k == 0), stop=(k == KT - 1))
                    last.then_inc(tile_done.sem, 1)

        def close_products(n, n_free=None):
            tile_done.base += 8 * n
            tile_free.base += 8 * (n if n_free is None else n_free)
            state["G"] += n

        def wait_tile(eng, n, g=0):
            eng.wait_ge(tile_done.sem, g * 8 + (tile_done.base + n + 1))

        def act_norm(eng, src, cols=T, ready=None):
            for k in range(KT):
                if k >= 2:
                    eng.wait_ge(sq_used.sem, sq_used.at(k - 1))
                if ready is not None and k == 0:
                    eng.wait_ge(*ready)
                nc.scalar.activation(sq[:, k % 2, 0:cols], src[:, k, 0:cols], ACT.Square).then_inc(sq_ready.sem, 1)
            eng.wait_ge(sq_used.sem, sq_used.at(KT))
            nc.scalar.activation(rstd[:, 0:cols], banks(4, cols), ACT.Sqrt, bias=pcol("eps"), scale=1.0 / D)\
                .then_inc(root_ready.sem, 1)

        def pe_norm(eng, cols=T):
            for k in range(KT):
                eng.wait_ge(sq_ready.sem, sq_ready.at(k + 1))
                last = nc.tensor.matmul(ps[:, 4, 0:512], ones, sq[:, k % 2, 0:512], start=(k == 0), stop=(k == KT - 1))
                if cols > 512:
                    last = nc.tensor.matmul(ps[:, 5, 0:cols - 512], ones, sq[:, k % 2, 512:cols],
                                            start=(k == 0), stop=(k == KT - 1))
                last.then_inc(sq_used.sem, 1)

        def dve_norm(eng, src, gain, dst, cols=T):
            eng.wait_ge(root_ready.sem, root_ready.at(1))
            dve_chain(nc.vector.reciprocal(rstd[:, 0:cols], rstd[:, 0:cols]))
            for k in range(KT):
                nc.vector.scalar_tensor_tensor(dst[:, k, 0:cols], src[:, k, 0:cols], pcol(gain, k, 1), rstd[:, 0:cols],
                                               ALU.mult, ALU.mult).then_inc(act_ready.sem, 1)

        def close_norm():
            sq_ready.base += KT
            sq_used.base += KT
            root_ready.base += 1
            act_ready.base += KT

        def head_norm_stage(items, mat, width, cols=T, extra=None):
            n_items = len(items)

            with nc.Block() as block:
                @block.scalar
                def _(a):
                    c = 0
                    for i, (srcs, gn, dsts) in enumerate(items):
                        for j, s in enumerate(srcs):
                            if c >= 2:
                                a.wait_ge(sq_used.sem, sq_used.at(c - 1))
                            nc.scalar.activation(sq[:, c % 2, 0:cols], s, ACT.Square).then_inc(sq_ready.sem, 1)
                            c += 1
                        a.wait_ge(sq_used.sem, sq_used.at(c))
                        if i >= 1:
                            a.wait_ge(normed.sem, normed.at(i))
                        nc.scalar.activation(rstd[:, 0:cols], banks(4 + 2 * (i % 2), cols), ACT.Sqrt, bias=pcol("eps"),
                                             scale=1.0 / width).then_inc(root_ready.sem, 1)

                @block.tensor
                def _(pe):
                    c = 0
                    for i, (srcs, gn, dsts) in enumerate(items):
                        if i >= 2:
                            pe.wait_ge(root_ready.sem, root_ready.at(i - 1))
                        for j, s in enumerate(srcs):
                            pe.wait_ge(sq_ready.sem, sq_ready.at(c + 1))
                            st, sp_ = j == 0, j == len(srcs) - 1
                            b = 4 + 2 * (i % 2)
                            last = nc.tensor.matmul(ps[:, b, :], mat, sq[:, c % 2, 0:512], start=st, stop=sp_)
                            if cols > 512:
                                last = nc.tensor.matmul(ps[:, b + 1, 0:cols - 512], mat, sq[:, c % 2, 512:cols],
                                                        start=st, stop=sp_)
                            last.then_inc(sq_used.sem, 1)
                            c += 1

                @block.vector
                def _(v):
                    dve_chain.start(v)
                    for i, (srcs, gn, dsts) in enumerate(items):
                        v.wait_ge(root_ready.sem, root_ready.at(i + 1))
                        dve_chain(nc.vector.reciprocal(rstd[:, 0:cols], rstd[:, 0:cols]))
                        for s, g_, d in zip(srcs, gn, dsts):
                            last = nc.vector.scalar_tensor_tensor(d, s, g_, rstd[:, 0:cols], ALU.mult, ALU.mult)
                        last.then_inc(normed.sem, 1)
                        if extra is not None:
                            extra(v, i)
                    dve_chain.close()
            n_sq = sum(len(i[0]) for i in items)
            sq_ready.base += n_sq
            sq_used.base += n_sq
            root_ready.base += n_items
            normed.base += n_items

        with nc.Block() as block:
            @block.sync
            def _(sp):
                sp.dma_start(par[:, :], params).then_inc(loaded.sem, 16)
                sp.dma_start(x[:, :, :], x_in.rearrange("(k p) t -> p k t", p=P)).then_inc(loaded.sem, 16)
                for s in range(RING):
                    sp.dma_start(ring[:, s, :, :], wstream[s].rearrange("p (k n) -> p k n", k=KT))\
                        .then_inc(w_loaded[s].sem, 16)
                sp.wait_ge(loaded.sem, 32)

            @block.vector
            def _(v):
                v.wait_ge(loaded.sem, 32)
                nc.vector.tensor_scalar(gains[:, 0:1], pcol("dq"), float(64 ** -0.5), None, ALU.mult).then_inc(ev["ev0"].sem, 1)
                nc.vector.tensor_scalar(gains[:, 1:2], pcol("dnorm"), 1.0 - LAMBDA_INIT, None, ALU.mult).then_inc(ev["ev0"].sem, 1)
                nc.vector.tensor_scalar(gains[:, 2:4], pcol("xq0"), 1.0 / 16.0, None, ALU.mult).then_inc(ev["ev0"].sem, 1)
                nc.vector.tensor_scalar(gains[:, 4:6], pcol("xq1"), 1.0 / 16.0, None, ALU.mult).then_inc(ev["ev0"].sem, 1)
                v.wait_ge(ev["ev0"].sem, 4)
        loaded.base += 32
        ev["ev0"].base += 4

        def product_stage(rhs, kinds, evac, norm=None, cols=T, evac_engine="vector",
                          dve_pre=None, act_pre=None, dve_post=None):
            n = len(kinds)
            with nc.Block() as block:
                @block.sync
                def _(sp):
                    sp_weights(sp, n)

                @block.tensor
                def _(pe):
                    if norm is not None:
                        pe_norm(pe, cols)
                    for g in range(n):
                        pe_product(pe, rhs, kinds[g], g, cols=cols,
                                   ready=act_ready if norm is not None and g == 0 else None)

                @block.vector
                def _(v):
                    dve_chain.start(v)
                    if dve_pre is not None:
                        dve_pre(v)
                    if norm is not None:
                        dve_norm(v, norm[0], norm[1], rhs, cols)
                    if dve_post is not None:
                        dve_post(v)
                    if evac_engine == "vector":
                        for g in range(n):
                            for i in range(8):
                                wait_tile(v, i, g)
                                evac(v, g, i)
                    dve_chain.close()

                @block.scalar
                def _(a):
                    if act_pre is not None:
                        act_pre(a)
                    if norm is not None:
                        act_norm(a, norm[0], cols)
                    if evac_engine == "scalar":
                        for g in range(n):
                            for i in range(8):
                                wait_tile(a, i, g)
                                evac(a, g, i)
            if norm is not None:
                close_norm()
            close_products(n)

        def free(ins):
            return ins.then_inc(tile_free.sem, 1)

        def add_residual(v, g, i):
            free(nc.vector.tensor_tensor(x[:, i, :], banks(2 * (i % 2)), x[:, i, :], ALU.add))

        def mlp(layer):
            with nc.Block() as block:
                @block.sync
                def _(sp):
                    sp_weights(sp, 2 * FB)

                @block.tensor
                def _(pe):
                    pe_norm(pe)
                    pe.wait_ge(act_ready.sem, act_ready.at(KT))
                    with pe.Fori(0, FB, 1) as fb:
                        def up_wait(n):
                            if n < 2:
                                pe.wait_ge(tile_free.sem, fb * 8 + (tile_free.base + n - 1))
                            else:
                                pe.wait_ge(hid_free.sem, fb * 8 + (hid_free.base + n - 1))

                        def down_wait(n):
                            if n < 2:
                                pe.wait_ge(hid_free.sem, fb * 8 + (hid_free.base + 8 + n - 1))
                            else:
                                pe.wait_ge(tile_free.sem, fb * 8 + (tile_free.base + n - 1))
                        pe_product(pe, act, "ffff", fb * 2, free_wait=up_wait)
                        pe_product(pe, b1, "ffff", fb * 2 + 1, ready=hid_ready, ready_at=fb * KT, free_wait=down_wait)

                @block.vector
                def _(v):
                    dve_chain.start(v)
                    dve_norm(v, x, f"mlp{layer}", act)
                    with v.Fori(0, FB, 1) as fb:
                        for i in range(8):
                            wait_tile(v, i, fb * 2 + 1)
                            add_residual(v, 0, i)
                    dve_chain.close()

                @block.scalar
                def _(a):
                    act_norm(a, x)
                    with a.Fori(0, FB, 1) as fb:
                        for i in range(8):
                            wait_tile(a, i, fb * 2)
                            nc.scalar.activation(sq[:, i % 2, :], banks(2 * (i % 2)), ACT.Relu).then_inc(hid_free.sem, 1)
                            a.wait_ge(hid_free.sem, fb * 8 + (hid_free.base + i + 1))
                            nc.scalar.activation(b1[:, i, :], sq[:, i % 2, :], ACT.Square).then_inc(hid_ready.sem, 1)
            close_norm()
            close_products(2 * FB, FB)
            hid_free.base += 8 * FB
            hid_ready.base += KT * FB

        def cross(layer):
            local = ExitStack()
            memT, mkv = b1, b2
            km = b3[:, 0:6, :].rearrange("p k t -> p (k t)")[:, 0:KT * M].rearrange("p (k m) -> p k m", k=KT)
            vm = sb(f"vm{layer}", [P, 4, D], on=local)
            s_sb = sb(f"xs{layer}", [P, TT, 256], on=local)
            pt = sb(f"xpt{layer}", [P, 2, T], on=local)
            st = sb(f"xst{layer}", [P, 4, TT], on=local)
            mem = b1[:, 0:6, :].rearrange("p k t -> p (k t)")[:, 0:KT * M].rearrange("p (k m) -> p k m", k=KT)
            mact = b2[:, 0:6, :].rearrange("p k t -> p (k t)")[:, 0:KT * M].rearrange("p (k m) -> p k m", k=KT)
            ld = dma["dma0"]
            with nc.Block() as block:
                @block.sync
                def _(sp):
                    sp.dma_start(mem, mem_in.rearrange("(k p) t -> p k t", p=P)).then_inc(ld.sem, 16)
                    sp.wait_ge(ld.sem, ld.at(16))
            ld.base += 16

            def evac_mem(a, g, i):
                if g == 0:
                    free(nc.scalar.activation(km[:, i, :], ps[:, 2 * (i % 2), :], ACT.Copy))
                else:
                    s, half = i // 2, i % 2
                    free(nc.scalar.activation(vm[:, 2 * half:2 * half + 2, s * UC:(s + 1) * UC],
                                              ps[:, 2 * half, :].rearrange("p (j n) -> p j n", j=2), ACT.Copy))
            product_stage(mact, ["ffff", "tttt"], evac_mem, norm=(mem, f"mem{layer}"), cols=M, evac_engine="scalar")
            head_norm_stage([([km[:, 2 * h + j, :] for j in range(2)], [pcol(f"xk{layer}", j, 1) for j in range(2)],
                              [km[:, 2 * h + j, :] for j in range(2)]) for h in range(XH)], ones, 256, cols=M)

            def evac_q(a, g, i):
                free(nc.scalar.activation(b1[:, i, :], banks(2 * (i % 2)), ACT.Copy))
            product_stage(act, ["ffff"], evac_q, norm=(x, f"cross{layer}"), evac_engine="scalar")
            head_norm_stage([([b1[:, 2 * h + j, :] for j in range(2)], [gains[:, 2 + 2 * layer + j:3 + 2 * layer + j] for j in range(2)],
                              [b1[:, 2 * h + j, :] for j in range(2)]) for h in range(XH)], ones, 256)

            sc_done, neg_ready, exp_done, p_ready, tr_done, pt_ready, o_done, o_free = (ev[f"ev{i}"] for i in range(8))
            with nc.Block() as block:
                @block.tensor
                def _(pe):
                    for h in range(XH):
                        if h >= 1:
                            pe.wait_ge(exp_done.sem, exp_done.at(h))
                        for q in range(TT):
                            mo = 0 if q < 4 else 256
                            dst = ps[:, q // 2, (q % 2) * 256:(q % 2) * 256 + 256]
                            for j in range(2):
                                last = nc.tensor.matmul(dst, b1[:, 2 * h + j, q * P:(q + 1) * P], km[:, 2 * h + j, mo:mo + 256],
                                                        start=(j == 0), stop=(j == 1))
                        last.then_inc(sc_done.sem, 1)
                        pe.wait_ge(p_ready.sem, p_ready.at(h + 1))
                        if h >= 1:
                            pe.wait_ge(pt_ready.sem, pt_ready.at(h))
                        for q in range(TT):
                            for j in range(2):
                                c = (q * 2 + j) * P
                                last = nc.tensor.transpose(ps[:, 4 + c // 512, c % 512:c % 512 + P],
                                                           s_sb[:, q, j * P:(j + 1) * P], ident)
                        last.then_inc(tr_done.sem, 1)
                        pe.wait_ge(pt_ready.sem, pt_ready.at(h + 1))
                        for j in range(2):
                            n = 2 * h + j
                            if n >= 1:
                                pe.wait_ge(o_free.sem, o_free.at(n))
                            for kt in range(2):
                                lhs = vm[:, kt, (2 * h + j) * P:(2 * h + j + 1) * P]
                                nc.tensor.matmul(ps[:, 7, :], lhs, pt[:, kt, 0:512], start=(kt == 0), stop=(kt == 1))
                            for kt in range(2):
                                lhs = vm[:, 2 + kt, (2 * h + j) * P:(2 * h + j + 1) * P]
                                last = nc.tensor.matmul(ps[:, 3, 0:256], lhs, pt[:, kt, 512:T], start=(kt == 0), stop=(kt == 1))
                            last.then_inc(o_done.sem, 1)

                @block.vector
                def _(v):
                    dve_chain.start(v)
                    for h in range(XH):
                        v.wait_ge(sc_done.sem, sc_done.at(h + 1))
                        if h >= 1:
                            v.wait_ge(exp_done.sem, exp_done.at(h))
                        sc = ps[:, 0:3, :].rearrange("p b (q n) -> p (b q) n", q=2)
                        dve_chain(nc.vector.tensor_reduce(st[:, 0, :], sc, AX.X, ALU.max))
                        nc.vector.tensor_scalar(st[:, 1, :], st[:, 0, :], -1.0, None, ALU.mult).then_inc(neg_ready.sem, 1)
                        v.wait_ge(exp_done.sem, exp_done.at(h + 1))
                        dve_chain(nc.vector.reciprocal(st[:, 3, :], st[:, 2, :]))
                        nc.vector.tensor_tensor(s_sb[:, :, :], s_sb[:, :, :],
                                                st[:, 3, :].unsqueeze(2).to_broadcast([P, TT, 256]), ALU.mult)\
                            .then_inc(p_ready.sem, 1)
                        for j in range(2):
                            n = 2 * h + j
                            v.wait_ge(o_done.sem, o_done.at(n + 1))
                            nc.vector.tensor_copy(act[:, n, 0:512], ps[:, 7, :])
                            nc.vector.tensor_copy(act[:, n, 512:T], ps[:, 3, 0:256]).then_inc(o_free.sem, 1)
                    dve_chain.close()

                @block.scalar
                def _(a):
                    for h in range(XH):
                        a.wait_ge(neg_ready.sem, neg_ready.at(h + 1))
                        if h >= 1:
                            a.wait_ge(tr_done.sem, tr_done.at(h))
                        for q in range(TT):
                            last = nc.scalar.activation(s_sb[:, q, :], ps[:, q // 2, (q % 2) * 256:(q % 2) * 256 + 256],
                                                        ACT.Exp, bias=st[:, 1, q:q + 1], accum_out=st[:, 2, q:q + 1])
                        last.then_inc(exp_done.sem, 1)
                        a.wait_ge(tr_done.sem, tr_done.at(h + 1))
                        if h >= 1:
                            a.wait_ge(o_done.sem, o_done.at(2 * h))
                        tr = ps[:, 4:7, :].rearrange("p b n -> p (b n)").rearrange("p (q j n) -> p j q n", j=2, n=P)
                        nc.scalar.activation(pt[:, 0, :].rearrange("p (q n) -> p q n", n=P), tr[:, 0], ACT.Copy)
                        nc.scalar.activation(pt[:, 1, :].rearrange("p (q n) -> p q n", n=P), tr[:, 1], ACT.Copy)\
                            .then_inc(pt_ready.sem, 1)
            for s_ in (sc_done, neg_ready, exp_done, p_ready, tr_done, pt_ready):
                s_.base += XH
            o_done.base += 2 * XH
            o_free.base += 2 * XH
            local.close()
            product_stage(act, ["ffff"], add_residual)

        def diff_attention():
            local = ExitStack()

            def evac(a, g, i):
                if g < 2:
                    free(nc.scalar.activation((b1, b2)[g][:, i, :], banks(2 * (i % 2)), ACT.Copy))
                else:
                    s, half = i // 2, i % 2
                    src = banks(2 * half).rearrange("p (j n) -> p j n", j=3)
                    free(nc.scalar.activation(vtok[:, 3 * half:3 * half + 3, s * UC:(s + 1) * UC], src, ACT.Copy))
            vtok = b3[:, :, :].rearrange("p k t -> p (k t)").rearrange("p (j n) -> p j n", j=TT)
            product_stage(act, ["ffff", "ffff", "tttt"], evac, norm=(x, "mix1"), evac_engine="scalar")
            head_norm_stage([([b1[:, h, :]], [gains[:, 0:1]], [b1[:, h, :]]) for h in range(DH)]
                            + [([b2[:, h, :]], [pcol("dk")], [b2[:, h, :]]) for h in range(DH)], ones64, 64)

            sc = sb("dsc", [P, 2, 2, 512], on=local)
            bias = sb("dbias", [P, 2, DIST], on=local)
            at = sb("dat", [P, 2, 512], on=local)
            st = sb("dst", [P, 2, 8], on=local)
            lam = sb("dlam", [P, 8], on=local)
            sc_done, neg_ready, exp_done, a_ready, tr_done, at_ready, o_done, o_free, bias_ready, bias_used, lam_a, lam_b, e0_ready = (
                ev[f"ev{i}"] for i in range(13))
            items = [(h, q) for h in range(DH) for q in range(TT)]
            with nc.Block() as block:
                @block.vector
                def _(v):
                    dve_chain.start(v)
                    nc.vector.tensor_tensor(lam[:, 0:2], pcol("lq"), pcol("lk"), ALU.mult).then_inc(lam_a.sem, 1)
                    v.wait_ge(lam_a.sem, lam_a.at(3))
                    dve_chain(nc.vector.tensor_tensor(lam[:, 4:5], lam[:, 3:4], lam[:, 2:3], ALU.subtract))
                    dve_chain(nc.vector.tensor_scalar(lam[:, 5:6], lam[:, 4:5], -LAMBDA_INIT, None, ALU.add))
                    for n, (h, q) in enumerate(items):
                        keys, k0 = (512, 0) if q < 4 else (256, 512)
                        b = n % 2
                        off = 384 - P * (q if q < 4 else q - 4)
                        if q == 0:
                            v.wait_ge(bias_ready.sem, bias_ready.at(h + 1))
                        v.wait_ge(sc_done.sem, sc_done.at(n + 1))
                        if n >= 2:
                            v.wait_ge(tr_done.sem, tr_done.at(n - 1))
                        for z in range(2):
                            nc.vector.tensor_tensor_reduce(
                                out=sc[:, b, z, 0:keys], in0=ps[:, 2 * b + z, 0:keys], in1=bias[:, h % 2, off:off + keys],
                                scale=1.0, scalar=-3.0e38, op0=ALU.add, op1=ALU.max, accum_out=st[:, b, z:z + 1])\
                                .then_inc(dchain.sem, 1)
                            dve_chain.n += 1
                        v.wait_ge(dchain.sem, dchain.base + dve_chain.n)
                        nc.vector.tensor_scalar(st[:, b, 2:4], st[:, b, 0:2], -1.0, None, ALU.mult).then_inc(neg_ready.sem, 1)
                        v.wait_ge(exp_done.sem, exp_done.at(n + 1))
                        dve_chain(nc.vector.reciprocal(st[:, b, 6:8], st[:, b, 4:6]))
                        dve_chain(nc.vector.tensor_tensor(st[:, b, 7:8], st[:, b, 7:8], lam[:, 5:6], ALU.mult))
                        dve_chain(nc.vector.tensor_scalar(sc[:, b, 0, 0:keys], sc[:, b, 0, 0:keys], st[:, b, 6:7], None, ALU.mult))
                        nc.vector.scalar_tensor_tensor(sc[:, b, 0, 0:keys], sc[:, b, 1, 0:keys], st[:, b, 7:8],
                                                       sc[:, b, 0, 0:keys], ALU.mult, ALU.add).then_inc(a_ready.sem, 1)
                    dve_chain.close()

                @block.gpsimd
                def _(g):
                    for h in range(DH):
                        if h >= 2:
                            g.wait_ge(neg_ready.sem, neg_ready.at(TT * (h - 1)))
                        nc.gpsimd.tensor_scalar(bias[:, h % 2, :], pcol("dist"), -float(2.0 ** -(h + 1)), None, ALU.mult)\
                            .then_inc(bias_ready.sem, 1)

                @block.scalar
                def _(a):
                    a.wait_ge(lam_a.sem, lam_a.at(2))
                    nc.scalar.activation(lam[:, 2:4], ps[:, 7, 0:2], ACT.Exp).then_inc(lam_a.sem, 1)

                    def after(n):
                        h, q = items[n]
                        nk = 4 if q < 4 else 2
                        a.wait_ge(tr_done.sem, tr_done.at(n + 1))
                        if n >= 2:
                            a.wait_ge(o_done.sem, o_done.at(n - 1))
                        nc.scalar.activation(at[:, n % 2, 0:nk * P], ps[:, 4 + n % 2, 0:nk * P], ACT.Copy).then_inc(at_ready.sem, 1)
                        if q == TT - 1:
                            a.wait_ge(o_done.sem, o_done.at(n + 1))
                            nc.scalar.activation(b1[:, h, :], banks(6), ACT.Copy).then_inc(o_free.sem, 1)
                    for n, (h, q) in enumerate(items):
                        keys = 512 if q < 4 else 256
                        b = n % 2
                        a.wait_ge(neg_ready.sem, neg_ready.at(n + 1))
                        for z in range(2):
                            last = nc.scalar.activation(sc[:, b, z, 0:keys], sc[:, b, z, 0:keys], ACT.Exp,
                                                        bias=st[:, b, 2 + z:3 + z], accum_out=st[:, b, 4 + z:5 + z])
                        last.then_inc(exp_done.sem, 1)
                        if n >= 1:
                            after(n - 1)
                    after(len(items) - 1)

                @block.tensor
                def _(pe):
                    pe.wait_ge(lam_a.sem, lam_a.at(1))
                    nc.tensor.matmul(ps[:, 7, 0:2], ones, lam[:, 0:2], start=True, stop=True).then_inc(lam_a.sem, 1)

                    def scores(n):
                        h, q = items[n]
                        keys, k0 = (512, 0) if q < 4 else (256, 512)
                        if n >= 2:
                            pe.wait_ge(neg_ready.sem, neg_ready.at(n - 1))
                        for z in range(2):
                            rows = slice(64 * z, 64 * z + 64)
                            last = nc.tensor.matmul(ps[:, 2 * (n % 2) + z, 0:keys], b1[rows, h, q * P:(q + 1) * P],
                                                    b2[rows, h, k0:k0 + keys], start=True, stop=True)
                        last.then_inc(sc_done.sem, 1)

                    def values(n):
                        h, q = items[n]
                        nk, t0 = (4, 0) if q < 4 else (2, 4)
                        pe.wait_ge(a_ready.sem, a_ready.at(n + 1))
                        if n >= 2:
                            pe.wait_ge(at_ready.sem, at_ready.at(n - 1))
                        for j in range(nk):
                            last = nc.tensor.transpose(ps[:, 4 + n % 2, j * P:(j + 1) * P], sc[:, n % 2, 0, j * P:(j + 1) * P], ident)
                        last.then_inc(tr_done.sem, 1)

                    def outputs(n):
                        h, q = items[n]
                        nk, t0 = (4, 0) if q < 4 else (2, 4)
                        pe.wait_ge(at_ready.sem, at_ready.at(n + 1))
                        if q == 0 and h >= 1:
                            pe.wait_ge(o_free.sem, o_free.at(h))
                        if n == 0:
                            pe.wait_ge(lam_a.sem, lam_a.at(3))
                        for j in range(nk):
                            last = nc.tensor.matmul(banks(6)[:, q * P:(q + 1) * P], vtok[:, t0 + j, h * P:(h + 1) * P],
                                                    at[:, n % 2, j * P:(j + 1) * P], start=(j == 0), stop=(j == nk - 1))
                        last.then_inc(o_done.sem, 1)
                    scores(0)
                    for n in range(len(items)):
                        if n + 1 < len(items):
                            scores(n + 1)
                        values(n)
                        if n >= 1:
                            outputs(n - 1)
                    outputs(len(items) - 1)
            ni = len(items)
            for s_ in (sc_done, neg_ready, exp_done, a_ready, tr_done, at_ready, o_done):
                s_.base += ni
            o_free.base += DH
            bias_ready.base += DH
            lam_a.base += 3
            local.close()
            head_norm_stage([([b1[:, h, :]], [gains[:, 1:2]], [act[:, h, :]]) for h in range(DH)], ones, 128)
            product_stage(act, ["ffff"], add_residual)

        def s5_gla():
            outer, local, prep = ExitStack(), ExitStack(), ExitStack()
            lr = sb("lr", [32, T], on=outer)
            sm = sb("s5small", [P, 32, G], on=local)
            names = ["step", "zr", "zi", "kk", "r", "rh", "sin", "sinh", "cos", "mag", "r8", "lbr", "lbi", "nr", "den", "cr",
                     "ci", "t0", "t1", "t2", "t3", "p2r", "p2i", "p4r", "p4i"]
            S = {n: sm[:, i, :] for i, n in enumerate(names)}
            bbar = sb("bbar", [P, 2, G, GC], on=local)
            cc = sb("cc", [P, 2, G, GC], on=local)
            qf = sb("qf", [P, 2, POS, G], on=local)
            qr = sb("qr", [P, 2, SC, G], on=local)
            dd = sb("dd", [GC, G, GC], on=local)
            pw = sb("pw", [P, 2, SC + 1, G], on=prep)
            wglr = sb("wglr_sb", [P, KT, 32], on=prep)
            rot = [b3[:, 4 * i:4 * i + 4, :].rearrange("p k t -> p (k t)").rearrange("p (g j) -> p g j", j=NCH) for i in range(2)]
            pc_in, pc_out = ev["ev0"], ev["ev1"]
            ld = dma["dma0"]

            def tt(o, a, b, op):
                dve_chain(nc.vector.tensor_tensor(o, a, b, op))

            def ts(o, a, s1, s2, op0, op1=None):
                dve_chain(nc.vector.tensor_scalar(o, a, s1, s2, op0, op1) if op1 is not None
                          else nc.vector.tensor_scalar(o, a, s1, s2, op0))

            def cmul(dr, di, ar, ai, br, bi, t, conj=False):
                nc.vector.tensor_tensor(t[0], ar, br, ALU.mult)
                nc.vector.tensor_tensor(t[1], ai, bi, ALU.mult)
                nc.vector.tensor_tensor(t[2], ar, bi, ALU.mult)
                dve_chain(nc.vector.tensor_tensor(t[3], ai, br, ALU.mult))
                nc.vector.tensor_tensor(dr, t[0], t[1], ALU.add if conj else ALU.subtract)
                if conj:
                    dve_chain(nc.vector.tensor_tensor(di, t[3], t[2], ALU.subtract))
                else:
                    dve_chain(nc.vector.tensor_tensor(di, t[3], t[2], ALU.add))

            def bc_g(a, n):
                return a.unsqueeze(2).to_broadcast([P, a.shape[1], n])

            def dve_pre(v):
                v.wait_ge(pc_in.sem, pc_in.at(1))
                tt(S["zr"], pcol("lre"), S["step"], ALU.mult)
                tt(S["zi"], pcol("lim"), S["step"], ALU.mult)
                ts(S["kk"], S["zi"], 1.0 / (2 * math.pi), MAGIC, ALU.mult, ALU.add)
                ts(S["kk"], S["kk"], -MAGIC, None, ALU.add)
                dve_chain(nc.vector.scalar_tensor_tensor(S["r"], S["kk"], -TWO_PI_HI, S["zi"], ALU.mult, ALU.add))
                dve_chain(nc.vector.scalar_tensor_tensor(S["r"], S["kk"], -TWO_PI_LO, S["r"], ALU.mult, ALU.add))
                nc.vector.tensor_scalar(S["r"], S["r"], 3.1415925, -3.1415925, ALU.min, ALU.max).then_inc(pc_out.sem, 1)

            def act_pre(a):
                nc.scalar.activation(S["step"], pcol("lstep"), ACT.Exp).then_inc(pc_in.sem, 1)
                a.wait_ge(pc_out.sem, pc_out.at(1))
                nc.scalar.activation(S["mag"], S["zr"], ACT.Exp)
                nc.scalar.activation(S["r8"], S["zr"], ACT.Exp, scale=float(SC))
                nc.scalar.activation(S["sin"], S["r"], ACT.Sin)
                nc.scalar.activation(S["sinh"], S["r"], ACT.Sin, scale=0.5).then_inc(pc_in.sem, 1)

            def dve_post(v):
                v.wait_ge(pc_in.sem, pc_in.at(2))
                tmp = [S[f"t{i}"] for i in range(4)]
                tt(S["t0"], S["sinh"], S["sinh"], ALU.mult)
                ts(S["cos"], S["t0"], -2.0, 1.0, ALU.mult, ALU.add)
                tt(S["lbr"], S["mag"], S["cos"], ALU.mult)
                tt(S["lbi"], S["mag"], S["sin"], ALU.mult)
                ts(S["nr"], S["lbr"], -1.0, None, ALU.add)
                tt(S["t0"], pcol("lre"), pcol("lre"), ALU.mult)
                tt(S["t1"], pcol("lim"), pcol("lim"), ALU.mult)
                tt(S["den"], S["t0"], S["t1"], ALU.add)
                dve_chain(nc.vector.reciprocal(S["den"], S["den"]))
                cmul(S["cr"], S["ci"], S["nr"], S["lbi"], pcol("lre"), pcol("lim"), tmp, conj=True)
                tt(S["cr"], S["cr"], S["den"], ALU.mult)
                tt(S["ci"], S["ci"], S["den"], ALU.mult)
                v.wait_ge(ld.sem, ld.at(48))
                t3 = [sq[:, i // 2, (i % 2) * 384:(i % 2) * 384 + 256].rearrange("p (g c) -> p g c", c=GC) for i in range(4)]
                for h in range(2):
                    gs = slice(16 * h, 16 * h + 16)
                    cmul(bbar[:, 0, gs, :], bbar[:, 1, gs, :], bin_[:, 0, gs, :], bin_[:, 1, gs, :],
                         bc_g(S["cr"][:, gs], GC), bc_g(S["ci"][:, gs], GC), t3)
                nc.vector.memset(pw[:, 0, 0, :], 1.0)
                nc.vector.memset(pw[:, 1, 0, :], 0.0)
                nc.vector.tensor_copy(pw[:, 0, 1, :], S["lbr"])
                dve_chain(nc.vector.tensor_copy(pw[:, 1, 1, :], S["lbi"]))
                t4 = [sq[:, i // 2, (i % 2) * 384:(i % 2) * 384 + 4 * G].rearrange("p (n g) -> p n g", g=G) for i in range(4)]
                for n in (1, 2, 4):
                    by = [pw[:, i, n:n + 1, :].to_broadcast([P, n, G]) for i in range(2)]
                    cmul(pw[:, 0, n + 1:2 * n + 1, :], pw[:, 1, n + 1:2 * n + 1, :], pw[:, 0, 1:n + 1, :], pw[:, 1, 1:n + 1, :],
                         by[0], by[1], [q[:, 0:n, :] for q in t4])
                for i in range(2):
                    nc.vector.memset(qf[0:NS, i, SC + 1, :], 0.0)
                    nc.vector.memset(qf[NS:P, i, 0, :], 0.0)
                    nc.vector.tensor_copy(qf[0:NS, i, 0:SC + 1, :], pw[0:NS, i, :, :])
                    for pos in range(1, POS):
                        nc.vector.tensor_copy(qf[NS:P, i, pos, :], pw[NS:P, i, SC + 1 - pos, :])
                    nc.vector.tensor_copy(qr[NS:P, i, :, :], pw[NS:P, i, 0:SC, :])
                    for s in range(SC):
                        nc.vector.tensor_copy(qr[0:NS, i, s, :], pw[0:NS, i, SC - 1 - s, :])
                cmul(S["p2r"], S["p2i"], S["cos"], S["sin"], S["cos"], S["sin"], tmp)
                cmul(S["p4r"], S["p4i"], S["p2r"], S["p2i"], S["p2r"], S["p2i"], tmp)
                cmul(S["p2r"], S["p2i"], S["p4r"], S["p4i"], S["p4r"], S["p4i"], tmp)
                dve_chain(nc.vector.tensor_scalar(S["p2i"][NS:P], S["p2i"][NS:P], -1.0, None, ALU.mult))
                nc.vector.memset(rot[0][:, :, 0:1], 1.0)
                dve_chain(nc.vector.memset(rot[1][:, :, 0:1], 0.0))
                n, pr, pi, nr_, ni_ = 1, S["p2r"], S["p2i"], S["p4r"], S["p4i"]
                while n < NCH:
                    m = min(n, NCH - n)
                    for g0 in range(0, G, 8 if m > 16 else 16):
                        w_ = 8 if m > 16 else 16
                        gs = slice(g0, g0 + w_)
                        tw = [sq[:, i // 2, (i % 2) * 384:(i % 2) * 384 + w_ * min(m, 32)].rearrange("p (g j) -> p g j", g=w_)
                              for i in range(4)]
                        for m0 in range(0, m, 32):
                            mm = min(32, m - m0)
                            cmul(rot[0][:, gs, n + m0:n + m0 + mm], rot[1][:, gs, n + m0:n + m0 + mm],
                                 rot[0][:, gs, m0:m0 + mm], rot[1][:, gs, m0:m0 + mm],
                                 bc_g(pr[:, gs], mm), bc_g(pi[:, gs], mm), [q[:, :, 0:mm] for q in tw])
                    cmul(nr_, ni_, pr, pi, pr, pi, tmp)
                    pr, pi, nr_, ni_ = nr_, ni_, pr, pi
                    n *= 2
                nc.vector.tensor_tensor(dd[:, :, :], pcol("s5d")[0:GC].unsqueeze(2).to_broadcast([GC, G, GC]),
                                        ident[0:GC, 0:GC].unsqueeze(1).to_broadcast([GC, G, GC]), ALU.mult).then_inc(pc_out.sem, 1)
                v.wait_ge(pc_out.sem, pc_out.at(2))

            bin_ = b3[:, 0:2, :].rearrange("p k t -> p (k t)")[:, 0:2 * G * GC].rearrange("p (i g c) -> p i g c", i=2, c=GC)
            with nc.Block() as block:
                @block.sync
                def _(sp):
                    sp.dma_start(bin_, bc_in[0:2].rearrange("i p (g c) -> p i g c", c=GC)).then_inc(ld.sem, 16)
                    sp.dma_start(cc[:, :, :, :], bc_in[2:4].rearrange("i p (g c) -> p i g c", c=GC)).then_inc(ld.sem, 16)
                    sp.dma_start(wglr[:, :, :], wglr_in).then_inc(ld.sem, 16)

            def evac(a, g, i):
                if g == 0 and i < 4:
                    free(nc.scalar.activation(b1[:, i, :].rearrange("p (s j) -> p s j", s=SC),
                                              banks(2 * (i % 2)).rearrange("p (j s) -> p s j", s=SC), ACT.Copy))
                elif g == 0:
                    free(nc.scalar.activation(b1[:, i, :], banks(2 * (i % 2)), ACT.Copy, scale=float(DK ** -0.5) if i < 6 else 1.0))
                elif i < 4:
                    s, half = i // 2, i % 2
                    free(nc.scalar.activation(vt[:, 3 * half:3 * half + 3, s * UC:(s + 1) * UC],
                                              banks(2 * half).rearrange("p (j n) -> p j n", j=3), ACT.Copy))
                else:
                    free(nc.scalar.activation(b2[:, i, :], banks(2 * (i % 2)), ACT.Copy))
            vt = b2[:, 0:4, :].rearrange("p k t -> p (k t)").rearrange("p (j n) -> p j n", n=GH * DV)
            product_stage(act, ["ffff", "ttff"], evac, norm=(x, "mix0"), evac_engine="scalar", dve_pre=dve_pre,
                          act_pre=act_pre, dve_post=dve_post)
            ld.base += 48
            pc_in.base += 2
            pc_out.base += 2

            ud, yd = dma["dma1"], dma["dma2"]
            with nc.Block() as block:
                @block.sync
                def _(sp):
                    sp.dma_start(u_dram.rearrange("(k p) s j -> p k (s j)", p=P), b1[:, 0:4, :]).then_inc(ud.sem, 16)
                    sp.wait_ge(ud.sem, ud.at(16))

                @block.tensor
                def _(pe):
                    for k in range(KT):
                        nc.tensor.matmul(ps[0:32, 0, :], wglr[:, k, :], act[:, k, 0:512], start=(k == 0), stop=(k == KT - 1))
                        last = nc.tensor.matmul(ps[0:32, 1, 0:TS], wglr[:, k, :], act[:, k, 512:T],
                                                start=(k == 0), stop=(k == KT - 1))
                    last.then_inc(pc_in.sem, 1)

                @block.scalar
                def _(a):
                    a.wait_ge(pc_in.sem, pc_in.at(1))
                    nc.scalar.activation(lr[:, :], banks(0)[0:32], ACT.Copy).then_inc(pc_out.sem, 1)
            ud.base += 16
            pc_in.base += 1
            pc_out.base += 1

            prep.close()
            s5 = ExitStack()
            u2 = act[:, 0, :].rearrange("p (g j) -> p g j", j=NCH)
            cl = sb("cl", [P, 2, GB, POS, GC], on=s5)
            vv = sb("vv", [P, 2, GB, P], on=s5)
            b1f = b1[:, 0:4, :].rearrange("p k t -> p (k t)")
            vT = b1f[:, 0:2 * GB * P].rearrange("p (i g c) -> p i g c", i=2, g=GB)
            mt = b1f[:, 2 * GB * P:3 * GB * P].rearrange("p (g c) -> p g c", g=GB)
            rt = act[0:GC, 2:5, :].rearrange("p k t -> p (k t)")[:, 0:GB * LAG * GC]\
                .rearrange("p (g n c) -> p g n c", g=GB, n=LAG)
            dec = act[:, 1, :]
            bp = [act[:, 2 + i, :] for i in range(2)]
            sp_ = [act[:, 4 + i, :] for i in range(2)]
            so = [act[:, 6 + i, :] for i in range(2)]
            tmpA = [rstd[:, :]] + [vv[:, 0, :, :].rearrange("p g c -> p (g c)")[:, 0:T],
                                   vv[:, 1, :, :].rearrange("p g c -> p (g c)")[:, 0:T], sq[:, 0, :]]
            ysb, yg = sq[:, 1, :], rstd[:, :]
            (t_v, vt_done, vt_ready, lag_done, rt_ready, m_loaded, bu_done, bu_read, st_ready, y_done, y_ready, y_e, y_e2,
             yg_ready) = (ev[f"ev{i}"] for i in range(14))

            def g3(a):
                return a.rearrange("p (g j) -> p g j", j=NCH)

            for b in range(NB):
                gs = slice(GB * b, GB * b + GB)
                with nc.Block() as block:
                    @block.sync
                    def _(sp):
                        src = u_dram[P * b:P * b + P].rearrange("(g c) s j -> s c g j", c=GC)
                        for s in range(SC):
                            sp.dma_start(u2[GC * s:GC * s + GC], src[s]).then_inc(ld.sem, 16)
                        sp.wait_ge(rt_ready.sem, rt_ready.at(1))
                        for s in range(SC):
                            sp.dma_start(mt[GC * s:GC * s + GC, :, :],
                                         rt[:, :, SC - 1 - s:2 * SC - 1 - s, :].rearrange("c g t d -> c g (t d)"))\
                                .then_inc(m_loaded.sem, 16)
                        sp.wait_ge(yg_ready.sem, yg_ready.at(1))
                        dst = y_dram[P * b:P * b + P].rearrange("(g c) t j -> t c g j", c=GC)
                        for s in range(SC):
                            sp.dma_start(dst[s], g3(yg)[GC * s:GC * s + GC]).then_inc(yd.sem, 16)
                        sp.wait_ge(yd.sem, yd.at(16 * SC))

                    @block.vector
                    def _(v):
                        dve_chain.start(v)
                        clf = [cl[:, i, :, :, :] for i in range(2)]
                        tc = [vT[:, 0, :, :].rearrange("p g c -> p (g c)"), vT[:, 1, :, :].rearrange("p g c -> p (g c)")]

                        def cb(i, h):
                            return cc[:, i, GB * b + 4 * h:GB * b + 4 * h + 4, :].unsqueeze(2).to_broadcast([P, 4, POS, GC])

                        def qb(i, h):
                            return qf[:, i, :, GB * b + 4 * h:GB * b + 4 * h + 4].rearrange("p n g -> p g n").unsqueeze(3)\
                                .to_broadcast([P, 4, POS, GC])
                        for h in range(2):
                            ta = [t_[:, 0:4 * POS * GC].rearrange("p (g n c) -> p g n c", g=4, n=POS) for t_ in tc]
                            o = [c_[:, 4 * h:4 * h + 4] for c_ in clf]
                            nc.vector.tensor_tensor(ta[0], cb(0, h), qb(0, h), ALU.mult)
                            dve_chain(nc.vector.tensor_tensor(ta[1], cb(1, h), qb(1, h), ALU.mult))
                            dve_chain(nc.vector.tensor_tensor(o[0], ta[0], ta[1], ALU.subtract))
                            nc.vector.tensor_tensor(ta[0], cb(0, h), qb(1, h), ALU.mult)
                            dve_chain(nc.vector.tensor_tensor(ta[1], cb(1, h), qb(0, h), ALU.mult))
                            dve_chain(nc.vector.scalar_tensor_tensor(
                                o[1].rearrange("p g n c -> p (g n c)"), ta[0].rearrange("p g n c -> p (g n c)"), -1.0,
                                ta[1].rearrange("p g n c -> p (g n c)"), ALU.mult, ALU.subtract))
                        for h in range(2):
                            hs = slice(GB * b + 4 * h, GB * b + 4 * h + 4)
                            bb = [bbar[:, i, hs, :].unsqueeze(2).to_broadcast([P, 4, SC, GC]) for i in range(2)]
                            qq = [qr[:, i, :, hs].rearrange("p n g -> p g n").unsqueeze(3).to_broadcast([P, 4, SC, GC])
                                  for i in range(2)]
                            ta = [t_[:, 0:4 * P].rearrange("p (g n c) -> p g n c", g=4, n=SC) for t_ in tc]
                            o = [vv[:, i, 4 * h:4 * h + 4, :].rearrange("p g (n c) -> p g n c", n=SC) for i in range(2)]
                            for i, (q0, q1, op) in enumerate(((0, 1, ALU.subtract), (1, 0, ALU.add))):
                                nc.vector.tensor_tensor(ta[0], bb[0], qq[q0], ALU.mult)
                                dve_chain(nc.vector.tensor_tensor(ta[1], bb[1], qq[q1], ALU.mult))
                                dve_chain(nc.vector.tensor_tensor(o[i], ta[0], ta[1], op))
                        dve_chain(nc.vector.tensor_tensor(g3(dec), bc_g(S["r8"][:, gs], NCH),
                                                          pcol("chunkmask").unsqueeze(1).to_broadcast([P, GB, NCH]), ALU.mult))
                        nc.vector.memset(so[0], 0.0)
                        nc.vector.memset(so[1], 0.0).then_inc(t_v.sem, 1)
                        v.wait_ge(lag_done.sem, lag_done.at(1))
                        lagf = banks(4, 1024)[0:GC].rearrange("c (g n d) -> c g n d", g=GB, n=SC)
                        lagb = banks(6, 1024)[0:GC].rearrange("c (g n d) -> c g n d", g=GB, n=SC)
                        dve_chain(nc.vector.tensor_copy(rt[:, :, 0:SC, :], lagb))
                        nc.vector.tensor_copy(rt[:, :, SC:LAG, :], lagf[:, :, 1:SC, :])
                        dve_chain(nc.vector.tensor_tensor(rt[:, :, SC - 1, :], rt[:, :, SC - 1, :], lagf[:, :, 0, :], ALU.add))
                        nc.vector.tensor_tensor(rt[:, :, SC - 1, :], rt[:, :, SC - 1, :], dd[:, gs, :], ALU.add).then_inc(rt_ready.sem, 1)
                        v.wait_ge(bu_done.sem, bu_done.at(1))
                        bur = banks(0, 1024).rearrange("p (g j) -> p g j", j=P)[:, :, 0:NCH]
                        bui = banks(2, 1024).rearrange("p (g j) -> p g j", j=P)[:, :, 0:NCH]
                        er, ei = rot[0][:, gs, :], rot[1][:, gs, :]
                        v.wait_ge(m_loaded.sem, m_loaded.at(16 * SC))
                        cmul(g3(bp[0]), g3(bp[1]), bur, bui, er, ei, [g3(t_) for t_ in tmpA], conj=True)
                        for i in range(2):
                            nc.vector.tensor_tensor_scan(out=sp_[i][0:NS], data0=dec[0:NS], data1=bp[i][0:NS], initial=0.0,
                                                         op0=ALU.mult, op1=ALU.add)
                            ins = nc.vector.tensor_tensor_scan(out=sp_[i][NS:P, ::-1], data0=dec[NS:P, ::-1],
                                                               data1=bp[i][NS:P, ::-1], initial=0.0, op0=ALU.mult, op1=ALU.add)
                        dve_chain(ins)
                        nc.vector.tensor_tensor(g3(tmpA[0]), g3(sp_[0]), er, ALU.mult)
                        nc.vector.tensor_tensor(g3(tmpA[1]), g3(sp_[1]), ei, ALU.mult)
                        nc.vector.tensor_tensor(g3(tmpA[2]), g3(sp_[0]), ei, ALU.mult)
                        dve_chain(nc.vector.tensor_tensor(g3(tmpA[3]), g3(sp_[1]), er, ALU.mult))
                        for i, op in ((0, ALU.subtract), (1, ALU.add)):
                            o, a_, b_ = g3(so[i]), g3(tmpA[2 * i]), g3(tmpA[2 * i + 1])
                            nc.vector.tensor_tensor(o[0:NS, :, 1:NCH], a_[0:NS, :, 0:NCH - 1], b_[0:NS, :, 0:NCH - 1], op)
                            dve_chain(nc.vector.tensor_tensor(o[NS:P, :, 0:NCH - 1], a_[NS:P, :, 1:NCH], b_[NS:P, :, 1:NCH], op))
                            nc.vector.memset(o[0:NS, :, TP // SC:TP // SC + 1], 0.0)
                            last = nc.vector.memset(o[NS:P, :, TP // SC - 1:TP // SC], 0.0)
                        last.then_inc(st_ready.sem, 1)
                        v.wait_ge(y_ready.sem, y_ready.at(1))
                        t_ = tmpA[1]
                        tt(t_, ysb, ysb, ALU.mult)
                        ts(t_, t_, 0.044715, 1.0, ALU.mult, ALU.add)
                        tt(t_, t_, ysb, ALU.mult)
                        nc.vector.tensor_scalar(t_, t_, -50.0, None, ALU.max).then_inc(y_e.sem, 1)
                        v.wait_ge(y_e2.sem, y_e2.at(1))
                        ts(t_, t_, 1.0, None, ALU.add)
                        dve_chain(nc.vector.reciprocal(t_, t_))
                        nc.vector.tensor_tensor(yg, t_, ysb, ALU.mult).then_inc(yg_ready.sem, 1)
                        dve_chain.close()

                    @block.tensor
                    def _(pe):
                        pe.wait_ge(t_v.sem, t_v.at(1))
                        for i in range(2):
                            for g in range(GB):
                                last = nc.tensor.transpose(banks(2 * i, 1024)[:, g * P:(g + 1) * P], vv[:, i, g, :], ident)
                        last.then_inc(vt_done.sem, 1)
                        for g in range(GB):
                            for z in range(2):
                                rows = slice(NS * z, NS * z + NS)
                                lo = 0 if z == 0 else 2
                                for i in range(2):
                                    last = nc.tensor.matmul(banks(4 + 2 * z, 1024)[0:GC, g * P:(g + 1) * P],
                                                            bbar[rows, i, GB * b + g, :],
                                                            cl[rows, i, g, lo:lo + SC, :].rearrange("p n c -> p (n c)"),
                                                            start=(i == 0), stop=(i == 1))
                        last.then_inc(lag_done.sem, 1)
                        pe.wait_ge(vt_ready.sem, vt_ready.at(1))
                        pe.wait_ge(ld.sem, ld.at(16 * SC))
                        for i in range(2):
                            for g in range(GB):
                                last = nc.tensor.matmul(banks(2 * i, 1024)[:, g * P:g * P + NCH], vT[:, i, g, :], u2[:, g, :],
                                                        start=True, stop=True)
                        last.then_inc(bu_done.sem, 1)
                        pe.wait_ge(m_loaded.sem, m_loaded.at(16 * SC))
                        pe.wait_ge(st_ready.sem, st_ready.at(1))
                        for g in range(GB):
                            o = banks(4, 1024)[:, g * P:g * P + NCH]
                            nc.tensor.matmul(o, mt[:, g, :], u2[:, g, :], start=True, stop=False)
                            for i in range(2):
                                last = nc.tensor.matmul(o, cl[:, i, g, 1:SC + 1, :].rearrange("p n c -> p (n c)"),
                                                        g3(so[i])[:, g, :], start=False, stop=(i == 1))
                        last.then_inc(y_done.sem, 1)

                    @block.scalar
                    def _(a):
                        a.wait_ge(vt_done.sem, vt_done.at(1))
                        a.wait_ge(lag_done.sem, lag_done.at(1))
                        for i in range(2):
                            last = nc.scalar.activation(vT[:, i, :, :].rearrange("p g c -> p (g c)"), banks(2 * i, 1024), ACT.Copy)
                        last.then_inc(vt_ready.sem, 1)
                        a.wait_ge(y_done.sem, y_done.at(1))
                        nc.scalar.activation(g3(ysb), banks(4, 1024).rearrange("p (g j) -> p g j", j=P)[:, :, 0:NCH], ACT.Copy)\
                            .then_inc(y_ready.sem, 1)
                        a.wait_ge(y_e.sem, y_e.at(1))
                        nc.scalar.activation(tmpA[1], tmpA[1], ACT.Exp, scale=-2.0 * math.sqrt(2.0 / math.pi)).then_inc(y_e2.sem, 1)
                for s_ in (t_v, vt_done, vt_ready, lag_done, rt_ready, bu_done, st_ready, y_done, y_ready, y_e, y_e2, yg_ready):
                    s_.base += 1
                ld.base += 16 * SC
                m_loaded.base += 16 * SC
                yd.base += 16 * SC
            s5.close()

            glu = ExitStack()
            wglu = sb("wglu_sb", [P, 4, 512], on=glu)
            et = sb("glu_t", [P, 2, T], on=glu)
            with nc.Block() as block:
                @block.sync
                def _(sp):
                    sp.dma_start(b1[:, 0:4, :], y_dram.rearrange("(k p) s j -> p k (s j)", p=P)).then_inc(ld.sem, 16)
                    sp.dma_start(wglu[:, :, :], wglu_in).then_inc(ld.sem, 16)

                @block.tensor
                def _(pe):
                    pe.wait_ge(ld.sem, ld.at(32))
                    for o in range(4):
                        if o >= 2:
                            pe.wait_ge(vt_ready.sem, vt_ready.at(o - 1))
                        for k in range(4):
                            nc.tensor.matmul(ps[:, 2 * (o % 2), :], wglu[:, k, o * P:(o + 1) * P], b1[:, k, 0:512],
                                             start=(k == 0), stop=(k == 3))
                            last = nc.tensor.matmul(ps[:, 2 * (o % 2) + 1, 0:TS], wglu[:, k, o * P:(o + 1) * P], b1[:, k, 512:T],
                                                    start=(k == 0), stop=(k == 3))
                        last.then_inc(vt_done.sem, 1)

                @block.scalar
                def _(a):
                    for o in range(4):
                        a.wait_ge(vt_done.sem, vt_done.at(o + 1))
                        if o >= 2:
                            a.wait_ge(st_ready.sem, st_ready.at(o - 1))
                        nc.scalar.activation(et[:, o % 2, :], banks(2 * (o % 2)), ACT.Exp, scale=-1.0).then_inc(vt_ready.sem, 1)

                @block.vector
                def _(v):
                    dve_chain.start(v)
                    for o in range(4):
                        v.wait_ge(vt_ready.sem, vt_ready.at(o + 1))
                        e_ = et[:, o % 2, :]
                        ts(e_, e_, 1.0, None, ALU.add)
                        dve_chain(nc.vector.reciprocal(e_, e_))
                        nc.vector.tensor_tensor(act[:, o, :].rearrange("p (j s) -> p s j", s=SC),
                                                e_.rearrange("p (s j) -> p s j", s=SC),
                                                b1[:, o, :].rearrange("p (s j) -> p s j", s=SC), ALU.mult).then_inc(st_ready.sem, 1)
                    v.wait_ge(st_ready.sem, st_ready.at(4))
                    dve_chain.close()
            ld.base += 32
            for s_ in (vt_done, vt_ready, st_ready):
                s_.base += 4
            glu.close()
            local.close()

            gl = ExitStack()
            wg = sb("wg", [32, 2, 256], on=gl)
            gm = sb("gm", [P, 2, T], on=gl)
            gt = b1[:, 0:4, :]
            qrel = b3[:, 5:7, :]
            krel = sb("krel", [P, 2, T], on=gl)
            ko = b3[:, 7, :]
            koT = b3[:, 4, :].rearrange("p (j d) -> p j d", d=P)
            qout = sb("qout", [P, 2, T], on=gl)
            sprev = [b3[:, 2 * z:2 * z + 2, :].rearrange("p k t -> p (k t)").rearrange("p (c d) -> p c d", d=DV) for z in range(2)]
            scT = sb("scT", [P, 2, T], on=gl)
            decay = sb("decay", [P, NC12], on=gl)
            (z_done, z_read, e_in, e_out, l_out, d_in, d_out, ko_ready, kt_done, kt_ready, kv_done, s_ready, sc_done, sc_ready,
             oo_done, oo_read) = (ev[f"ev{i}"] for i in range(16))

            def kv_ps(c):
                b = 4 + 2 * (c % 2) + c // 2 // 4
                return ps[:, b, (c // 2 % 4) * DV:(c // 2 % 4) * DV + DV]

            def c3(a):
                return a.rearrange("p (c i) -> p c i", i=CH)
            with nc.Block() as block:
                @block.sync
                def _(sp):
                    sp.dma_start(wg[:, :, :], wgate_in).then_inc(ld.sem, 16)
                    sp.wait_ge(ld.sem, ld.at(16))

                @block.gpsimd
                def _(g):
                    nc.gpsimd.memset(gm[:, :, :], 1.0).then_inc(pchain.sem, 1)
                    g.wait_ge(pchain.sem, pchain.at(1))
                    nc.gpsimd.memset(c3(gm[:, 0, :])[:, :, 0:1], 0.0)
                    nc.gpsimd.memset(c3(gm[:, 1, :])[:, :, CH - 1:CH], 0.0)
                    for z in range(2):
                        nc.gpsimd.memset(sprev[z][:, 0 if z == 0 else TP // CH - 1, :], 0.0)
                        nc.gpsimd.memset(sprev[z][:, TP // CH if z == 0 else NC12 - 1, :], 0.0)
                    nc.gpsimd.memset(scT[:, :, :], 0.0).then_inc(pchain.sem, 1)
                    g.wait_ge(pchain.sem, pchain.at(2))
            pchain.base += 2
            ld.base += 16
            for t in range(2):
                for z in range(2):
                    with nc.Block() as block:
                        @block.tensor
                        def _(pe):
                            nc.tensor.matmul(ps[:, 0, :], wg[:, z, t * P:(t + 1) * P], lr[:, 0:512], start=True, stop=True)
                            nc.tensor.matmul(ps[:, 1, 0:TS], wg[:, z, t * P:(t + 1) * P], lr[:, 512:T], start=True, stop=True)\
                                .then_inc(z_done.sem, 1)
                            pe.wait_ge(ko_ready.sem, ko_ready.at(1))
                            for j in range(TT):
                                last = nc.tensor.transpose(banks(2)[:, j * P:(j + 1) * P], ko[:, j * P:(j + 1) * P], ident)
                            last.then_inc(kt_done.sem, 1)
                            pe.wait_ge(kt_ready.sem, kt_ready.at(1))
                            for c in range(NC12):
                                rows = slice(CH * (c % 2), CH * (c % 2) + CH)
                                for hh in range(2):
                                    h = 2 * t + hh
                                    last = nc.tensor.matmul(kv_ps(c)[DK * hh:DK * hh + DK],
                                                            koT[rows, c // 2, DK * hh:DK * hh + DK],
                                                            vt[rows, c // 2, h * DV:(h + 1) * DV], start=True, stop=True)
                            last.then_inc(kv_done.sem, 1)

                        @block.vector
                        def _(v):
                            dve_chain.start(v)
                            g_, cum, ta, tb = (gt[:, i, :] for i in range(4))
                            v.wait_ge(z_done.sem, z_done.at(1))
                            col = COLS["bgate"][0] + 2 * z + t
                            dve_chain(nc.vector.tensor_scalar(g_, banks(0), par[:, col:col + 1], None, ALU.add))
                            ts(ta, g_, -1.0, None, ALU.mult)
                            nc.vector.tensor_tensor(ta, ta, g_, ALU.min).then_inc(e_in.sem, 1)
                            v.wait_ge(e_out.sem, e_out.at(1))
                            dve_chain(nc.vector.scalar_tensor_tensor(g_, g_, 0.0, ta, ALU.min, ALU.subtract))
                            if z == 0:
                                dve_chain(nc.vector.tensor_tensor_scan(out=cum, data0=gm[:, 0, :], data1=g_, initial=0.0,
                                                                       op0=ALU.mult, op1=ALU.add))
                            else:
                                dve_chain(nc.vector.tensor_tensor_scan(out=cum[:, ::-1], data0=gm[:, 1, ::-1], data1=g_[:, ::-1],
                                                                       initial=0.0, op0=ALU.mult, op1=ALU.add))
                            ref = CH // 2 - 1 if z == 0 else CH // 2
                            end = CH - 1 if z == 0 else 0
                            refs = c3(cum)[:, :, ref:ref + 1].to_broadcast([P, NC12, CH])
                            ends = c3(cum)[:, :, end:end + 1].to_broadcast([P, NC12, CH])
                            nc.vector.tensor_tensor(c3(ta), c3(cum), refs, ALU.subtract)
                            nc.vector.tensor_tensor(c3(tb), ends, c3(cum), ALU.subtract).then_inc(d_in.sem, 1)
                            v.wait_ge(d_out.sem, d_out.at(1))
                            nc.vector.tensor_tensor(ko[:, :], b1[:, 6 + t, :], tb, ALU.mult).then_inc(ko_ready.sem, 1)
                            nc.vector.tensor_tensor(qout[:, z, :], b1[:, 4 + t, :], cum, ALU.mult)
                            nc.vector.tensor_tensor(qrel[:, z, :], b1[:, 4 + t, :], ta, ALU.mult)
                            nc.vector.tensor_tensor(krel[:, z, :], b1[:, 6 + t, :], g_, ALU.mult)
                            v.wait_ge(kv_done.sem, kv_done.at(1))
                            order = [(0, 8), (8, 12)]
                            for lo, hi in order:
                                cs = list(range(lo, hi)) if z == 0 else list(range(hi - 1, lo - 1, -1))
                                for c, nx in zip(cs[:-1], cs[1:]):
                                    dve_chain(nc.vector.scalar_tensor_tensor(
                                        sprev[z][:, nx, :], sprev[z][:, c, :], decay[:, c:c + 1],
                                        kv_ps(c), ALU.mult, ALU.add))
                            dve_chain.close()

                        @block.scalar
                        def _(a):
                            g_, cum, ta, tb = (gt[:, i, :] for i in range(4))
                            a.wait_ge(e_in.sem, e_in.at(1))
                            nc.scalar.activation(ta, ta, ACT.Exp).then_inc(achain.sem, 1)
                            a.wait_ge(achain.sem, achain.at(1))
                            nc.scalar.activation(ta, ta, ACT.Ln, bias=pcol("one")).then_inc(e_out.sem, 1)
                            a.wait_ge(d_in.sem, d_in.at(1))
                            cumends = c3(cum)[:, :, CH - 1 if z == 0 else 0]
                            nc.scalar.activation(decay[:, :], cumends, ACT.Exp, scale=1.0 / 16)
                            nc.scalar.activation(g_, ta, ACT.Exp, scale=-1.0 / 16).then_inc(achain.sem, 1)
                            a.wait_ge(achain.sem, achain.at(2))
                            nc.scalar.activation(ta, ta, ACT.Exp, scale=1.0 / 16)
                            nc.scalar.activation(tb, tb, ACT.Exp, scale=1.0 / 16)
                            nc.scalar.activation(cum, cum, ACT.Exp, scale=1.0 / 16).then_inc(d_out.sem, 1)
                            a.wait_ge(kt_done.sem, kt_done.at(1))
                            nc.scalar.activation(koT.rearrange("p j d -> p (j d)"), banks(2), ACT.Copy).then_inc(kt_ready.sem, 1)
                    for s_ in (z_done, e_in, e_out, d_in, d_out, ko_ready, kt_done, kt_ready, kv_done):
                        s_.base += 1
                    achain.base += 2
                with nc.Block() as block:
                    @block.tensor
                    def _(pe):
                        for hh in range(2):
                            h = 2 * t + hh
                            rows = slice(DK * hh, DK * hh + DK)
                            if hh == 1:
                                pe.wait_ge(sc_ready.sem, sc_ready.at(1))
                            for z in range(2):
                                for j in range(TT):
                                    js = slice(j * P, (j + 1) * P)
                                    last = nc.tensor.matmul(banks(2 * z)[:, js], krel[rows, z, js], qrel[rows, z, js],
                                                            start=True, stop=True)
                            last.then_inc(sc_done.sem, 1)
                            pe.wait_ge(sc_ready.sem, sc_ready.at(hh + 1))
                            ob = banks(4 + 2 * hh)
                            for j in range(TT):
                                js = slice(j * P, (j + 1) * P)
                                for z in range(2):
                                    nc.tensor.matmul(ob[:, js], vt[:, j, h * DV:(h + 1) * DV], scT[:, z, js],
                                                     start=(z == 0), stop=False, skip_group_check=True)
                                for z in range(2):
                                    for c in (2 * j, 2 * j + 1):
                                        cs = slice(CH * c, CH * c + CH)
                                        last = nc.tensor.matmul(ob[:, cs], sprev[z][rows, c, :], qout[rows, z, cs],
                                                                start=False, stop=(z == 1), skip_group_check=True)
                            last.then_inc(oo_done.sem, 1)

                    @block.vector
                    def _(v):
                        for hh in range(2):
                            v.wait_ge(sc_done.sem, sc_done.at(hh + 1))
                            if hh == 1:
                                v.wait_ge(oo_done.sem, oo_done.at(1))
                            for z in range(2):
                                mk = pcol("masks", P * z, P).bitcast(mybir.dt.uint32).unsqueeze(1).to_broadcast([P, TT, P])
                                last = nc.vector.copy_predicated(scT[:, z, :].rearrange("p (j i) -> p j i", i=P), mk,
                                                                 banks(2 * z).rearrange("p (j i) -> p j i", i=P))
                            last.then_inc(sc_ready.sem, 1)

                    @block.scalar
                    def _(a):
                        for hh in range(2):
                            a.wait_ge(oo_done.sem, oo_done.at(hh + 1))
                            nc.scalar.activation(act[:, 4 + 2 * t + hh, :], banks(4 + 2 * hh), ACT.Copy)
                for s_ in (sc_done, sc_ready, oo_done):
                    s_.base += 2
            with nc.Block() as block:
                @block.scalar
                def _(a):
                    for h in range(GH):
                        nc.scalar.activation(gt[:, h, :], b2[:, 4 + h, :], ACT.Exp, scale=-1.0).then_inc(e_in.sem, 1)

                @block.vector
                def _(v):
                    dve_chain.start(v)
                    for h in range(GH):
                        v.wait_ge(e_in.sem, e_in.at(h + 1))
                        ts(gt[:, h, :], gt[:, h, :], 1.0, None, ALU.add)
                        dve_chain(nc.vector.reciprocal(gt[:, h, :], gt[:, h, :]))
                        tt(b2[:, 4 + h, :], b2[:, 4 + h, :], gt[:, h, :], ALU.mult)
                    dve_chain.close()
            e_in.base += GH

            def gate(v, h):
                v.wait_ge(normed.sem, normed.at(h + 1))
                nc.vector.tensor_tensor(act[:, 4 + h, :], act[:, 4 + h, :], b2[:, 4 + h, :], ALU.mult)
            head_norm_stage([([act[:, 4 + h, :]], [pcol("gnorm")], [act[:, 4 + h, :]]) for h in range(GH)], ones, DV, extra=gate)
            gl.close()
            outer.close()

        def mix0():
            s5_gla()
            product_stage(act, ["ffff"], add_residual)

        def dump_act():
            with nc.Block() as block:
                @block.vector
                def _(v):
                    nc.vector.tensor_copy(x[:, :, :], act[:, :, :])
        mix0()
        cross(0)
        mlp(0)
        diff_attention()
        cross(1)
        mlp(1)

        with nc.Block() as block:
            @block.sync
            def _(sp):
                sp.dma_start(out.rearrange("(k p) t -> p k t", p=P), x[:, :, :]).then_inc(dma["dma1"].sem, 16)
                sp.wait_ge(dma["dma1"].sem, dma["dma1"].at(16))


def kernel(**inputs):
    import numpy as _np
    import concourse.bacc as _bacc
    from concourse import mybir as _mybir
    from concourse.bass_utils import run_bass_kernel_spmd as _run

    w = {k: _np.asarray(v) for k, v in inputs.items()}

    def cols(v):
        return v.reshape(-1, P).T

    par = _np.zeros((P, NPAR), _np.float32)

    def put(name, v):
        a, n = COLS[name]
        par[:v.shape[0], a:a + n] = v

    for layer in range(DEPTH):
        for short, name in (("mix", "norm_mix"), ("cross", "norm_cross"), ("mem", "norm_mem"), ("mlp", "norm_mlp"),
                            ("xq", "x_q_norm"), ("xk", "x_k_norm")):
            put(f"{short}{layer}", cols(w[name][layer]))
    for name, src in (("dq", "diff_q_norm"), ("dk", "diff_k_norm")):
        put(name, _np.concatenate([w[src][0], w[src][0]])[:, None])
    put("dnorm", w["diff_norm"][0][:, None])
    put("gnorm", w["gla_norm"][0][:, None])
    put("lq", _np.stack([w["diff_lambda_q1"][0], w["diff_lambda_q2"][0]], 1))
    put("lk", _np.stack([w["diff_lambda_k1"][0], w["diff_lambda_k2"][0]], 1))
    put("bgate", w["gla_b_gate"][0].reshape(2, 2, P).transpose(2, 0, 1).reshape(P, 4))
    put("lre", w["s5_lambda_re"][0].transpose(0, 2, 1).reshape(P, G))
    put("lim", w["s5_lambda_im"][0].transpose(0, 2, 1).reshape(P, G))
    put("lstep", _np.repeat(w["s5_log_step"][0], NS, axis=0))
    put("s5d", w["s5_d"][0].T)
    put("eps", _np.full((P, 1), EPS, _np.float32))
    put("one", _np.ones((P, 1), _np.float32))
    mask = _np.ones((P, NCH), _np.float32)
    mask[:NS, [0, TP // SC]] = 0
    mask[NS:, [TP // SC - 1, NCH - 1]] = 0
    put("chunkmask", mask)
    put("ident", _np.eye(P, dtype=_np.float32))
    put("ones", _np.ones((P, P), _np.float32))
    put("ones64", _np.kron(_np.eye(2, dtype=_np.float32), _np.ones((64, 64), _np.float32)))
    put("dist", _np.abs(_np.arange(P)[:, None] + 384 - _np.arange(DIST)[None, :]).astype(_np.float32))

    b_ri = [w[n][0].transpose(0, 2, 1, 3).reshape(P, G * GC) for n in ("s5_b_re", "s5_b_im")]
    c_ri = [w[n][0].transpose(0, 3, 1, 2).reshape(P, G * GC) for n in ("s5_c_re", "s5_c_im")]
    bc = _np.stack(b_ri + c_ri)

    def units(a):
        n = a.shape[1] // UC
        return a.reshape(KT, P, n, UC).transpose(2, 1, 0, 3).reshape(n, P, KT * UC)

    ev = w["ev_w_in"][0]
    u_, q_, k_, v_, og_, glr_ = _np.split(ev, [512, 768, 1024, 1536, 2048], axis=1)
    parts = [units(_np.concatenate([u_, q_, k_], 1)), units(_np.concatenate([v_, og_], 1)), units(w["ev_w_out"][0])]

    def tail(layer):
        r = [units(w["x_w_kv"][layer]), units(w["x_w_q"][layer]), units(w["x_w_o"][layer])]
        for fb in range(FB):
            r.append(units(w["mlp_w1"][layer][:, fb * 1024:(fb + 1) * 1024]))
            r.append(units(w["mlp_w2"][layer][fb * 1024:(fb + 1) * 1024]))
        return r

    parts += tail(0) + [units(w["od_w_in"][0]), units(w["od_w_out"][0])] + tail(1)
    wgate = _np.zeros((2 * 16, 2, 256), _np.float32)
    for z in range(2):
        wgate[16 * z:16 * z + 16, z] = w["gla_w_gate"][0][z]
    j, i = _np.arange(P)[:, None], _np.arange(P)[None, :]
    same = j // CH == i // CH
    put("masks", _np.concatenate([same & (j <= i), same & (j >= i)], 1).astype(_np.float32))

    arrays = {
        "params": par,
        "x_in": _np.concatenate([w["x_prompt"][0], w["x_sample"][0]], 0).T,
        "mem_in": _np.concatenate([w["mem_prompt"][0], w["mem_sample"][0]], 0).T,
        "wstream": _np.concatenate(parts, 0),
        "wglr": glr_.reshape(KT, P, 32).transpose(1, 0, 2),
        "wglu": w["s5_w_glu"][0].reshape(4, P, 512).transpose(1, 0, 2),
        "wgate": wgate,
        "bc": bc,
    }
    arrays = {k: _np.ascontiguousarray(v) for k, v in arrays.items()}
    nc = _bacc.Bacc("TRN2", target_bir_lowering=False, num_devices=1)
    args = [nc.dram_tensor(k, a.shape, _mybir.dt.from_np(a.dtype), kind="ExternalInput").ap() for k, a in arrays.items()]
    scratch = [nc.dram_tensor(n, (512, SC, NCH), F32, kind="Internal").ap() for n in ("u_scratch", "y_scratch")]
    out = nc.dram_tensor("y_out", (D, T), F32, kind="ExternalOutput").ap()
    build(nc, *args, *scratch, out)
    r = _run(nc, [arrays], core_ids=[0])
    y = r.results[0]["y_out"].T
    return (y[None, :TP], y[None, TP:])
```

```python
import math
from contextlib import ExitStack

import numpy as np

import concourse.bass as bass
from concourse import mybir

F32 = mybir.dt.float32
F32R = mybir.dt.float32r
U8 = mybir.dt.uint8
ALU = mybir.AluOpType
ACT = mybir.ActivationFunctionType
AX = mybir.AxisListType

P = 128
D = 1024
KT = D // P
TP, TS = 512, 256
T = TP + TS
TT = T // P
M = 512
UC = 256
RAW = 2
SPL = 2
UPP = 4
DEPTH = 2
FB = 4
EPS = 1e-6
G, NS, GC = 32, 64, 16
SC = 8
NCH = T // SC
GB = 8
NB = G // GB
LAG = 2 * SC - 1
POS = SC + 2
GH, DK, DV, CH = 4, 64, 128, 64
NC12 = T // CH
DH = 8
XH = 4
LAMBDA_INIT = 0.8 - 0.6 * math.exp(-0.3)
DIST = 896
MAGIC = 12582912.0
TWO_PI_HI = 6.28125
TWO_PI_LO = 2 * math.pi - 6.28125


def _param_columns():
    widths = [("mix0", 8), ("mix1", 8), ("cross0", 8), ("cross1", 8), ("mem0", 8), ("mem1", 8), ("mlp0", 8),
              ("mlp1", 8), ("xq0", 2), ("xq1", 2), ("xk0", 2), ("xk1", 2), ("dq", 1), ("dk", 1), ("dnorm", 1),
              ("gnorm", 1), ("lq", 2), ("lk", 2), ("bgate", 4), ("lre", 32), ("lim", 32), ("lstep", 32), ("s5d", 32),
              ("eps", 1), ("one", 1), ("ident", 128), ("ones", 128), ("ones64", 128)]
    at, out = 0, {}
    for name, w in widths:
        out[name] = (at, w)
        at += w
    return out, at


COLS, NPAR = _param_columns()
TAB = {"dist": (0, DIST), "masks": (DIST, 256), "chunkmask": (DIST + 256, 96)}
NTAB = DIST + 256 + 96


class Signal:

    def __init__(self, ctx, nc, name):
        self.sem = ctx.enter_context(nc.semaphore(name))
        self.base = 0

    def at(self, n):
        return self.base + n


class Chain:

    def __init__(self, sig):
        self.sig = sig
        self.n = 0
        self.eng = None
        self.reg = None

    def start(self, eng):
        self.eng, self.n = eng, 0

    def loop(self, reg, per):
        self.reg, self.per, self.in_loop = reg, per, 0

    def end_loop(self, times):
        assert self.in_loop == self.per, (self.in_loop, self.per)
        self.n += self.per * times
        self.reg = None

    def __call__(self, ins):
        ins.then_inc(self.sig.sem, 1)
        if self.reg is None:
            self.n += 1
            self.eng.wait_ge(self.sig.sem, self.sig.base + self.n)
        else:
            self.in_loop += 1
            self.eng.wait_ge(self.sig.sem, self.reg * self.per + (self.sig.base + self.n + self.in_loop))

    def close(self):
        self.sig.base += self.n
        self.n = 0


def build(nc, params, x_in, mem_in, wstream, wglr_in, wglu_in, wgate_in, bc_in, tab_in, u_dram, y_dram, out):
    ctx = ExitStack()
    with ctx:
        def sb(name, shape, dt=F32, on=ctx):
            return on.enter_context(nc.sbuf_tensor(name, shape, dt))

        def sig(name):
            return Signal(ctx, nc, name)

        par = sb("par", [P, NPAR])
        x = sb("x", [P, KT, T])
        raw = sb("raw", [P, RAW, KT, UC])
        rstd = sb("rstd", [P, T])
        sq = sb("sq", [P, 2, T])
        gains = sb("gains", [P, 8])
        ps = ctx.enter_context(nc.psum_tensor("ps", [P, 8, 512], F32))

        def pcol(name, lo=0, n=None):
            a, w = COLS[name]
            return par[:, a + lo:a + lo + (w if n is None else n)]

        ident, ones, ones64 = pcol("ident"), pcol("ones"), pcol("ones64")

        def banks(b, n=T):
            return ps[:, b:b + 2, :].rearrange("p b n -> p (b n)")[:, 0:n]

        loaded = sig("loaded")
        w_loaded = [sig(f"w_loaded{s}") for s in range(RAW)]
        w_high = sig("w_high")
        w_ready = sig("w_ready")
        in_high = sig("in_high")
        in_made = sig("in_made")
        tile_done = sig("tile_done")
        tile_free = sig("tile_free")
        act_ready = sig("act_ready")
        sq_ready = sig("sq_ready")
        sq_used = sig("sq_used")
        root_ready = sig("root_ready")
        normed = sig("normed")
        hid_free = sig("hid_free")
        hid_made = sig("hid_made")
        hid_high = sig("hid_high")
        hid_ready = sig("hid_ready")
        dchain = sig("dchain")
        achain = sig("achain")
        pchain = sig("pchain")
        dve_chain, act_chain, pool_chain = Chain(dchain), Chain(achain), Chain(pchain)
        ev = {n: sig(n) for n in ("ev0", "ev1", "ev2", "ev3", "ev4", "ev5", "ev6", "ev7", "ev8", "ev9", "ev10",
                                  "ev11", "ev12", "ev13", "ev14", "ev15")}
        dma = {n: sig(n) for n in ("dma0", "dma1", "dma2", "dma3")}
        state = {"G": 0}

        NU = wstream.shape[0]
        serial = [0]

        class Split:

            def __init__(self, on, cols=T):
                serial[0] += 1
                n = serial[0]
                self.in_h = sb(f"in_h{n}", [P, KT, cols], F32R, on=on)
                self.in_l = sb(f"in_l{n}", [P, KT, cols], F32R, on=on)
                self.w_h = sb(f"w_h{n}", [P, SPL, KT, UC], F32R, on=on)
                self.w_l = sb(f"w_l{n}", [P, SPL, KT, UC], F32R, on=on)

        def sp_weights(sp, n):
            u0 = state["G"] * UPP

            def one(i, s):
                sp.wait_ge(w_ready.sem, i + (w_ready.base + s + 1))
                sp.dma_start(raw[:, s, :, :], wstream[bass.ds(i + (u0 + RAW + s), 1)]
                             .rearrange("a p n -> p (a n)").rearrange("p (k n) -> p k n", k=KT))\
                    .then_inc(w_loaded[s].sem, 16)
            n_load = min(n, NU - RAW - u0)
            if n_load > 0:
                with sp.Fori(0, n_load // RAW, 1) as i:
                    for s in range(RAW):
                        one(i * RAW, s)

        def act_high(a, sp_, u, i=0):
            s = u % SPL
            a.wait_ge(w_loaded[s].sem, i * 8 + 16 * ((state["G"] * UPP + u) // RAW + 1))
            if u >= SPL or not isinstance(i, int):
                a.wait_ge(tile_done.sem, i * 2 + (tile_done.base + 2 * (u - SPL + 1)))
            nc.scalar.activation(sp_.w_h[:, s, :, :], raw[:, s, :, :], ACT.Copy).then_inc(w_high.sem, 1)

        def pool_low(g, sp_, n):
            with g.Fori(0, n // SPL, 1) as i:
                for s in range(SPL):
                    g.wait_ge(w_high.sem, i * SPL + (w_high.base + s + 1))
                    nc.gpsimd.tensor_tensor(sp_.w_l[:, s, :, :], raw[:, s, :, :], sp_.w_h[:, s, :, :].bitcast(F32), ALU.subtract)\
                        .then_inc(w_ready.sem, 1)

        def pe_product(pe, sp_, kind, g=0, rhs=None, ready=None, ready_at=0, cols=T, free_wait=None):
            in_h, in_l = (sp_.in_h, sp_.in_l) if rhs is None else rhs
            for u in range(UPP):
                s = u % SPL
                for half in range(2):
                    n = 2 * u + half
                    if half == 0:
                        pe.wait_ge(w_ready.sem, g * UPP + (w_ready.base + u + 1))
                    if free_wait is not None:
                        free_wait(n)
                    elif n >= 2 or g > 0 or tile_free.base > 0:
                        pe.wait_ge(tile_free.sem, tile_free.base + g * 8 + n - 1)
                    bank = 2 * half
                    parts = ((sp_.w_h, in_h), (sp_.w_h, in_l), (sp_.w_l, in_h))
                    if kind[u] == "f":
                        for k in range(KT):
                            if n == 0 and ready is not None:
                                pe.wait_ge(ready.sem, ready_at + (ready.base + k + 1))
                            for j, (w_, x_) in enumerate(parts):
                                lhs = w_[:, s, k, P * half:P * half + P]
                                st, en = k == 0 and j == 0, k == KT - 1 and j == 2
                                last = nc.tensor.matmul(ps[:, bank, :], lhs, x_[:, k, 0:512], start=st, stop=en)
                                if cols > 512:
                                    last = nc.tensor.matmul(ps[:, bank + 1, 0:cols - 512], lhs, x_[:, k, 512:cols],
                                                            start=st, stop=en)
                    else:
                        per = cols // P // 2
                        if n == 0 and ready is not None:
                            pe.wait_ge(ready.sem, ready_at + (ready.base + KT))
                        for q in range(per):
                            tok = (half * per + q) * P
                            dst = banks(bank, 1024)[:, q * UC:(q + 1) * UC]
                            for k in range(KT):
                                for j, (w_, x_) in enumerate(parts):
                                    last = nc.tensor.matmul(dst, x_[:, k, tok:tok + P], w_[:, s, k, :],
                                                            start=(k == 0 and j == 0), stop=(k == KT - 1 and j == 2))
                    last.then_inc(tile_done.sem, 1)

        def close_products(n, n_free=None):
            tile_done.base += 8 * n
            tile_free.base += 8 * (n if n_free is None else n_free)
            state["G"] += n
            w_high.base += UPP * n
            w_ready.base += UPP * n

        def wait_tile(eng, n, g=0):
            eng.wait_ge(tile_done.sem, g * 8 + (tile_done.base + n + 1))

        def act_rsqrt(eng, dst, mean, square, src, scale):
            nc.scalar.activation(dst, src, ACT.Ln, bias=pcol("eps"), scale=scale).then_inc(achain.sem, 1)
            nc.scalar.activation(mean, src, ACT.Identity, bias=pcol("eps"), scale=scale)
            eng.wait_ge(achain.sem, achain.base + act_chain.n + 1)
            nc.scalar.activation(dst, dst, ACT.Exp, scale=-0.5).then_inc(achain.sem, 1)
            eng.wait_ge(achain.sem, achain.base + act_chain.n + 2)
            nc.scalar.activation(square, dst, ACT.Square).then_inc(root_ready.sem, 1)
            act_chain.n += 2

        def refine(root, mean, square):
            dve_chain(nc.vector.scalar_tensor_tensor(mean, mean, -0.5, square, ALU.mult, ALU.mult))
            dve_chain(nc.vector.scalar_tensor_tensor(root, mean, 1.5, root, ALU.add, ALU.mult))

        def act_norm(eng, src, cols=T, ready=None):
            for k in range(KT):
                if k >= 2:
                    eng.wait_ge(sq_used.sem, sq_used.at(k - 1))
                if ready is not None and k == 0:
                    eng.wait_ge(*ready)
                nc.scalar.activation(sq[:, k % 2, 0:cols], src[:, k, 0:cols], ACT.Square).then_inc(sq_ready.sem, 1)
            eng.wait_ge(sq_used.sem, sq_used.at(KT))
            act_rsqrt(eng, rstd[:, 0:cols], sq[:, 0, 0:cols], sq[:, 1, 0:cols], banks(4, cols), 1.0 / D)

        def pe_norm(eng, cols=T):
            for k in range(KT):
                eng.wait_ge(sq_ready.sem, sq_ready.at(k + 1))
                last = nc.tensor.matmul(ps[:, 4, 0:512], ones, sq[:, k % 2, 0:512], start=(k == 0), stop=(k == KT - 1))
                if cols > 512:
                    last = nc.tensor.matmul(ps[:, 5, 0:cols - 512], ones, sq[:, k % 2, 512:cols],
                                            start=(k == 0), stop=(k == KT - 1))
                last.then_inc(sq_used.sem, 1)

        def dve_norm(eng, src, gain, sp_, cols=T):
            eng.wait_ge(root_ready.sem, root_ready.at(1))
            refine(rstd[:, 0:cols], sq[:, 0, 0:cols], sq[:, 1, 0:cols])

            def low(k):
                eng.wait_ge(in_high.sem, in_high.at(k + 1))
                nc.vector.tensor_tensor(sp_.in_l[:, k, 0:cols], sq[:, k % 2, 0:cols], sp_.in_h[:, k, 0:cols].bitcast(F32),
                                        ALU.subtract).then_inc(act_ready.sem, 1)
            for k in range(KT):
                if k >= 2:
                    eng.wait_ge(act_ready.sem, act_ready.at(k - 1))
                nc.vector.scalar_tensor_tensor(sq[:, k % 2, 0:cols], src[:, k, 0:cols], pcol(gain, k, 1), rstd[:, 0:cols],
                                               ALU.mult, ALU.mult).then_inc(in_made.sem, 1)
                if k >= 1:
                    low(k - 1)
            low(KT - 1)

        def act_norm_high(eng, sp_, cols=T):
            for k in range(KT):
                eng.wait_ge(in_made.sem, in_made.at(k + 1))
                nc.scalar.activation(sp_.in_h[:, k, 0:cols], sq[:, k % 2, 0:cols], ACT.Copy).then_inc(in_high.sem, 1)

        def dve_split(eng, src, sp_, cols=T):
            for k in range(KT):
                nc.vector.tensor_copy(sp_.in_h[:, k, 0:cols], src[:, k, 0:cols]).then_inc(in_high.sem, 1)
            for k in range(KT):
                eng.wait_ge(in_high.sem, in_high.at(k + 1))
                nc.vector.tensor_tensor(sp_.in_l[:, k, 0:cols], src[:, k, 0:cols], sp_.in_h[:, k, 0:cols].bitcast(F32),
                                        ALU.subtract).then_inc(act_ready.sem, 1)

        def close_norm():
            sq_ready.base += KT
            sq_used.base += KT
            root_ready.base += 1
            in_high.base += KT
            in_made.base += KT

        def head_norm_stage(items, mat, width, cols=T, extra=None):
            n_items = len(items)
            hn = ExitStack()
            serial[0] += 1
            rstd_b = sb(f"rstd_b{serial[0]}", [P, T], on=hn)

            nt = sb(f"newton{serial[0]}", [P, 2, 2, T], on=hn)

            def rstd2(i):
                return rstd if i % 2 == 0 else rstd_b

            with nc.Block() as block:
                @block.scalar
                def _(a):
                    c = 0
                    for i, (srcs, gn, dsts) in enumerate(items):
                        for j, s in enumerate(srcs):
                            if c >= 2:
                                a.wait_ge(sq_used.sem, sq_used.at(c - 1))
                            nc.scalar.activation(sq[:, c % 2, 0:cols], s, ACT.Square).then_inc(sq_ready.sem, 1)
                            c += 1
                        a.wait_ge(sq_used.sem, sq_used.at(c))
                        if i >= 2:
                            a.wait_ge(normed.sem, normed.at(i - 1))
                        act_rsqrt(a, rstd2(i)[:, 0:cols], nt[:, i % 2, 0, 0:cols], nt[:, i % 2, 1, 0:cols],
                                  banks(4 + 2 * (i % 2), cols), 1.0 / width)
                    act_chain.close()

                @block.tensor
                def _(pe):
                    c = 0
                    for i, (srcs, gn, dsts) in enumerate(items):
                        if i >= 2:
                            pe.wait_ge(root_ready.sem, root_ready.at(i - 1))
                        for j, s in enumerate(srcs):
                            pe.wait_ge(sq_ready.sem, sq_ready.at(c + 1))
                            st, sp_ = j == 0, j == len(srcs) - 1
                            b = 4 + 2 * (i % 2)
                            last = nc.tensor.matmul(ps[:, b, :], mat, sq[:, c % 2, 0:512], start=st, stop=sp_)
                            if cols > 512:
                                last = nc.tensor.matmul(ps[:, b + 1, 0:cols - 512], mat, sq[:, c % 2, 512:cols],
                                                        start=st, stop=sp_)
                            last.then_inc(sq_used.sem, 1)
                            c += 1

                @block.vector
                def _(v):
                    dve_chain.start(v)
                    for i, (srcs, gn, dsts) in enumerate(items):
                        v.wait_ge(root_ready.sem, root_ready.at(i + 1))
                        refine(rstd2(i)[:, 0:cols], nt[:, i % 2, 0, 0:cols], nt[:, i % 2, 1, 0:cols])
                        for s, g_, d in zip(srcs, gn, dsts):
                            last = nc.vector.scalar_tensor_tensor(d, s, g_, rstd2(i)[:, 0:cols], ALU.mult, ALU.mult)
                        last.then_inc(normed.sem, 1)
                        if extra is not None:
                            extra(v, i)
                    dve_chain.close()
            hn.close()
            n_sq = sum(len(i[0]) for i in items)
            sq_ready.base += n_sq
            sq_used.base += n_sq
            root_ready.base += n_items
            normed.base += n_items

        with nc.Block() as block:
            @block.sync
            def _(sp):
                sp.dma_start(par[:, :], params).then_inc(loaded.sem, 16)
                sp.dma_start(x[:, :, :], x_in.rearrange("(k p) t -> p k t", p=P)).then_inc(loaded.sem, 16)
                for s in range(RAW):
                    sp.dma_start(raw[:, s, :, :], wstream[s].rearrange("p (k n) -> p k n", k=KT))\
                        .then_inc(w_loaded[s].sem, 16)
                sp.wait_ge(loaded.sem, 32)

            @block.scalar
            def _(a):
                nc.scalar.preload_act_table_set("natural_log_exp_and_others")

            @block.vector
            def _(v):
                v.wait_ge(loaded.sem, 32)
                nc.vector.tensor_scalar(gains[:, 0:1], pcol("dq"), float(64 ** -0.5), None, ALU.mult).then_inc(ev["ev0"].sem, 1)
                nc.vector.tensor_scalar(gains[:, 1:2], pcol("dnorm"), 1.0 - LAMBDA_INIT, None, ALU.mult).then_inc(ev["ev0"].sem, 1)
                nc.vector.tensor_scalar(gains[:, 2:4], pcol("xq0"), 1.0 / 16.0, None, ALU.mult).then_inc(ev["ev0"].sem, 1)
                nc.vector.tensor_scalar(gains[:, 4:6], pcol("xq1"), 1.0 / 16.0, None, ALU.mult).then_inc(ev["ev0"].sem, 1)
                v.wait_ge(ev["ev0"].sem, 4)
        loaded.base += 32
        ev["ev0"].base += 4

        def product_stage(src, kinds, evac, norm=None, cols=T, evac_engine="vector",
                          dve_pre=None, act_pre=None, dve_post=None, pe_post=None):
            n = len(kinds)
            local = ExitStack()
            sp_ = Split(local, cols)
            with nc.Block() as block:
                @block.sync
                def _(sp):
                    sp_weights(sp, n * UPP)

                @block.gpsimd
                def _(g):
                    pool_low(g, sp_, n * UPP)

                @block.tensor
                def _(pe):
                    if norm is not None:
                        pe_norm(pe, cols)
                    for g in range(n):
                        pe_product(pe, sp_, kinds[g], g, cols=cols, ready=act_ready if g == 0 else None)
                    if pe_post is not None:
                        pe_post(pe, sp_)

                @block.vector
                def _(v):
                    dve_chain.start(v)
                    if dve_pre is not None:
                        dve_pre(v)
                    if norm is not None:
                        dve_norm(v, src, norm, sp_, cols)
                    else:
                        dve_split(v, src, sp_, cols)
                    if dve_post is not None:
                        dve_post(v)
                    if evac_engine == "vector":
                        for g in range(n):
                            for i in range(8):
                                wait_tile(v, i, g)
                                evac(v, g, i)
                    dve_chain.close()

                @block.scalar
                def _(a):
                    if act_pre is not None:
                        act_pre(a)
                    for u in range(SPL):
                        act_high(a, sp_, u)
                    if norm is not None:
                        act_norm(a, src, cols)
                        act_norm_high(a, sp_, cols)
                    for u in range(n * UPP):
                        if 1 <= u and u + 1 < n * UPP:
                            act_high(a, sp_, u + 1)
                        if evac_engine == "scalar":
                            for i in (2 * u, 2 * u + 1):
                                wait_tile(a, i)
                                evac(a, i // 8, i % 8)
                    act_chain.close()
            if norm is not None:
                close_norm()
            else:
                in_high.base += KT
            act_ready.base += KT
            close_products(n)
            local.close()

        def free(ins):
            return ins.then_inc(tile_free.sem, 1)

        def add_residual(v, g, i):
            free(nc.vector.tensor_tensor(x[:, i, :], banks(2 * (i % 2)), x[:, i, :], ALU.add))

        def mlp(layer):
            local = ExitStack()
            sp_ = Split(local)
            h_h = sb(f"h_h{layer}", [P, KT, T], F32R, on=local)
            h_l = sb(f"h_l{layer}", [P, KT, T], F32R, on=local)
            ht = sb(f"ht{layer}", [P, 2, T], on=local)
            with nc.Block() as block:
                @block.sync
                def _(sp):
                    sp_weights(sp, 2 * FB * UPP)

                @block.gpsimd
                def _(g):
                    pool_low(g, sp_, 2 * FB * UPP)

                @block.tensor
                def _(pe):
                    pe_norm(pe)
                    pe.wait_ge(act_ready.sem, act_ready.at(KT))
                    with pe.Fori(0, FB, 1) as fb:
                        def up_wait(n):
                            if n < 2:
                                pe.wait_ge(tile_free.sem, fb * 8 + (tile_free.base + n - 1))
                            else:
                                pe.wait_ge(hid_free.sem, fb * 8 + (hid_free.base + n - 1))

                        def down_wait(n):
                            if n < 2:
                                pe.wait_ge(hid_free.sem, fb * 8 + (hid_free.base + 8 + n - 1))
                            else:
                                pe.wait_ge(tile_free.sem, fb * 8 + (tile_free.base + n - 1))
                        pe_product(pe, sp_, "ffff", fb * 2, free_wait=up_wait)
                        pe_product(pe, sp_, "ffff", fb * 2 + 1, rhs=(h_h, h_l), ready=hid_ready, ready_at=fb * KT,
                                   free_wait=down_wait)

                @block.vector
                def _(v):
                    dve_chain.start(v)
                    dve_norm(v, x, f"mlp{layer}", sp_)
                    with v.Fori(0, FB, 1) as fb:
                        for i in range(8):
                            v.wait_ge(hid_made.sem, fb * 8 + (hid_made.base + i + 1))
                            nc.vector.tensor_copy(h_h[:, i, :], ht[:, i % 2, :]).then_inc(hid_high.sem, 1)
                            v.wait_ge(hid_high.sem, fb * 8 + (hid_high.base + i + 1))
                            nc.vector.tensor_tensor(h_l[:, i, :], ht[:, i % 2, :], h_h[:, i, :].bitcast(F32), ALU.subtract)\
                                .then_inc(hid_ready.sem, 1)
                        for i in range(8):
                            wait_tile(v, i, fb * 2 + 1)
                            add_residual(v, 0, i)
                    dve_chain.close()

                @block.scalar
                def _(a):
                    act_high(a, sp_, 0)
                    act_high(a, sp_, 1)
                    act_norm(a, x)
                    act_norm_high(a, sp_)

                    def up(i, fb):
                        wait_tile(a, i, fb * 2)
                        nc.scalar.activation(sq[:, i % 2, :], banks(2 * (i % 2)), ACT.Relu).then_inc(hid_free.sem, 1)
                        a.wait_ge(hid_free.sem, fb * 8 + (hid_free.base + i + 1))
                        if fb * 8 + i >= 2:
                            a.wait_ge(hid_ready.sem, fb * 8 + (hid_ready.base + i - 1))
                        nc.scalar.activation(ht[:, i % 2, :], sq[:, i % 2, :], ACT.Square).then_inc(hid_made.sem, 1)

                    for fb in range(FB):
                        for u in range(2 * UPP):
                            n = 2 * UPP * fb + u + 1
                            if 2 <= n < 2 * UPP * FB:
                                act_high(a, sp_, n)
                            if u < UPP:
                                up(2 * u, fb)
                                up(2 * u + 1, fb)
                    act_chain.close()
            close_norm()
            act_ready.base += KT
            close_products(2 * FB, FB)
            hid_free.base += 8 * FB
            hid_ready.base += KT * FB
            hid_made.base += KT * FB
            hid_high.base += KT * FB
            local.close()

        def cross(layer):
            local, l_mem = ExitStack(), ExitStack()
            km = sb(f"km{layer}", [P, KT, M], on=local)
            vm = sb(f"vm{layer}", [P, 4, D], on=local)
            mem = sb(f"mem{layer}", [P, KT, M], on=l_mem)
            ld = dma["dma0"]
            with nc.Block() as block:
                @block.sync
                def _(sp):
                    sp.dma_start(mem[:, :, :], mem_in.rearrange("(k p) t -> p k t", p=P)).then_inc(ld.sem, 16)
                    sp.wait_ge(ld.sem, ld.at(16))
            ld.base += 16

            def evac_mem(a, g, i):
                if g == 0:
                    free(nc.scalar.activation(km[:, i, :], ps[:, 2 * (i % 2), :], ACT.Copy))
                else:
                    s, half = i // 2, i % 2
                    free(nc.scalar.activation(vm[:, 2 * half:2 * half + 2, s * UC:(s + 1) * UC],
                                              ps[:, 2 * half, :].rearrange("p (j n) -> p j n", j=2), ACT.Copy))
            product_stage(mem, ["ffff", "tttt"], evac_mem, norm=f"mem{layer}", cols=M, evac_engine="scalar")
            l_mem.close()
            head_norm_stage([([km[:, 2 * h + j, :] for j in range(2)], [pcol(f"xk{layer}", j, 1) for j in range(2)],
                              [km[:, 2 * h + j, :] for j in range(2)]) for h in range(XH)], ones, 256, cols=M)

            def evac_q(a, g, i):
                free(nc.scalar.activation(qx[:, i, :], banks(2 * (i % 2)), ACT.Copy))
            qx = sb(f"qx{layer}", [P, KT, T], on=local)
            product_stage(x, ["ffff"], evac_q, norm=f"cross{layer}", evac_engine="scalar")
            head_norm_stage([([qx[:, 2 * h + j, :] for j in range(2)], [gains[:, 2 + 2 * layer + j:3 + 2 * layer + j] for j in range(2)],
                              [qx[:, 2 * h + j, :] for j in range(2)]) for h in range(XH)], ones, 256)

            att = ExitStack()
            s_sb = sb(f"xs{layer}", [P, TT, 256], on=att)
            pt = sb(f"xpt{layer}", [P, 2, T], on=att)
            st = sb(f"xst{layer}", [P, 4, TT], on=att)
            sc_done, neg_ready, exp_done, p_ready, tr_done, pt_ready, o_done, o_free = (ev[f"ev{i}"] for i in range(8))
            with nc.Block() as block:
                @block.tensor
                def _(pe):
                    for h in range(XH):
                        if h >= 1:
                            pe.wait_ge(exp_done.sem, exp_done.at(h))
                        for q in range(TT):
                            mo = 0 if q < 4 else 256
                            dst = ps[:, q // 2, (q % 2) * 256:(q % 2) * 256 + 256]
                            for j in range(2):
                                last = nc.tensor.matmul(dst, qx[:, 2 * h + j, q * P:(q + 1) * P], km[:, 2 * h + j, mo:mo + 256],
                                                        start=(j == 0), stop=(j == 1))
                        last.then_inc(sc_done.sem, 1)
                        pe.wait_ge(p_ready.sem, p_ready.at(h + 1))
                        if h >= 1:
                            pe.wait_ge(pt_ready.sem, pt_ready.at(h))
                        for q in range(TT):
                            for j in range(2):
                                c = (q * 2 + j) * P
                                last = nc.tensor.transpose(ps[:, 4 + c // 512, c % 512:c % 512 + P],
                                                           s_sb[:, q, j * P:(j + 1) * P], ident)
                        last.then_inc(tr_done.sem, 1)
                        pe.wait_ge(pt_ready.sem, pt_ready.at(h + 1))
                        for j in range(2):
                            n = 2 * h + j
                            if n >= 1:
                                pe.wait_ge(o_free.sem, o_free.at(n))
                            for kt in range(2):
                                lhs = vm[:, kt, (2 * h + j) * P:(2 * h + j + 1) * P]
                                nc.tensor.matmul(ps[:, 7, :], lhs, pt[:, kt, 0:512], start=(kt == 0), stop=(kt == 1))
                            for kt in range(2):
                                lhs = vm[:, 2 + kt, (2 * h + j) * P:(2 * h + j + 1) * P]
                                last = nc.tensor.matmul(ps[:, 3, 0:256], lhs, pt[:, kt, 512:T], start=(kt == 0), stop=(kt == 1))
                            last.then_inc(o_done.sem, 1)

                @block.vector
                def _(v):
                    dve_chain.start(v)
                    for h in range(XH):
                        v.wait_ge(sc_done.sem, sc_done.at(h + 1))
                        if h >= 1:
                            v.wait_ge(exp_done.sem, exp_done.at(h))
                        sc = ps[:, 0:3, :].rearrange("p b (q n) -> p (b q) n", q=2)
                        dve_chain(nc.vector.tensor_reduce(st[:, 0, :], sc, AX.X, ALU.max))
                        nc.vector.tensor_scalar(st[:, 1, :], st[:, 0, :], -1.0, None, ALU.mult).then_inc(neg_ready.sem, 1)
                        v.wait_ge(exp_done.sem, exp_done.at(h + 1))
                        dve_chain(nc.vector.reciprocal(st[:, 3, :], st[:, 2, :]))
                        nc.vector.tensor_tensor(s_sb[:, :, :], s_sb[:, :, :],
                                                st[:, 3, :].unsqueeze(2).to_broadcast([P, TT, 256]), ALU.mult)\
                            .then_inc(p_ready.sem, 1)
                        for j in range(2):
                            n = 2 * h + j
                            v.wait_ge(o_done.sem, o_done.at(n + 1))
                            nc.vector.tensor_copy(qx[:, n, 0:512], ps[:, 7, :])
                            nc.vector.tensor_copy(qx[:, n, 512:T], ps[:, 3, 0:256]).then_inc(o_free.sem, 1)
                    dve_chain.close()

                @block.scalar
                def _(a):
                    for h in range(XH):
                        a.wait_ge(neg_ready.sem, neg_ready.at(h + 1))
                        if h >= 1:
                            a.wait_ge(tr_done.sem, tr_done.at(h))
                        for q in range(TT):
                            last = nc.scalar.activation(s_sb[:, q, :], ps[:, q // 2, (q % 2) * 256:(q % 2) * 256 + 256],
                                                        ACT.Exp, bias=st[:, 1, q:q + 1], accum_out=st[:, 2, q:q + 1])
                        last.then_inc(exp_done.sem, 1)
                        a.wait_ge(tr_done.sem, tr_done.at(h + 1))
                        if h >= 1:
                            a.wait_ge(o_done.sem, o_done.at(2 * h))
                        tr = ps[:, 4:7, :].rearrange("p b n -> p (b n)").rearrange("p (q j n) -> p j q n", j=2, n=P)
                        nc.scalar.activation(pt[:, 0, :].rearrange("p (q n) -> p q n", n=P), tr[:, 0], ACT.Copy)
                        nc.scalar.activation(pt[:, 1, :].rearrange("p (q n) -> p q n", n=P), tr[:, 1], ACT.Copy)\
                            .then_inc(pt_ready.sem, 1)
            for s_ in (sc_done, neg_ready, exp_done, p_ready, tr_done, pt_ready):
                s_.base += XH
            o_done.base += 2 * XH
            o_free.base += 2 * XH
            att.close()
            product_stage(qx, ["ffff"], add_residual)
            local.close()

        def diff_attention():
            qkv, local = ExitStack(), ExitStack()
            b1, b2, b3 = (sb(n, [P, KT, T], on=qkv) for n in ("dq_sb", "dk_sb", "dv_sb"))

            def evac(a, g, i):
                if g < 2:
                    free(nc.scalar.activation((b1, b2)[g][:, i, :], banks(2 * (i % 2)), ACT.Copy))
                else:
                    s, half = i // 2, i % 2
                    src = banks(2 * half).rearrange("p (j n) -> p j n", j=3)
                    free(nc.scalar.activation(vtok[:, 3 * half:3 * half + 3, s * UC:(s + 1) * UC], src, ACT.Copy))
            vtok = b3[:, :, :].rearrange("p k t -> p (k t)").rearrange("p (j n) -> p j n", j=TT)
            product_stage(x, ["ffff", "ffff", "tttt"], evac, norm="mix1", evac_engine="scalar")
            head_norm_stage([([b1[:, h, :]], [gains[:, 0:1]], [b1[:, h, :]]) for h in range(DH)]
                            + [([b2[:, h, :]], [pcol("dk")], [b2[:, h, :]]) for h in range(DH)], ones64, 64)

            sc = sb("dsc", [P, 2, 2, 512], on=local)
            bias = sb("dbias", [P, 2, DIST], on=local)
            at = sb("dat", [P, 2, 512], on=local)
            st = sb("dst", [P, 2, 8], on=local)
            dist = sb("dist", [P, DIST], on=local)
            lam = sb("dlam", [P, 8], on=local)
            sc_done, neg_ready, exp_done, a_ready, tr_done, at_ready, o_done, o_free, bias_ready, bias_used, lam_a, lam_b, e0_ready = (
                ev[f"ev{i}"] for i in range(13))
            items = [(h, q) for h in range(DH) for q in range(TT)]
            with nc.Block() as block:
                @block.sync
                def _(sp):
                    sp.dma_start(dist[:, :], tab_in[:, TAB["dist"][0]:TAB["dist"][0] + DIST]).then_inc(dma["dma0"].sem, 16)

                @block.vector
                def _(v):
                    dve_chain.start(v)
                    nc.vector.tensor_tensor(lam[:, 0:2], pcol("lq"), pcol("lk"), ALU.mult).then_inc(lam_a.sem, 1)
                    v.wait_ge(lam_a.sem, lam_a.at(3))
                    dve_chain(nc.vector.tensor_tensor(lam[:, 4:5], lam[:, 3:4], lam[:, 2:3], ALU.subtract))
                    dve_chain(nc.vector.tensor_scalar(lam[:, 5:6], lam[:, 4:5], -LAMBDA_INIT, None, ALU.add))
                    for n, (h, q) in enumerate(items):
                        keys, k0 = (512, 0) if q < 4 else (256, 512)
                        b = n % 2
                        off = 384 - P * (q if q < 4 else q - 4)
                        if q == 0:
                            v.wait_ge(bias_ready.sem, bias_ready.at(h + 1))
                        v.wait_ge(sc_done.sem, sc_done.at(n + 1))
                        if n >= 2:
                            v.wait_ge(tr_done.sem, tr_done.at(n - 1))
                        for z in range(2):
                            nc.vector.tensor_tensor_reduce(
                                out=sc[:, b, z, 0:keys], in0=ps[:, 2 * b + z, 0:keys], in1=bias[:, h % 2, off:off + keys],
                                scale=1.0, scalar=-3.0e38, op0=ALU.add, op1=ALU.max, accum_out=st[:, b, z:z + 1])\
                                .then_inc(dchain.sem, 1)
                            dve_chain.n += 1
                        v.wait_ge(dchain.sem, dchain.base + dve_chain.n)
                        nc.vector.tensor_scalar(st[:, b, 2:4], st[:, b, 0:2], -1.0, None, ALU.mult).then_inc(neg_ready.sem, 1)
                        v.wait_ge(exp_done.sem, exp_done.at(n + 1))
                        dve_chain(nc.vector.reciprocal(st[:, b, 6:8], st[:, b, 4:6]))
                        dve_chain(nc.vector.tensor_tensor(st[:, b, 7:8], st[:, b, 7:8], lam[:, 5:6], ALU.mult))
                        dve_chain(nc.vector.tensor_scalar(sc[:, b, 0, 0:keys], sc[:, b, 0, 0:keys], st[:, b, 6:7], None, ALU.mult))
                        nc.vector.scalar_tensor_tensor(sc[:, b, 0, 0:keys], sc[:, b, 1, 0:keys], st[:, b, 7:8],
                                                       sc[:, b, 0, 0:keys], ALU.mult, ALU.add).then_inc(a_ready.sem, 1)
                    dve_chain.close()

                @block.gpsimd
                def _(g):
                    g.wait_ge(dma["dma0"].sem, dma["dma0"].at(16))
                    for h in range(DH):
                        if h >= 2:
                            g.wait_ge(neg_ready.sem, neg_ready.at(TT * (h - 1)))
                        nc.gpsimd.tensor_scalar(bias[:, h % 2, :], dist[:, :], -float(2.0 ** -(h + 1)), None, ALU.mult)\
                            .then_inc(bias_ready.sem, 1)

                @block.scalar
                def _(a):
                    a.wait_ge(lam_a.sem, lam_a.at(2))
                    nc.scalar.activation(lam[:, 2:4], ps[:, 7, 0:2], ACT.Exp).then_inc(lam_a.sem, 1)

                    def after(n):
                        h, q = items[n]
                        nk = 4 if q < 4 else 2
                        a.wait_ge(tr_done.sem, tr_done.at(n + 1))
                        if n >= 2:
                            a.wait_ge(o_done.sem, o_done.at(n - 1))
                        nc.scalar.activation(at[:, n % 2, 0:nk * P], ps[:, 4 + n % 2, 0:nk * P], ACT.Copy).then_inc(at_ready.sem, 1)
                        if q == TT - 1:
                            a.wait_ge(o_done.sem, o_done.at(n + 1))
                            nc.scalar.activation(b1[:, h, :], banks(6), ACT.Copy).then_inc(o_free.sem, 1)
                    for n, (h, q) in enumerate(items):
                        keys = 512 if q < 4 else 256
                        b = n % 2
                        a.wait_ge(neg_ready.sem, neg_ready.at(n + 1))
                        for z in range(2):
                            last = nc.scalar.activation(sc[:, b, z, 0:keys], sc[:, b, z, 0:keys], ACT.Exp,
                                                        bias=st[:, b, 2 + z:3 + z], accum_out=st[:, b, 4 + z:5 + z])
                        last.then_inc(exp_done.sem, 1)
                        if n >= 1:
                            after(n - 1)
                    after(len(items) - 1)

                @block.tensor
                def _(pe):
                    pe.wait_ge(lam_a.sem, lam_a.at(1))
                    nc.tensor.matmul(ps[:, 7, 0:2], ones, lam[:, 0:2], start=True, stop=True).then_inc(lam_a.sem, 1)

                    def scores(n):
                        h, q = items[n]
                        keys, k0 = (512, 0) if q < 4 else (256, 512)
                        if n >= 2:
                            pe.wait_ge(neg_ready.sem, neg_ready.at(n - 1))
                        for z in range(2):
                            rows = slice(64 * z, 64 * z + 64)
                            last = nc.tensor.matmul(ps[:, 2 * (n % 2) + z, 0:keys], b1[rows, h, q * P:(q + 1) * P],
                                                    b2[rows, h, k0:k0 + keys], start=True, stop=True)
                        last.then_inc(sc_done.sem, 1)

                    def values(n):
                        h, q = items[n]
                        nk, t0 = (4, 0) if q < 4 else (2, 4)
                        pe.wait_ge(a_ready.sem, a_ready.at(n + 1))
                        if n >= 2:
                            pe.wait_ge(at_ready.sem, at_ready.at(n - 1))
                        for j in range(nk):
                            last = nc.tensor.transpose(ps[:, 4 + n % 2, j * P:(j + 1) * P], sc[:, n % 2, 0, j * P:(j + 1) * P], ident)
                        last.then_inc(tr_done.sem, 1)

                    def outputs(n):
                        h, q = items[n]
                        nk, t0 = (4, 0) if q < 4 else (2, 4)
                        pe.wait_ge(at_ready.sem, at_ready.at(n + 1))
                        if q == 0 and h >= 1:
                            pe.wait_ge(o_free.sem, o_free.at(h))
                        if n == 0:
                            pe.wait_ge(lam_a.sem, lam_a.at(3))
                        for j in range(nk):
                            last = nc.tensor.matmul(banks(6)[:, q * P:(q + 1) * P], vtok[:, t0 + j, h * P:(h + 1) * P],
                                                    at[:, n % 2, j * P:(j + 1) * P], start=(j == 0), stop=(j == nk - 1))
                        last.then_inc(o_done.sem, 1)
                    scores(0)
                    for n in range(len(items)):
                        if n + 1 < len(items):
                            scores(n + 1)
                        values(n)
                        if n >= 1:
                            outputs(n - 1)
                    outputs(len(items) - 1)
            ni = len(items)
            for s_ in (sc_done, neg_ready, exp_done, a_ready, tr_done, at_ready, o_done):
                s_.base += ni
            o_free.base += DH
            bias_ready.base += DH
            lam_a.base += 3
            dma["dma0"].base += 16
            local.close()
            head_norm_stage([([b1[:, h, :]], [gains[:, 1:2]], [b1[:, h, :]]) for h in range(DH)], ones, 128)
            product_stage(b1, ["ffff"], add_residual)
            qkv.close()

        def s5_gla():
            outer, local, prep, s5mem = ExitStack(), ExitStack(), ExitStack(), ExitStack()
            b1 = sb("uqk", [P, KT, T], on=outer)
            b2 = sb("vog", [P, KT, T], on=outer)
            lr = sb("lr", [32, T], on=outer)
            sm = sb("s5small", [P, 32, G], on=local)
            names = ["step", "zr", "zi", "kk", "r", "rh", "sin", "sinh", "cos", "mag", "r8", "lbr", "lbi", "nr", "den", "cr",
                     "ci", "t0", "t1", "t2", "t3", "p2r", "p2i", "p4r", "p4i"]
            S = {n: sm[:, i, :] for i, n in enumerate(names)}
            bbar = sb("bbar", [P, 2, G, GC], on=local)
            cc = sb("cc", [P, 2, G, GC], on=local)
            qf = sb("qf", [P, 2, POS, G], on=local)
            qr = sb("qr", [P, 2, SC, G], on=local)
            pw = sb("pw", [P, 2, SC + 1, G], on=prep)
            wglr = sb("wglr_sb", [P, KT, 32], on=prep)
            bin_ = sb("bin", [P, 2, G, GC], on=prep)
            pc_in, pc_out = ev["ev0"], ev["ev1"]
            ld = dma["dma0"]

            def tt(o, a, b, op):
                dve_chain(nc.vector.tensor_tensor(o, a, b, op))

            def ts(o, a, s1, s2, op0, op1=None):
                dve_chain(nc.vector.tensor_scalar(o, a, s1, s2, op0, op1) if op1 is not None
                          else nc.vector.tensor_scalar(o, a, s1, s2, op0))

            def cmul(dr, di, ar, ai, br, bi, t, conj=False):
                nc.vector.tensor_tensor(t[0], ar, br, ALU.mult)
                nc.vector.tensor_tensor(t[1], ai, bi, ALU.mult)
                nc.vector.tensor_tensor(t[2], ar, bi, ALU.mult)
                dve_chain(nc.vector.tensor_tensor(t[3], ai, br, ALU.mult))
                nc.vector.tensor_tensor(dr, t[0], t[1], ALU.add if conj else ALU.subtract)
                if conj:
                    dve_chain(nc.vector.tensor_tensor(di, t[3], t[2], ALU.subtract))
                else:
                    dve_chain(nc.vector.tensor_tensor(di, t[3], t[2], ALU.add))

            def bc_g(a, n):
                return a.unsqueeze(2).to_broadcast([P, a.shape[1], n])

            def dve_pre(v):
                v.wait_ge(pc_in.sem, pc_in.at(1))
                tt(S["zr"], pcol("lre"), S["step"], ALU.mult)
                tt(S["zi"], pcol("lim"), S["step"], ALU.mult)
                ts(S["kk"], S["zi"], 1.0 / (2 * math.pi), MAGIC, ALU.mult, ALU.add)
                ts(S["kk"], S["kk"], -MAGIC, None, ALU.add)
                dve_chain(nc.vector.scalar_tensor_tensor(S["r"], S["kk"], -TWO_PI_HI, S["zi"], ALU.mult, ALU.add))
                dve_chain(nc.vector.scalar_tensor_tensor(S["r"], S["kk"], -TWO_PI_LO, S["r"], ALU.mult, ALU.add))
                nc.vector.tensor_scalar(S["r"], S["r"], 3.1415925, -3.1415925, ALU.min, ALU.max).then_inc(pc_out.sem, 1)

            def act_pre(a):
                nc.scalar.activation(S["step"], pcol("lstep"), ACT.Exp).then_inc(pc_in.sem, 1)
                a.wait_ge(pc_out.sem, pc_out.at(1))
                nc.scalar.activation(S["mag"], S["zr"], ACT.Exp)
                nc.scalar.activation(S["r8"], S["zr"], ACT.Exp, scale=float(SC))
                nc.scalar.activation(S["sin"], S["r"], ACT.Sin)
                nc.scalar.activation(S["sinh"], S["r"], ACT.Sin, scale=0.5).then_inc(pc_in.sem, 1)

            def dve_post(v):
                v.wait_ge(pc_in.sem, pc_in.at(2))
                tmp = [S[f"t{i}"] for i in range(4)]
                tt(S["t0"], S["sinh"], S["sinh"], ALU.mult)
                ts(S["cos"], S["t0"], -2.0, 1.0, ALU.mult, ALU.add)
                tt(S["lbr"], S["mag"], S["cos"], ALU.mult)
                tt(S["lbi"], S["mag"], S["sin"], ALU.mult)
                ts(S["nr"], S["lbr"], -1.0, None, ALU.add)
                tt(S["t0"], pcol("lre"), pcol("lre"), ALU.mult)
                tt(S["t1"], pcol("lim"), pcol("lim"), ALU.mult)
                tt(S["den"], S["t0"], S["t1"], ALU.add)
                dve_chain(nc.vector.reciprocal(S["den"], S["den"]))
                cmul(S["cr"], S["ci"], S["nr"], S["lbi"], pcol("lre"), pcol("lim"), tmp, conj=True)
                tt(S["cr"], S["cr"], S["den"], ALU.mult)
                tt(S["ci"], S["ci"], S["den"], ALU.mult)
                v.wait_ge(ld.sem, ld.at(48))
                t3 = [sq[:, i // 2, (i % 2) * 384:(i % 2) * 384 + 256].rearrange("p (g c) -> p g c", c=GC) for i in range(4)]
                for h in range(2):
                    gs = slice(16 * h, 16 * h + 16)
                    cmul(bbar[:, 0, gs, :], bbar[:, 1, gs, :], bin_[:, 0, gs, :], bin_[:, 1, gs, :],
                         bc_g(S["cr"][:, gs], GC), bc_g(S["ci"][:, gs], GC), t3)
                nc.vector.memset(pw[:, 0, 0, :], 1.0)
                nc.vector.memset(pw[:, 1, 0, :], 0.0)
                nc.vector.tensor_copy(pw[:, 0, 1, :], S["lbr"])
                dve_chain(nc.vector.tensor_copy(pw[:, 1, 1, :], S["lbi"]))
                t4 = [sq[:, i // 2, (i % 2) * 384:(i % 2) * 384 + 4 * G].rearrange("p (n g) -> p n g", g=G) for i in range(4)]
                for n in (1, 2, 4):
                    by = [pw[:, i, n:n + 1, :].to_broadcast([P, n, G]) for i in range(2)]
                    cmul(pw[:, 0, n + 1:2 * n + 1, :], pw[:, 1, n + 1:2 * n + 1, :], pw[:, 0, 1:n + 1, :], pw[:, 1, 1:n + 1, :],
                         by[0], by[1], [q[:, 0:n, :] for q in t4])
                for i in range(2):
                    nc.vector.memset(qf[0:NS, i, SC + 1, :], 0.0)
                    nc.vector.memset(qf[NS:P, i, 0, :], 0.0)
                    nc.vector.tensor_copy(qf[0:NS, i, 0:SC + 1, :], pw[0:NS, i, :, :])
                    for pos in range(1, POS):
                        nc.vector.tensor_copy(qf[NS:P, i, pos, :], pw[NS:P, i, SC + 1 - pos, :])
                    nc.vector.tensor_copy(qr[NS:P, i, :, :], pw[NS:P, i, 0:SC, :])
                    for s in range(SC):
                        nc.vector.tensor_copy(qr[0:NS, i, s, :], pw[0:NS, i, SC - 1 - s, :])
                cmul(S["p2r"], S["p2i"], S["cos"], S["sin"], S["cos"], S["sin"], tmp)
                cmul(S["p4r"], S["p4i"], S["p2r"], S["p2i"], S["p2r"], S["p2i"], tmp)
                cmul(S["p2r"], S["p2i"], S["p4r"], S["p4i"], S["p4r"], S["p4i"], tmp)
                dve_chain(nc.vector.tensor_scalar(S["p2i"][NS:P], S["p2i"][NS:P], -1.0, None, ALU.mult))

            with nc.Block() as block:
                @block.sync
                def _(sp):
                    sp.dma_start(bin_[:, :, :, :], bc_in[0:2].rearrange("i p (g c) -> p i g c", c=GC)).then_inc(ld.sem, 16)
                    sp.dma_start(cc[:, :, :, :], bc_in[2:4].rearrange("i p (g c) -> p i g c", c=GC)).then_inc(ld.sem, 16)
                    sp.dma_start(wglr[:, :, :], wglr_in).then_inc(ld.sem, 16)

            def evac(a, g, i):
                if g == 0 and i < 4:
                    free(nc.scalar.activation(b1[:, i, :].rearrange("p (s j) -> p s j", s=SC),
                                              banks(2 * (i % 2)).rearrange("p (j s) -> p s j", s=SC), ACT.Copy))
                elif g == 0:
                    free(nc.scalar.activation(b1[:, i, :], banks(2 * (i % 2)), ACT.Copy, scale=float(DK ** -0.5) if i < 6 else 1.0))
                elif i < 4:
                    s, half = i // 2, i % 2
                    free(nc.scalar.activation(vt[:, 3 * half:3 * half + 3, s * UC:(s + 1) * UC],
                                              banks(2 * half).rearrange("p (j n) -> p j n", j=3), ACT.Copy))
                else:
                    free(nc.scalar.activation(b2[:, i, :], banks(2 * (i % 2)), ACT.Copy))
            def low_rank(pe, sp_):
                for k in range(KT):
                    for j, part in enumerate((sp_.in_h, sp_.in_l)):
                        st, en = k == 0 and j == 0, k == KT - 1 and j == 1
                        nc.tensor.matmul(ps[0:32, 4, :], wglr[:, k, :], part[:, k, 0:512].bitcast(F32), start=st, stop=en)
                        last = nc.tensor.matmul(ps[0:32, 5, 0:TS], wglr[:, k, :], part[:, k, 512:T].bitcast(F32), start=st, stop=en)
                last.then_inc(pc_in.sem, 1)
            vt = b2[:, 0:4, :].rearrange("p k t -> p (k t)").rearrange("p (j n) -> p j n", n=GH * DV)
            product_stage(x, ["ffff", "ttff"], evac, norm="mix0", evac_engine="scalar", dve_pre=dve_pre,
                          act_pre=act_pre, dve_post=dve_post, pe_post=low_rank)
            ld.base += 48
            pc_in.base += 3
            pc_out.base += 1
            prep.close()
            act = sb("s5act", [P, KT, T], on=local)
            rot = [sb(n, [P, G, NCH], on=s5mem) for n in ("rot_re", "rot_im")]
            dd = sb("dd", [GC, G, GC], on=s5mem)
            chunkmask = sb("chunkmask", [P, NCH], on=s5mem)

            ud, yd = dma["dma1"], dma["dma2"]
            with nc.Block() as block:
                @block.sync
                def _(sp):
                    sp.dma_start(u_dram.rearrange("(k p) s j -> p k (s j)", p=P), b1[:, 0:4, :]).then_inc(ud.sem, 16)
                    lo = TAB["chunkmask"][0]
                    sp.dma_start(chunkmask[:, :], tab_in[:, lo:lo + NCH]).then_inc(ld.sem, 16)
                    sp.wait_ge(ud.sem, ud.at(16))
                    sp.wait_ge(ld.sem, ld.at(16))

                @block.scalar
                def _(a):
                    nc.scalar.activation(lr[:, :], banks(4)[0:32], ACT.Copy)

                @block.vector
                def _(v):
                    dve_chain.start(v)
                    tmp = [S[f"t{i}"] for i in range(4)]
                    nc.vector.memset(rot[0][:, :, 0:1], 1.0)
                    dve_chain(nc.vector.memset(rot[1][:, :, 0:1], 0.0))
                    n, pr, pi, nr_, ni_ = 1, S["p2r"], S["p2i"], S["p4r"], S["p4i"]
                    while n < NCH:
                        m = min(n, NCH - n)
                        for g0 in range(0, G, 8 if m > 16 else 16):
                            w_ = 8 if m > 16 else 16
                            gs = slice(g0, g0 + w_)
                            tw = [sq[:, i // 2, (i % 2) * 384:(i % 2) * 384 + w_ * min(m, 32)].rearrange("p (g j) -> p g j", g=w_)
                                  for i in range(4)]
                            for m0 in range(0, m, 32):
                                mm = min(32, m - m0)
                                cmul(rot[0][:, gs, n + m0:n + m0 + mm], rot[1][:, gs, n + m0:n + m0 + mm],
                                     rot[0][:, gs, m0:m0 + mm], rot[1][:, gs, m0:m0 + mm],
                                     bc_g(pr[:, gs], mm), bc_g(pi[:, gs], mm), [q[:, :, 0:mm] for q in tw])
                        cmul(nr_, ni_, pr, pi, pr, pi, tmp)
                        pr, pi, nr_, ni_ = nr_, ni_, pr, pi
                        n *= 2
                    nc.vector.tensor_tensor(dd[:, :, :], pcol("s5d")[0:GC].unsqueeze(2).to_broadcast([GC, G, GC]),
                                            ident[0:GC, 0:GC].unsqueeze(1).to_broadcast([GC, G, GC]), ALU.mult)


                    dve_chain.close()
            ud.base += 16
            ld.base += 16

            s5 = ExitStack()
            u2 = act[:, 0, :].rearrange("p (g j) -> p g j", j=NCH)
            cl = sb("cl", [P, 2, GB, POS, GC], on=s5)
            vv = sb("vv", [P, 2, GB, P], on=s5)
            b1f = b1[:, 0:4, :].rearrange("p k t -> p (k t)")
            vT = b1f[:, 0:2 * GB * P].rearrange("p (i g c) -> p i g c", i=2, g=GB)
            mt = b1f[:, 2 * GB * P:3 * GB * P].rearrange("p (g c) -> p g c", g=GB)
            rt = act[0:GC, 2:5, :].rearrange("p k t -> p (k t)")[:, 0:GB * LAG * GC]\
                .rearrange("p (g n c) -> p g n c", g=GB, n=LAG)
            dec = act[:, 1, :]
            bp = [act[:, 2 + i, :] for i in range(2)]
            sp_ = [act[:, 4 + i, :] for i in range(2)]
            so = [act[:, 6 + i, :] for i in range(2)]
            tmpA = [rstd[:, :]] + [vv[:, 0, :, :].rearrange("p g c -> p (g c)")[:, 0:T],
                                   vv[:, 1, :, :].rearrange("p g c -> p (g c)")[:, 0:T], sq[:, 0, :]]
            ysb, yg = sq[:, 1, :], rstd[:, :]
            (t_v, vt_done, vt_ready, lag_done, rt_ready, m_loaded, bu_done, bu_read, st_ready, y_done, y_ready, y_e, y_e2,
             yg_ready) = (ev[f"ev{i}"] for i in range(14))

            def g3(a):
                return a.rearrange("p (g j) -> p g j", j=NCH)

            for b in range(NB):
                gs = slice(GB * b, GB * b + GB)
                with nc.Block() as block:
                    @block.sync
                    def _(sp):
                        src = u_dram[P * b:P * b + P].rearrange("(g c) s j -> s c g j", c=GC)
                        for s in range(SC):
                            sp.dma_start(u2[GC * s:GC * s + GC], src[s]).then_inc(ld.sem, 16)
                        sp.wait_ge(rt_ready.sem, rt_ready.at(1))
                        for s in range(SC):
                            sp.dma_start(mt[GC * s:GC * s + GC, :, :],
                                         rt[:, :, SC - 1 - s:2 * SC - 1 - s, :].rearrange("c g t d -> c g (t d)"))\
                                .then_inc(m_loaded.sem, 16)
                        sp.wait_ge(yg_ready.sem, yg_ready.at(1))
                        dst = y_dram[P * b:P * b + P].rearrange("(g c) t j -> t c g j", c=GC)
                        for s in range(SC):
                            sp.dma_start(dst[s], g3(yg)[GC * s:GC * s + GC]).then_inc(yd.sem, 16)
                        sp.wait_ge(yd.sem, yd.at(16 * SC))

                    @block.vector
                    def _(v):
                        dve_chain.start(v)
                        clf = [cl[:, i, :, :, :] for i in range(2)]
                        tc = [vT[:, 0, :, :].rearrange("p g c -> p (g c)"), vT[:, 1, :, :].rearrange("p g c -> p (g c)")]

                        def cb(i, h):
                            return cc[:, i, GB * b + 4 * h:GB * b + 4 * h + 4, :].unsqueeze(2).to_broadcast([P, 4, POS, GC])

                        def qb(i, h):
                            return qf[:, i, :, GB * b + 4 * h:GB * b + 4 * h + 4].rearrange("p n g -> p g n").unsqueeze(3)\
                                .to_broadcast([P, 4, POS, GC])
                        for h in range(2):
                            ta = [t_[:, 0:4 * POS * GC].rearrange("p (g n c) -> p g n c", g=4, n=POS) for t_ in tc]
                            o = [c_[:, 4 * h:4 * h + 4] for c_ in clf]
                            nc.vector.tensor_tensor(ta[0], cb(0, h), qb(0, h), ALU.mult)
                            dve_chain(nc.vector.tensor_tensor(ta[1], cb(1, h), qb(1, h), ALU.mult))
                            dve_chain(nc.vector.tensor_tensor(o[0], ta[0], ta[1], ALU.subtract))
                            nc.vector.tensor_tensor(ta[0], cb(0, h), qb(1, h), ALU.mult)
                            dve_chain(nc.vector.tensor_tensor(ta[1], cb(1, h), qb(0, h), ALU.mult))
                            dve_chain(nc.vector.scalar_tensor_tensor(
                                o[1].rearrange("p g n c -> p (g n c)"), ta[0].rearrange("p g n c -> p (g n c)"), -1.0,
                                ta[1].rearrange("p g n c -> p (g n c)"), ALU.mult, ALU.subtract))
                        for h in range(2):
                            hs = slice(GB * b + 4 * h, GB * b + 4 * h + 4)
                            bb = [bbar[:, i, hs, :].unsqueeze(2).to_broadcast([P, 4, SC, GC]) for i in range(2)]
                            qq = [qr[:, i, :, hs].rearrange("p n g -> p g n").unsqueeze(3).to_broadcast([P, 4, SC, GC])
                                  for i in range(2)]
                            ta = [t_[:, 0:4 * P].rearrange("p (g n c) -> p g n c", g=4, n=SC) for t_ in tc]
                            o = [vv[:, i, 4 * h:4 * h + 4, :].rearrange("p g (n c) -> p g n c", n=SC) for i in range(2)]
                            for i, (q0, q1, op) in enumerate(((0, 1, ALU.subtract), (1, 0, ALU.add))):
                                nc.vector.tensor_tensor(ta[0], bb[0], qq[q0], ALU.mult)
                                dve_chain(nc.vector.tensor_tensor(ta[1], bb[1], qq[q1], ALU.mult))
                                dve_chain(nc.vector.tensor_tensor(o[i], ta[0], ta[1], op))
                        dve_chain(nc.vector.tensor_tensor(g3(dec), bc_g(S["r8"][:, gs], NCH),
                                                          chunkmask[:, :].unsqueeze(1).to_broadcast([P, GB, NCH]), ALU.mult))
                        nc.vector.memset(so[0], 0.0)
                        nc.vector.memset(so[1], 0.0).then_inc(t_v.sem, 1)
                        v.wait_ge(lag_done.sem, lag_done.at(1))
                        lagf = banks(4, 1024)[0:GC].rearrange("c (g n d) -> c g n d", g=GB, n=SC)
                        lagb = banks(6, 1024)[0:GC].rearrange("c (g n d) -> c g n d", g=GB, n=SC)
                        dve_chain(nc.vector.tensor_copy(rt[:, :, 0:SC, :], lagb))
                        nc.vector.tensor_copy(rt[:, :, SC:LAG, :], lagf[:, :, 1:SC, :])
                        dve_chain(nc.vector.tensor_tensor(rt[:, :, SC - 1, :], rt[:, :, SC - 1, :], lagf[:, :, 0, :], ALU.add))
                        nc.vector.tensor_tensor(rt[:, :, SC - 1, :], rt[:, :, SC - 1, :], dd[:, gs, :], ALU.add).then_inc(rt_ready.sem, 1)
                        v.wait_ge(bu_done.sem, bu_done.at(1))
                        bur = banks(0, 1024).rearrange("p (g j) -> p g j", j=P)[:, :, 0:NCH]
                        bui = banks(2, 1024).rearrange("p (g j) -> p g j", j=P)[:, :, 0:NCH]
                        er, ei = rot[0][:, gs, :], rot[1][:, gs, :]
                        v.wait_ge(m_loaded.sem, m_loaded.at(16 * SC))
                        cmul(g3(bp[0]), g3(bp[1]), bur, bui, er, ei, [g3(t_) for t_ in tmpA], conj=True)
                        for i in range(2):
                            nc.vector.tensor_tensor_scan(out=sp_[i][0:NS], data0=dec[0:NS], data1=bp[i][0:NS], initial=0.0,
                                                         op0=ALU.mult, op1=ALU.add)
                            ins = nc.vector.tensor_tensor_scan(out=sp_[i][NS:P, ::-1], data0=dec[NS:P, ::-1],
                                                               data1=bp[i][NS:P, ::-1], initial=0.0, op0=ALU.mult, op1=ALU.add)
                        dve_chain(ins)
                        nc.vector.tensor_tensor(g3(tmpA[0]), g3(sp_[0]), er, ALU.mult)
                        nc.vector.tensor_tensor(g3(tmpA[1]), g3(sp_[1]), ei, ALU.mult)
                        nc.vector.tensor_tensor(g3(tmpA[2]), g3(sp_[0]), ei, ALU.mult)
                        dve_chain(nc.vector.tensor_tensor(g3(tmpA[3]), g3(sp_[1]), er, ALU.mult))
                        for i, op in ((0, ALU.subtract), (1, ALU.add)):
                            o, a_, b_ = g3(so[i]), g3(tmpA[2 * i]), g3(tmpA[2 * i + 1])
                            nc.vector.tensor_tensor(o[0:NS, :, 1:NCH], a_[0:NS, :, 0:NCH - 1], b_[0:NS, :, 0:NCH - 1], op)
                            dve_chain(nc.vector.tensor_tensor(o[NS:P, :, 0:NCH - 1], a_[NS:P, :, 1:NCH], b_[NS:P, :, 1:NCH], op))
                            nc.vector.memset(o[0:NS, :, TP // SC:TP // SC + 1], 0.0)
                            last = nc.vector.memset(o[NS:P, :, TP // SC - 1:TP // SC], 0.0)
                        last.then_inc(st_ready.sem, 1)
                        v.wait_ge(y_ready.sem, y_ready.at(1))
                        t_ = tmpA[1]
                        tt(t_, ysb, ysb, ALU.mult)
                        ts(t_, t_, 0.044715, 1.0, ALU.mult, ALU.add)
                        nc.vector.tensor_tensor(t_, t_, ysb, ALU.mult).then_inc(y_e.sem, 1)
                        v.wait_ge(y_e2.sem, y_e2.at(1))
                        ts(t_, t_, 0.5, 0.5, ALU.mult, ALU.add)
                        nc.vector.tensor_tensor(yg, t_, ysb, ALU.mult).then_inc(yg_ready.sem, 1)
                        dve_chain.close()

                    @block.tensor
                    def _(pe):
                        pe.wait_ge(t_v.sem, t_v.at(1))
                        for i in range(2):
                            for g in range(GB):
                                last = nc.tensor.transpose(banks(2 * i, 1024)[:, g * P:(g + 1) * P], vv[:, i, g, :], ident)
                        last.then_inc(vt_done.sem, 1)
                        for g in range(GB):
                            for z in range(2):
                                rows = slice(NS * z, NS * z + NS)
                                lo = 0 if z == 0 else 2
                                for i in range(2):
                                    last = nc.tensor.matmul(banks(4 + 2 * z, 1024)[0:GC, g * P:(g + 1) * P],
                                                            bbar[rows, i, GB * b + g, :],
                                                            cl[rows, i, g, lo:lo + SC, :].rearrange("p n c -> p (n c)"),
                                                            start=(i == 0), stop=(i == 1))
                        last.then_inc(lag_done.sem, 1)
                        pe.wait_ge(vt_ready.sem, vt_ready.at(1))
                        pe.wait_ge(ld.sem, ld.at(16 * SC))
                        for i in range(2):
                            for g in range(GB):
                                last = nc.tensor.matmul(banks(2 * i, 1024)[:, g * P:g * P + NCH], vT[:, i, g, :], u2[:, g, :],
                                                        start=True, stop=True)
                        last.then_inc(bu_done.sem, 1)
                        pe.wait_ge(m_loaded.sem, m_loaded.at(16 * SC))
                        pe.wait_ge(st_ready.sem, st_ready.at(1))
                        for g in range(GB):
                            o = banks(4, 1024)[:, g * P:g * P + NCH]
                            nc.tensor.matmul(o, mt[:, g, :], u2[:, g, :], start=True, stop=False)
                            for i in range(2):
                                last = nc.tensor.matmul(o, cl[:, i, g, 1:SC + 1, :].rearrange("p n c -> p (n c)"),
                                                        g3(so[i])[:, g, :], start=False, stop=(i == 1))
                        last.then_inc(y_done.sem, 1)

                    @block.scalar
                    def _(a):
                        a.wait_ge(vt_done.sem, vt_done.at(1))
                        a.wait_ge(lag_done.sem, lag_done.at(1))
                        for i in range(2):
                            last = nc.scalar.activation(vT[:, i, :, :].rearrange("p g c -> p (g c)"), banks(2 * i, 1024), ACT.Copy)
                        last.then_inc(vt_ready.sem, 1)
                        a.wait_ge(y_done.sem, y_done.at(1))
                        nc.scalar.activation(g3(ysb), banks(4, 1024).rearrange("p (g j) -> p g j", j=P)[:, :, 0:NCH], ACT.Copy)\
                            .then_inc(y_ready.sem, 1)
                        a.wait_ge(y_e.sem, y_e.at(1))
                        nc.scalar.activation(tmpA[1], tmpA[1], ACT.Tanh, scale=math.sqrt(2.0 / math.pi)).then_inc(y_e2.sem, 1)
                for s_ in (t_v, vt_done, vt_ready, lag_done, rt_ready, bu_done, st_ready, y_done, y_ready, y_e, y_e2, yg_ready):
                    s_.base += 1
                ld.base += 16 * SC
                m_loaded.base += 16 * SC
                yd.base += 16 * SC
            s5.close()

            glu = ExitStack()
            wglu = sb("wglu_sb", [P, 4, 512], on=glu)
            et = sb("glu_t", [P, 2, T], on=glu)
            with nc.Block() as block:
                @block.sync
                def _(sp):
                    sp.dma_start(b1[:, 0:4, :], y_dram.rearrange("(k p) s j -> p k (s j)", p=P)).then_inc(ld.sem, 16)
                    sp.dma_start(wglu[:, :, :], wglu_in).then_inc(ld.sem, 16)

                @block.tensor
                def _(pe):
                    pe.wait_ge(ld.sem, ld.at(32))
                    for o in range(4):
                        if o >= 2:
                            pe.wait_ge(vt_ready.sem, vt_ready.at(o - 1))
                        for k in range(4):
                            nc.tensor.matmul(ps[:, 2 * (o % 2), :], wglu[:, k, o * P:(o + 1) * P], b1[:, k, 0:512],
                                             start=(k == 0), stop=(k == 3))
                            last = nc.tensor.matmul(ps[:, 2 * (o % 2) + 1, 0:TS], wglu[:, k, o * P:(o + 1) * P], b1[:, k, 512:T],
                                                    start=(k == 0), stop=(k == 3))
                        last.then_inc(vt_done.sem, 1)

                @block.scalar
                def _(a):
                    for o in range(4):
                        a.wait_ge(vt_done.sem, vt_done.at(o + 1))
                        if o >= 2:
                            a.wait_ge(st_ready.sem, st_ready.at(o - 1))
                        nc.scalar.activation(et[:, o % 2, :], banks(2 * (o % 2)), ACT.Tanh, scale=0.5).then_inc(vt_ready.sem, 1)

                @block.vector
                def _(v):
                    dve_chain.start(v)
                    for o in range(4):
                        v.wait_ge(vt_ready.sem, vt_ready.at(o + 1))
                        e_ = et[:, o % 2, :]
                        ts(e_, e_, 0.5, 0.5, ALU.mult, ALU.add)
                        nc.vector.tensor_tensor(act[:, o, :].rearrange("p (j s) -> p s j", s=SC),
                                                e_.rearrange("p (s j) -> p s j", s=SC),
                                                b1[:, o, :].rearrange("p (s j) -> p s j", s=SC), ALU.mult).then_inc(st_ready.sem, 1)
                    v.wait_ge(st_ready.sem, st_ready.at(4))
                    dve_chain.close()
            ld.base += 32
            for s_ in (vt_done, vt_ready, st_ready):
                s_.base += 4
            glu.close()
            s5mem.close()

            gl = ExitStack()
            b3 = sb("gl_b3", [P, KT, T], on=gl)
            masks = sb("masks", [P, 2 * P], on=gl)
            wg = sb("wg", [32, 2, 256], on=gl)
            gm = sb("gm", [P, 2, T], on=gl)
            gt = b1[:, 0:4, :]
            qrel = b3[:, 5:7, :]
            krel = sb("krel", [P, 2, T], on=gl)
            ko = b3[:, 7, :]
            koT = b3[:, 4, :].rearrange("p (j d) -> p j d", d=P)
            qout = sb("qout", [P, 2, T], on=gl)
            sprev = [b3[:, 2 * z:2 * z + 2, :].rearrange("p k t -> p (k t)").rearrange("p (c d) -> p c d", d=DV) for z in range(2)]
            scT = sb("scT", [P, 2, T], on=gl)
            decay = sb("decay", [P, NC12], on=gl)
            (z_done, z_read, e_in, e_out, l_out, d_in, d_out, ko_ready, kt_done, kt_ready, kv_done, s_ready, sc_done, sc_ready,
             oo_done, oo_read) = (ev[f"ev{i}"] for i in range(16))

            def kv_ps(c):
                b = 4 + 2 * (c % 2) + c // 2 // 4
                return ps[:, b, (c // 2 % 4) * DV:(c // 2 % 4) * DV + DV]

            def c3(a):
                return a.rearrange("p (c i) -> p c i", i=CH)
            with nc.Block() as block:
                @block.sync
                def _(sp):
                    sp.dma_start(wg[:, :, :], wgate_in).then_inc(ld.sem, 16)
                    lo = TAB["masks"][0]
                    sp.dma_start(masks[:, :], tab_in[:, lo:lo + 2 * P]).then_inc(ld.sem, 16)
                    sp.wait_ge(ld.sem, ld.at(32))

                @block.scalar
                def _(a):
                    nc.scalar.preload_act_table_set("natural_log_exp_and_others")

                @block.gpsimd
                def _(g):
                    nc.gpsimd.memset(gm[:, :, :], 1.0).then_inc(pchain.sem, 1)
                    g.wait_ge(pchain.sem, pchain.at(1))
                    nc.gpsimd.memset(c3(gm[:, 0, :])[:, :, 0:1], 0.0)
                    nc.gpsimd.memset(c3(gm[:, 1, :])[:, :, CH - 1:CH], 0.0)
                    for z in range(2):
                        nc.gpsimd.memset(sprev[z][:, 0 if z == 0 else TP // CH - 1, :], 0.0)
                        nc.gpsimd.memset(sprev[z][:, TP // CH if z == 0 else NC12 - 1, :], 0.0)
                    nc.gpsimd.memset(scT[:, :, :], 0.0).then_inc(pchain.sem, 1)
                    g.wait_ge(pchain.sem, pchain.at(2))
            pchain.base += 2
            ld.base += 32
            for t in range(2):
                for z in range(2):
                    with nc.Block() as block:
                        @block.tensor
                        def _(pe):
                            nc.tensor.matmul(ps[:, 0, :], wg[:, z, t * P:(t + 1) * P], lr[:, 0:512], start=True, stop=True)
                            nc.tensor.matmul(ps[:, 1, 0:TS], wg[:, z, t * P:(t + 1) * P], lr[:, 512:T], start=True, stop=True)\
                                .then_inc(z_done.sem, 1)
                            pe.wait_ge(ko_ready.sem, ko_ready.at(1))
                            for j in range(TT):
                                last = nc.tensor.transpose(banks(2)[:, j * P:(j + 1) * P], ko[:, j * P:(j + 1) * P], ident)
                            last.then_inc(kt_done.sem, 1)
                            pe.wait_ge(kt_ready.sem, kt_ready.at(1))
                            for c in range(NC12):
                                rows = slice(CH * (c % 2), CH * (c % 2) + CH)
                                for hh in range(2):
                                    h = 2 * t + hh
                                    last = nc.tensor.matmul(kv_ps(c)[DK * hh:DK * hh + DK],
                                                            koT[rows, c // 2, DK * hh:DK * hh + DK],
                                                            vt[rows, c // 2, h * DV:(h + 1) * DV], start=True, stop=True)
                            last.then_inc(kv_done.sem, 1)

                        @block.vector
                        def _(v):
                            dve_chain.start(v)
                            g_, cum, ta, tb = (gt[:, i, :] for i in range(4))
                            v.wait_ge(z_done.sem, z_done.at(1))
                            col = COLS["bgate"][0] + 2 * z + t
                            dve_chain(nc.vector.tensor_scalar(g_, banks(0), par[:, col:col + 1], None, ALU.add))
                            ts(ta, g_, -1.0, None, ALU.mult)
                            nc.vector.tensor_tensor(ta, ta, g_, ALU.min).then_inc(e_in.sem, 1)
                            v.wait_ge(e_out.sem, e_out.at(1))
                            dve_chain(nc.vector.scalar_tensor_tensor(g_, g_, 0.0, ta, ALU.min, ALU.subtract))
                            if z == 0:
                                dve_chain(nc.vector.tensor_tensor_scan(out=cum, data0=gm[:, 0, :], data1=g_, initial=0.0,
                                                                       op0=ALU.mult, op1=ALU.add))
                            else:
                                dve_chain(nc.vector.tensor_tensor_scan(out=cum[:, ::-1], data0=gm[:, 1, ::-1], data1=g_[:, ::-1],
                                                                       initial=0.0, op0=ALU.mult, op1=ALU.add))
                            ref = CH // 2 - 1 if z == 0 else CH // 2
                            end = CH - 1 if z == 0 else 0
                            refs = c3(cum)[:, :, ref:ref + 1].to_broadcast([P, NC12, CH])
                            ends = c3(cum)[:, :, end:end + 1].to_broadcast([P, NC12, CH])
                            nc.vector.tensor_tensor(c3(ta), c3(cum), refs, ALU.subtract)
                            nc.vector.tensor_tensor(c3(tb), ends, c3(cum), ALU.subtract).then_inc(d_in.sem, 1)
                            v.wait_ge(d_out.sem, d_out.at(1))
                            nc.vector.tensor_tensor(ko[:, :], b1[:, 6 + t, :], tb, ALU.mult).then_inc(ko_ready.sem, 1)
                            nc.vector.tensor_tensor(qout[:, z, :], b1[:, 4 + t, :], cum, ALU.mult)
                            nc.vector.tensor_tensor(qrel[:, z, :], b1[:, 4 + t, :], ta, ALU.mult)
                            nc.vector.tensor_tensor(krel[:, z, :], b1[:, 6 + t, :], g_, ALU.mult)
                            v.wait_ge(kv_done.sem, kv_done.at(1))
                            order = [(0, 8), (8, 12)]
                            for lo, hi in order:
                                cs = list(range(lo, hi)) if z == 0 else list(range(hi - 1, lo - 1, -1))
                                for c, nx in zip(cs[:-1], cs[1:]):
                                    dve_chain(nc.vector.scalar_tensor_tensor(
                                        sprev[z][:, nx, :], sprev[z][:, c, :], decay[:, c:c + 1],
                                        kv_ps(c), ALU.mult, ALU.add))
                            dve_chain.close()

                        @block.scalar
                        def _(a):
                            g_, cum, ta, tb = (gt[:, i, :] for i in range(4))
                            a.wait_ge(e_in.sem, e_in.at(1))
                            nc.scalar.activation(ta, ta, ACT.Exp).then_inc(achain.sem, 1)
                            a.wait_ge(achain.sem, achain.at(1))
                            nc.scalar.activation(ta, ta, ACT.Ln, bias=pcol("one")).then_inc(e_out.sem, 1)
                            a.wait_ge(d_in.sem, d_in.at(1))
                            cumends = c3(cum)[:, :, CH - 1 if z == 0 else 0]
                            nc.scalar.activation(decay[:, :], cumends, ACT.Exp, scale=1.0 / 16)
                            nc.scalar.activation(g_, ta, ACT.Exp, scale=-1.0 / 16).then_inc(achain.sem, 1)
                            a.wait_ge(achain.sem, achain.at(2))
                            nc.scalar.activation(ta, ta, ACT.Exp, scale=1.0 / 16)
                            nc.scalar.activation(tb, tb, ACT.Exp, scale=1.0 / 16)
                            nc.scalar.activation(cum, cum, ACT.Exp, scale=1.0 / 16).then_inc(d_out.sem, 1)
                            a.wait_ge(kt_done.sem, kt_done.at(1))
                            nc.scalar.activation(koT.rearrange("p j d -> p (j d)"), banks(2), ACT.Copy).then_inc(kt_ready.sem, 1)
                    for s_ in (z_done, e_in, e_out, d_in, d_out, ko_ready, kt_done, kt_ready, kv_done):
                        s_.base += 1
                    achain.base += 2
                with nc.Block() as block:
                    @block.tensor
                    def _(pe):
                        for hh in range(2):
                            h = 2 * t + hh
                            rows = slice(DK * hh, DK * hh + DK)
                            if hh == 1:
                                pe.wait_ge(sc_ready.sem, sc_ready.at(1))
                            for z in range(2):
                                for j in range(TT):
                                    js = slice(j * P, (j + 1) * P)
                                    last = nc.tensor.matmul(banks(2 * z)[:, js], krel[rows, z, js], qrel[rows, z, js],
                                                            start=True, stop=True)
                            last.then_inc(sc_done.sem, 1)
                            pe.wait_ge(sc_ready.sem, sc_ready.at(hh + 1))
                            ob = banks(4 + 2 * hh)
                            for j in range(TT):
                                js = slice(j * P, (j + 1) * P)
                                for z in range(2):
                                    nc.tensor.matmul(ob[:, js], vt[:, j, h * DV:(h + 1) * DV], scT[:, z, js],
                                                     start=(z == 0), stop=False, skip_group_check=True)
                                for z in range(2):
                                    for c in (2 * j, 2 * j + 1):
                                        cs = slice(CH * c, CH * c + CH)
                                        last = nc.tensor.matmul(ob[:, cs], sprev[z][rows, c, :], qout[rows, z, cs],
                                                                start=False, stop=(z == 1), skip_group_check=True)
                            last.then_inc(oo_done.sem, 1)

                    @block.vector
                    def _(v):
                        for hh in range(2):
                            v.wait_ge(sc_done.sem, sc_done.at(hh + 1))
                            if hh == 1:
                                v.wait_ge(oo_done.sem, oo_done.at(1))
                            for z in range(2):
                                mk = masks[:, P * z:P * z + P].bitcast(mybir.dt.uint32).unsqueeze(1).to_broadcast([P, TT, P])
                                last = nc.vector.copy_predicated(scT[:, z, :].rearrange("p (j i) -> p j i", i=P), mk,
                                                                 banks(2 * z).rearrange("p (j i) -> p j i", i=P))
                            last.then_inc(sc_ready.sem, 1)

                    @block.scalar
                    def _(a):
                        for hh in range(2):
                            a.wait_ge(oo_done.sem, oo_done.at(hh + 1))
                            nc.scalar.activation(act[:, 4 + 2 * t + hh, :], banks(4 + 2 * hh), ACT.Copy)
                for s_ in (sc_done, sc_ready, oo_done):
                    s_.base += 2
            with nc.Block() as block:
                @block.scalar
                def _(a):
                    for h in range(GH):
                        nc.scalar.activation(gt[:, h, :], b2[:, 4 + h, :], ACT.Tanh, scale=0.5).then_inc(e_in.sem, 1)

                @block.vector
                def _(v):
                    dve_chain.start(v)
                    for h in range(GH):
                        v.wait_ge(e_in.sem, e_in.at(h + 1))
                        ts(gt[:, h, :], gt[:, h, :], 0.5, 0.5, ALU.mult, ALU.add)
                        tt(b2[:, 4 + h, :], b2[:, 4 + h, :], gt[:, h, :], ALU.mult)
                    dve_chain.close()
            e_in.base += GH

            def gate(v, h):
                v.wait_ge(normed.sem, normed.at(h + 1))
                nc.vector.tensor_tensor(b1[:, 4 + h, :], b1[:, 4 + h, :], b2[:, 4 + h, :], ALU.mult)
            with nc.Block() as block:
                @block.scalar
                def _(a):
                    nc.scalar.preload_act_table_set("natural_log_exp_and_others")
                    for k in range(4):
                        nc.scalar.activation(b1[:, k, :], act[:, k, :], ACT.Copy)
            gl.close()
            head_norm_stage([([act[:, 4 + h, :]], [pcol("gnorm")], [b1[:, 4 + h, :]]) for h in range(GH)], ones, DV, extra=gate)
            local.close()
            product_stage(b1, ["ffff"], add_residual)
            outer.close()
        s5_gla()
        cross(0)
        mlp(0)
        diff_attention()
        cross(1)
        mlp(1)

        with nc.Block() as block:
            @block.sync
            def _(sp):
                sp.dma_start(out.rearrange("(k p) t -> p k t", p=P), x[:, :, :]).then_inc(dma["dma1"].sem, 16)
                sp.wait_ge(dma["dma1"].sem, dma["dma1"].at(16))


def kernel(**inputs):
    import numpy as _np
    import concourse.bacc as _bacc
    from concourse import mybir as _mybir
    from concourse.bass_utils import run_bass_kernel_spmd as _run

    w = {k: _np.asarray(v) for k, v in inputs.items()}

    def cols(v):
        return v.reshape(-1, P).T

    par = _np.zeros((P, NPAR), _np.float32)

    def put(name, v):
        a, n = COLS[name]
        par[:v.shape[0], a:a + n] = v

    for layer in range(DEPTH):
        for short, name in (("mix", "norm_mix"), ("cross", "norm_cross"), ("mem", "norm_mem"), ("mlp", "norm_mlp"),
                            ("xq", "x_q_norm"), ("xk", "x_k_norm")):
            put(f"{short}{layer}", cols(w[name][layer]))
    for name, src in (("dq", "diff_q_norm"), ("dk", "diff_k_norm")):
        put(name, _np.concatenate([w[src][0], w[src][0]])[:, None])
    put("dnorm", w["diff_norm"][0][:, None])
    put("gnorm", w["gla_norm"][0][:, None])
    put("lq", _np.stack([w["diff_lambda_q1"][0], w["diff_lambda_q2"][0]], 1))
    put("lk", _np.stack([w["diff_lambda_k1"][0], w["diff_lambda_k2"][0]], 1))
    put("bgate", w["gla_b_gate"][0].reshape(2, 2, P).transpose(2, 0, 1).reshape(P, 4))
    put("lre", w["s5_lambda_re"][0].transpose(0, 2, 1).reshape(P, G))
    put("lim", w["s5_lambda_im"][0].transpose(0, 2, 1).reshape(P, G))
    put("lstep", _np.repeat(w["s5_log_step"][0], NS, axis=0))
    put("s5d", w["s5_d"][0].T)
    put("eps", _np.full((P, 1), EPS, _np.float32))
    put("one", _np.ones((P, 1), _np.float32))
    mask = _np.ones((P, NCH), _np.float32)
    mask[:NS, [0, TP // SC]] = 0
    mask[NS:, [TP // SC - 1, NCH - 1]] = 0
    put("ident", _np.eye(P, dtype=_np.float32))
    put("ones", _np.ones((P, P), _np.float32))
    put("ones64", _np.kron(_np.eye(2, dtype=_np.float32), _np.ones((64, 64), _np.float32)))
    dist = (_np.abs(_np.arange(P)[:, None] + 384 - _np.arange(DIST)[None, :]).astype(_np.float32))

    b_ri = [w[n][0].transpose(0, 2, 1, 3).reshape(P, G * GC) for n in ("s5_b_re", "s5_b_im")]
    c_ri = [w[n][0].transpose(0, 3, 1, 2).reshape(P, G * GC) for n in ("s5_c_re", "s5_c_im")]
    bc = _np.stack(b_ri + c_ri)

    def units(a):
        n = a.shape[1] // UC
        return a.reshape(KT, P, n, UC).transpose(2, 1, 0, 3).reshape(n, P, KT * UC)

    ev = w["ev_w_in"][0]
    u_, q_, k_, v_, og_, glr_ = _np.split(ev, [512, 768, 1024, 1536, 2048], axis=1)
    parts = [units(_np.concatenate([u_, q_, k_], 1)), units(_np.concatenate([v_, og_], 1)), units(w["ev_w_out"][0])]

    def tail(layer):
        r = [units(w["x_w_kv"][layer]), units(w["x_w_q"][layer]), units(w["x_w_o"][layer])]
        for fb in range(FB):
            r.append(units(w["mlp_w1"][layer][:, fb * 1024:(fb + 1) * 1024]))
            r.append(units(w["mlp_w2"][layer][fb * 1024:(fb + 1) * 1024]))
        return r

    parts += tail(0) + [units(w["od_w_in"][0]), units(w["od_w_out"][0])] + tail(1)
    wgate = _np.zeros((2 * 16, 2, 256), _np.float32)
    for z in range(2):
        wgate[16 * z:16 * z + 16, z] = w["gla_w_gate"][0][z]
    j, i = _np.arange(P)[:, None], _np.arange(P)[None, :]
    same = j // CH == i // CH
    tri = _np.concatenate([same & (j <= i), same & (j >= i)], 1).astype(_np.float32)

    arrays = {
        "params": par,
        "x_in": _np.concatenate([w["x_prompt"][0], w["x_sample"][0]], 0).T,
        "mem_in": _np.concatenate([w["mem_prompt"][0], w["mem_sample"][0]], 0).T,
        "wstream": _np.concatenate(parts, 0),
        "wglr": glr_.reshape(KT, P, 32).transpose(1, 0, 2),
        "wglu": w["s5_w_glu"][0].reshape(4, P, 512).transpose(1, 0, 2),
        "wgate": wgate,
        "bc": bc,
        "tab": _np.concatenate([dist, tri, mask], 1),
    }
    arrays = {k: _np.ascontiguousarray(v) for k, v in arrays.items()}
    nc = _bacc.Bacc("TRN2", target_bir_lowering=False, num_devices=1)
    args = [nc.dram_tensor(k, a.shape, _mybir.dt.from_np(a.dtype), kind="ExternalInput").ap() for k, a in arrays.items()]
    scratch = [nc.dram_tensor(n, (512, SC, NCH), F32, kind="Internal").ap() for n in ("u_scratch", "y_scratch")]
    out = nc.dram_tensor("y_out", (D, T), F32, kind="ExternalOutput").ap()
    build(nc, *args, *scratch, out)
    r = _run(nc, [arrays], core_ids=[0])
    y = r.results[0]["y_out"].T
    return (y[None, :TP], y[None, TP:])
```

```python
import math
from contextlib import ExitStack

import numpy as np

import concourse.bass as bass
from concourse import mybir

F32 = mybir.dt.float32
F32R = mybir.dt.float32r
U8 = mybir.dt.uint8
ALU = mybir.AluOpType
ACT = mybir.ActivationFunctionType
AX = mybir.AxisListType

P = 128
D = 1024
KT = D // P
TP, TS = 512, 256
T = TP + TS
TT = T // P
M = 512
UC = 256
RAW = 2
SPL = 2
UPP = 4
DEPTH = 2
FB = 4
EPS = 1e-6
G, NS, GC = 32, 64, 16
SC = 8
NCH = T // SC
GB = 8
NB = G // GB
LAG = 2 * SC - 1
POS = SC + 2
GH, DK, DV, CH = 4, 64, 128, 64
NC12 = T // CH
DH = 8
XH = 4
LAMBDA_INIT = 0.8 - 0.6 * math.exp(-0.3)
DIST = 896
MAGIC = 12582912.0
TWO_PI_HI = 6.28125
TWO_PI_LO = 2 * math.pi - 6.28125


def _param_columns():
    widths = [("mix0", 8), ("mix1", 8), ("cross0", 8), ("cross1", 8), ("mem0", 8), ("mem1", 8), ("mlp0", 8),
              ("mlp1", 8), ("xq0", 2), ("xq1", 2), ("xk0", 2), ("xk1", 2), ("dq", 1), ("dk", 1), ("dnorm", 1),
              ("gnorm", 1), ("lq", 2), ("lk", 2), ("bgate", 4), ("lre", 32), ("lim", 32), ("lstep", 32), ("s5d", 32),
              ("eps", 1), ("one", 1), ("ident", 128), ("ones", 128), ("ones64", 128)]
    at, out = 0, {}
    for name, w in widths:
        out[name] = (at, w)
        at += w
    return out, at


COLS, NPAR = _param_columns()
TAB = {"dist": (0, DIST), "masks": (DIST, 256), "chunkmask": (DIST + 256, 96)}
NTAB = DIST + 256 + 96


class Signal:

    def __init__(self, ctx, nc, name):
        self.sem = ctx.enter_context(nc.semaphore(name))
        self.base = 0

    def at(self, n):
        return self.base + n


class Chain:

    def __init__(self, sig):
        self.sig = sig
        self.n = 0
        self.eng = None
        self.reg = None

    def start(self, eng):
        self.eng, self.n = eng, 0

    def loop(self, reg, per):
        self.reg, self.per, self.in_loop = reg, per, 0

    def end_loop(self, times):
        assert self.in_loop == self.per, (self.in_loop, self.per)
        self.n += self.per * times
        self.reg = None

    def __call__(self, ins):
        ins.then_inc(self.sig.sem, 1)
        if self.reg is None:
            self.n += 1
            self.eng.wait_ge(self.sig.sem, self.sig.base + self.n)
        else:
            self.in_loop += 1
            self.eng.wait_ge(self.sig.sem, self.reg * self.per + (self.sig.base + self.n + self.in_loop))

    def close(self):
        self.sig.base += self.n
        self.n = 0


def build(nc, params, x_in, mem_in, wstream, wglr_in, wglu_in, wgate_in, bc_in, tab_in, u_dram, y_dram, out):
    ctx = ExitStack()
    with ctx:
        def sb(name, shape, dt=F32, on=ctx):
            return on.enter_context(nc.sbuf_tensor(name, shape, dt))

        def sig(name):
            return Signal(ctx, nc, name)

        par = sb("par", [P, NPAR])
        x = sb("x", [P, KT, T])
        raw = sb("raw", [P, RAW, KT, UC])
        rstd = sb("rstd", [P, T])
        sq = sb("sq", [P, 2, T])
        gains = sb("gains", [P, 8])
        ps = ctx.enter_context(nc.psum_tensor("ps", [P, 8, 512], F32))

        def pcol(name, lo=0, n=None):
            a, w = COLS[name]
            return par[:, a + lo:a + lo + (w if n is None else n)]

        ident, ones, ones64 = pcol("ident"), pcol("ones"), pcol("ones64")

        def banks(b, n=T):
            return ps[:, b:b + 2, :].rearrange("p b n -> p (b n)")[:, 0:n]

        loaded = sig("loaded")
        w_loaded = [sig(f"w_loaded{s}") for s in range(RAW)]
        w_high = sig("w_high")
        w_ready = sig("w_ready")
        in_high = sig("in_high")
        in_made = sig("in_made")
        tile_done = sig("tile_done")
        tile_free = sig("tile_free")
        act_ready = sig("act_ready")
        sq_ready = sig("sq_ready")
        sq_used = sig("sq_used")
        root_ready = sig("root_ready")
        hn_square = sig("hn_square")
        hn_sum = sig("hn_sum")
        hn_root = sig("hn_root")
        hn_done = sig("hn_done")
        normed = sig("normed")
        hid_free = sig("hid_free")
        hid_made = sig("hid_made")
        hid_high = sig("hid_high")
        hid_ready = sig("hid_ready")
        dchain = sig("dchain")
        achain = sig("achain")
        pchain = sig("pchain")
        dve_chain, act_chain, pool_chain = Chain(dchain), Chain(achain), Chain(pchain)
        ev = {n: sig(n) for n in ("ev0", "ev1", "ev2", "ev3", "ev4", "ev5", "ev6", "ev7", "ev8", "ev9", "ev10",
                                  "ev11", "ev12", "ev13", "ev14", "ev15")}
        dma = {n: sig(n) for n in ("dma0", "dma1", "dma2", "dma3")}
        state = {"G": 0}

        NU = wstream.shape[0]
        serial = [0]

        class Split:

            def __init__(self, on, cols=T):
                serial[0] += 1
                n = serial[0]
                self.in_h = sb(f"in_h{n}", [P, KT, cols], F32R, on=on)
                self.in_l = sb(f"in_l{n}", [P, KT, cols], F32R, on=on)
                self.w_h = sb(f"w_h{n}", [P, SPL, KT, UC], F32R, on=on)
                self.w_l = sb(f"w_l{n}", [P, SPL, KT, UC], F32R, on=on)

        def sp_weights(sp, n):
            u0 = state["G"] * UPP

            def one(i, s):
                sp.wait_ge(w_ready.sem, i + (w_ready.base + s + 1))
                sp.dma_start(raw[:, s, :, :], wstream[bass.ds(i + (u0 + RAW + s), 1)]
                             .rearrange("a p n -> p (a n)").rearrange("p (k n) -> p k n", k=KT))\
                    .then_inc(w_loaded[s].sem, 16)
            n_load = min(n, NU - RAW - u0)
            if n_load > 0:
                with sp.Fori(0, n_load // RAW, 1) as i:
                    for s in range(RAW):
                        one(i * RAW, s)

        def act_high(a, sp_, u, i=0):
            s = u % SPL
            a.wait_ge(w_loaded[s].sem, i * 8 + 16 * ((state["G"] * UPP + u) // RAW + 1))
            if u >= SPL or not isinstance(i, int):
                a.wait_ge(tile_done.sem, i * 2 + (tile_done.base + 2 * (u - SPL + 1)))
            nc.scalar.activation(sp_.w_h[:, s, :, :], raw[:, s, :, :], ACT.Copy).then_inc(w_high.sem, 1)

        def pool_low(g, sp_, n):
            with g.Fori(0, n // SPL, 1) as i:
                for s in range(SPL):
                    g.wait_ge(w_high.sem, i * SPL + (w_high.base + s + 1))
                    nc.gpsimd.tensor_tensor(sp_.w_l[:, s, :, :], raw[:, s, :, :], sp_.w_h[:, s, :, :].bitcast(F32), ALU.subtract)\
                        .then_inc(w_ready.sem, 1)

        def pe_product(pe, sp_, kind, g=0, rhs=None, ready=None, ready_at=0, cols=T, free_wait=None,
                       after=None):
            in_h, in_l = (sp_.in_h, sp_.in_l) if rhs is None else rhs
            for u in range(UPP):
                s = u % SPL
                for half in range(2):
                    n = 2 * u + half
                    if half == 0:
                        pe.wait_ge(w_ready.sem, g * UPP + (w_ready.base + u + 1))
                    if free_wait is not None:
                        free_wait(n)
                    elif n >= 2 or g > 0 or tile_free.base > 0:
                        pe.wait_ge(tile_free.sem, tile_free.base + g * 8 + n - 1)
                    bank = 2 * half
                    parts = ((sp_.w_h, in_h), (sp_.w_h, in_l), (sp_.w_l, in_h))
                    if kind[u] == "f":
                        for k in range(KT):
                            if n == 0 and ready is not None:
                                pe.wait_ge(ready.sem, ready_at + (ready.base + k + 1))
                            for j, (w_, x_) in enumerate(parts):
                                lhs = w_[:, s, k, P * half:P * half + P]
                                st, en = k == 0 and j == 0, k == KT - 1 and j == 2
                                last = nc.tensor.matmul(ps[:, bank, :], lhs, x_[:, k, 0:512], start=st, stop=en)
                                if cols > 512:
                                    last = nc.tensor.matmul(ps[:, bank + 1, 0:cols - 512], lhs, x_[:, k, 512:cols],
                                                            start=st, stop=en)
                    else:
                        per = cols // P // 2
                        if n == 0 and ready is not None:
                            pe.wait_ge(ready.sem, ready_at + (ready.base + KT))
                        for q in range(per):
                            tok = (half * per + q) * P
                            dst = banks(bank, 1024)[:, q * UC:(q + 1) * UC]
                            for k in range(KT):
                                for j, (w_, x_) in enumerate(parts):
                                    last = nc.tensor.matmul(dst, x_[:, k, tok:tok + P], w_[:, s, k, :],
                                                            start=(k == 0 and j == 0), stop=(k == KT - 1 and j == 2))
                    last.then_inc(tile_done.sem, 1)
                    if after is not None:
                        after(n)

        def close_products(n, n_free=None):
            tile_done.base += 8 * n
            tile_free.base += 8 * (n if n_free is None else n_free)
            state["G"] += n
            w_high.base += UPP * n
            w_ready.base += UPP * n

        def wait_tile(eng, n, g=0):
            eng.wait_ge(tile_done.sem, g * 8 + (tile_done.base + n + 1))

        def act_rsqrt(eng, dst, mean, square, src, scale, done=None):
            nc.scalar.activation(dst, src, ACT.Ln, bias=pcol("eps"), scale=scale).then_inc(achain.sem, 1)
            nc.scalar.activation(mean, src, ACT.Identity, bias=pcol("eps"), scale=scale)
            eng.wait_ge(achain.sem, achain.base + act_chain.n + 1)
            nc.scalar.activation(dst, dst, ACT.Exp, scale=-0.5).then_inc(achain.sem, 1)
            eng.wait_ge(achain.sem, achain.base + act_chain.n + 2)
            nc.scalar.activation(square, dst, ACT.Square).then_inc((done or root_ready).sem, 1)
            act_chain.n += 2

        def refine(root, mean, square):
            dve_chain(nc.vector.scalar_tensor_tensor(mean, mean, -0.5, square, ALU.mult, ALU.mult))
            dve_chain(nc.vector.scalar_tensor_tensor(root, mean, 1.5, root, ALU.add, ALU.mult))

        def act_norm(eng, src, cols=T, loads=None, before_root=None, after_root=None):
            for k in range(KT):
                if k >= 2:
                    eng.wait_ge(sq_used.sem, sq_used.at(k - 1))
                if loads is not None and k in loads:
                    eng.wait_ge(*loads[k])
                nc.scalar.activation(sq[:, k % 2, 0:cols], src[:, k, 0:cols], ACT.Square).then_inc(sq_ready.sem, 1)
            if before_root is not None:
                before_root()
            eng.wait_ge(sq_used.sem, sq_used.at(KT))
            act_rsqrt(eng, rstd[:, 0:cols], sq[:, 0, 0:cols], sq[:, 1, 0:cols], banks(4, cols), 1.0 / D)
            if after_root is not None:
                after_root()

        def pe_norm(eng, cols=T):
            for k in range(KT):
                eng.wait_ge(sq_ready.sem, sq_ready.at(k + 1))
                last = nc.tensor.matmul(ps[:, 4, 0:512], ones, sq[:, k % 2, 0:512], start=(k == 0), stop=(k == KT - 1))
                if cols > 512:
                    last = nc.tensor.matmul(ps[:, 5, 0:cols - 512], ones, sq[:, k % 2, 512:cols],
                                            start=(k == 0), stop=(k == KT - 1))
                last.then_inc(sq_used.sem, 1)

        def dve_norm(eng, src, gain, sp_, cols=T):
            eng.wait_ge(root_ready.sem, root_ready.at(1))
            refine(rstd[:, 0:cols], sq[:, 0, 0:cols], sq[:, 1, 0:cols])

            def low(k):
                eng.wait_ge(in_high.sem, in_high.at(k + 1))
                nc.vector.tensor_tensor(sp_.in_l[:, k, 0:cols], sq[:, k % 2, 0:cols], sp_.in_h[:, k, 0:cols].bitcast(F32),
                                        ALU.subtract).then_inc(act_ready.sem, 1)
            for k in range(KT):
                if k >= 2:
                    eng.wait_ge(act_ready.sem, act_ready.at(k - 1))
                nc.vector.scalar_tensor_tensor(sq[:, k % 2, 0:cols], src[:, k, 0:cols], pcol(gain, k, 1), rstd[:, 0:cols],
                                               ALU.mult, ALU.mult).then_inc(in_made.sem, 1)
                if k >= 1:
                    low(k - 1)
            low(KT - 1)

        def act_norm_high(eng, sp_, cols=T):
            for k in range(KT):
                eng.wait_ge(in_made.sem, in_made.at(k + 1))
                nc.scalar.activation(sp_.in_h[:, k, 0:cols], sq[:, k % 2, 0:cols], ACT.Copy).then_inc(in_high.sem, 1)

        def dve_split(eng, src, sp_, cols=T):
            for k in range(KT + 1):
                if k < KT:
                    nc.vector.tensor_copy(sp_.in_h[:, k, 0:cols], src[:, k, 0:cols]).then_inc(in_high.sem, 1)
                if k >= 1:
                    eng.wait_ge(in_high.sem, in_high.at(k))
                    nc.vector.tensor_tensor(sp_.in_l[:, k - 1, 0:cols], src[:, k - 1, 0:cols],
                                            sp_.in_h[:, k - 1, 0:cols].bitcast(F32), ALU.subtract).then_inc(act_ready.sem, 1)

        def close_norm():
            sq_ready.base += KT
            sq_used.base += KT
            root_ready.base += 1
            in_high.base += KT
            in_made.base += KT

        def head_norm_stage(items, mat, width, cols=T, extra=None):
            n_items = len(items)
            hn = ExitStack()
            serial[0] += 1
            rstd_b = sb(f"rstd_b{serial[0]}", [P, T], on=hn)

            nt = sb(f"newton{serial[0]}", [P, 2, 2, T], on=hn)

            def rstd2(i):
                return rstd if i % 2 == 0 else rstd_b

            with nc.Block() as block:
                @block.scalar
                def _(a):
                    c = 0
                    for i, (srcs, gn, dsts) in enumerate(items):
                        for j, s in enumerate(srcs):
                            if c >= 2:
                                a.wait_ge(sq_used.sem, sq_used.at(c - 1))
                            nc.scalar.activation(sq[:, c % 2, 0:cols], s, ACT.Square).then_inc(sq_ready.sem, 1)
                            c += 1
                        a.wait_ge(sq_used.sem, sq_used.at(c))
                        if i >= 2:
                            a.wait_ge(normed.sem, normed.at(i - 1))
                        act_rsqrt(a, rstd2(i)[:, 0:cols], nt[:, i % 2, 0, 0:cols], nt[:, i % 2, 1, 0:cols],
                                  banks(4 + 2 * (i % 2), cols), 1.0 / width)
                    act_chain.close()

                @block.tensor
                def _(pe):
                    c = 0
                    for i, (srcs, gn, dsts) in enumerate(items):
                        if i >= 2:
                            pe.wait_ge(root_ready.sem, root_ready.at(i - 1))
                        for j, s in enumerate(srcs):
                            pe.wait_ge(sq_ready.sem, sq_ready.at(c + 1))
                            st, sp_ = j == 0, j == len(srcs) - 1
                            b = 4 + 2 * (i % 2)
                            last = nc.tensor.matmul(ps[:, b, :], mat, sq[:, c % 2, 0:512], start=st, stop=sp_)
                            if cols > 512:
                                last = nc.tensor.matmul(ps[:, b + 1, 0:cols - 512], mat, sq[:, c % 2, 512:cols],
                                                        start=st, stop=sp_)
                            last.then_inc(sq_used.sem, 1)
                            c += 1

                @block.vector
                def _(v):
                    dve_chain.start(v)
                    for i, (srcs, gn, dsts) in enumerate(items):
                        v.wait_ge(root_ready.sem, root_ready.at(i + 1))
                        refine(rstd2(i)[:, 0:cols], nt[:, i % 2, 0, 0:cols], nt[:, i % 2, 1, 0:cols])
                        for s, g_, d in zip(srcs, gn, dsts):
                            last = nc.vector.scalar_tensor_tensor(d, s, g_, rstd2(i)[:, 0:cols], ALU.mult, ALU.mult)
                        last.then_inc(normed.sem, 1)
                        if extra is not None:
                            extra(v, i)
                    dve_chain.close()
            hn.close()
            n_sq = sum(len(i[0]) for i in items)
            sq_ready.base += n_sq
            sq_used.base += n_sq
            root_ready.base += n_items
            normed.base += n_items

        with nc.Block() as block:
            @block.sync
            def _(sp):
                sp.dma_start(par[:, :], params).then_inc(loaded.sem, 16)
                sp.dma_start(x[:, :, :], x_in.rearrange("(k p) t -> p k t", p=P)).then_inc(loaded.sem, 16)
                for s in range(RAW):
                    sp.dma_start(raw[:, s, :, :], wstream[s].rearrange("p (k n) -> p k n", k=KT))\
                        .then_inc(w_loaded[s].sem, 16)
                sp.wait_ge(loaded.sem, 32)

            @block.scalar
            def _(a):
                nc.scalar.preload_act_table_set("natural_log_exp_and_others")

            @block.vector
            def _(v):
                v.wait_ge(loaded.sem, 32)
                nc.vector.tensor_scalar(gains[:, 0:1], pcol("dq"), float(64 ** -0.5), None, ALU.mult).then_inc(ev["ev0"].sem, 1)
                nc.vector.tensor_scalar(gains[:, 1:2], pcol("dnorm"), 1.0 - LAMBDA_INIT, None, ALU.mult).then_inc(ev["ev0"].sem, 1)
                nc.vector.tensor_scalar(gains[:, 2:4], pcol("xq0"), 1.0 / 16.0, None, ALU.mult).then_inc(ev["ev0"].sem, 1)
                nc.vector.tensor_scalar(gains[:, 4:6], pcol("xq1"), 1.0 / 16.0, None, ALU.mult).then_inc(ev["ev0"].sem, 1)
                v.wait_ge(ev["ev0"].sem, 4)
        loaded.base += 32
        ev["ev0"].base += 4

        def product_stage(src, kinds, evac, norm=None, cols=T, evac_engine="vector",
                          dve_pre=None, act_pre=None, dve_post=None, pe_post=None, heads=None, loads=None):
            n = len(kinds)
            local = ExitStack()
            sp_ = Split(local, cols)
            if heads is not None:
                h_prod, h_per, h_mat, h_width, h_tile, h_gain = heads
                mean = sb(f"mean{serial[0]}", [P, cols], on=local)
                n_heads = 8 * h_prod // h_per

            def pe_head(pe, tile):
                if heads is None or tile == 0 or tile % h_per or tile // h_per > n_heads:
                    return
                i = tile // h_per - 1
                if i >= 1:
                    pe.wait_ge(hn_root.sem, hn_root.at(i))
                for j in range(h_per):
                    pe.wait_ge(hn_square.sem, hn_square.at(h_per * i + j + 1))
                    last = nc.tensor.matmul(ps[:, 4, 0:512], h_mat, sq[:, j, 0:512], start=(j == 0), stop=(j == h_per - 1))
                    if cols > 512:
                        last = nc.tensor.matmul(ps[:, 5, 0:cols - 512], h_mat, sq[:, j, 512:cols],
                                                start=(j == 0), stop=(j == h_per - 1))
                last.then_inc(hn_sum.sem, 1)

            def act_head(a, tile):
                if heads is None:
                    return
                if 0 < tile <= 8 * h_prod and tile % h_per == 0:
                    i = tile // h_per - 1
                    a.wait_ge(hn_sum.sem, hn_sum.at(i + 1))
                    if i >= 1:
                        a.wait_ge(hn_done.sem, hn_done.at(i))
                    act_rsqrt(a, rstd[:, 0:cols], mean[:, 0:cols], sq[:, h_per % 2, 0:cols], banks(4, cols), 1.0 / h_width,
                              done=hn_root)
                if tile < 8 * h_prod:
                    if h_per == 2 and tile >= 2 and tile % 2 == 0:
                        a.wait_ge(hn_done.sem, hn_done.at(tile // 2))
                    a.wait_ge(tile_free.sem, tile_free.base + tile + 1)
                    nc.scalar.activation(sq[:, tile % h_per, 0:cols], h_tile(tile), ACT.Square).then_inc(hn_square.sem, 1)

            def dve_heads(v):
                if heads is None:
                    return
                for i in range(n_heads):
                    v.wait_ge(hn_root.sem, hn_root.at(i + 1))
                    refine(rstd[:, 0:cols], mean[:, 0:cols], sq[:, h_per % 2, 0:cols])
                    for j in range(h_per):
                        t_ = h_tile(h_per * i + j)
                        last = nc.vector.scalar_tensor_tensor(t_, t_, h_gain(h_per * i + j), rstd[:, 0:cols],
                                                              ALU.mult, ALU.mult)
                    last.then_inc(hn_done.sem, 1)

            with nc.Block() as block:
                @block.sync
                def _(sp):
                    if loads is not None:
                        loads[0](sp)
                    sp_weights(sp, n * UPP)

                @block.gpsimd
                def _(g):
                    pool_low(g, sp_, n * UPP)

                @block.tensor
                def _(pe):
                    if norm is not None:
                        pe_norm(pe, cols)
                    for g in range(n):
                        pe_product(pe, sp_, kinds[g], g, cols=cols, ready=act_ready if g == 0 else None,
                                   after=lambda i, g=g: pe_head(pe, 8 * g + i))
                    if heads is not None and h_prod == n:
                        pe_head(pe, 8 * n)
                    if pe_post is not None:
                        pe_post(pe, sp_)

                @block.vector
                def _(v):
                    dve_chain.start(v)
                    if dve_pre is not None:
                        dve_pre(v)
                    if norm is not None:
                        dve_norm(v, src, norm, sp_, cols)
                    else:
                        dve_split(v, src, sp_, cols)
                    if dve_post is not None:
                        dve_post(v)
                    dve_heads(v)
                    if evac_engine == "vector":
                        for g in range(n):
                            for i in range(8):
                                wait_tile(v, i, g)
                                evac(v, g, i)
                    dve_chain.close()

                @block.scalar
                def _(a):
                    if act_pre is not None:
                        act_pre(a)
                    if norm is not None:
                        act_norm(a, src, cols, loads=None if loads is None else loads[1],
                                 before_root=lambda: act_high(a, sp_, 0), after_root=lambda: act_high(a, sp_, 1))
                        act_norm_high(a, sp_, cols)
                    else:
                        for u in range(SPL):
                            act_high(a, sp_, u)
                    for u in range(n * UPP):
                        if 1 <= u and u + 1 < n * UPP:
                            act_high(a, sp_, u + 1)
                        if evac_engine == "scalar":
                            for i in (2 * u, 2 * u + 1):
                                wait_tile(a, i)
                                evac(a, i // 8, i % 8)
                                act_head(a, i)
                    if heads is not None and h_prod == n:
                        act_head(a, 8 * n)
                    act_chain.close()
            if norm is not None:
                close_norm()
            else:
                in_high.base += KT
            act_ready.base += KT
            close_products(n)
            if heads is not None:
                hn_square.base += 8 * h_prod
                for s_ in (hn_sum, hn_root, hn_done):
                    s_.base += n_heads
            local.close()

        def free(ins):
            return ins.then_inc(tile_free.sem, 1)

        def add_residual(v, g, i):
            free(nc.vector.tensor_tensor(x[:, i, :], banks(2 * (i % 2)), x[:, i, :], ALU.add))

        def mlp(layer):
            local = ExitStack()
            sp_ = Split(local)
            h_h = sb(f"h_h{layer}", [P, KT, T], F32R, on=local)
            h_l = sb(f"h_l{layer}", [P, KT, T], F32R, on=local)
            ht = sb(f"ht{layer}", [P, 2, T], on=local)
            with nc.Block() as block:
                @block.sync
                def _(sp):
                    sp_weights(sp, 2 * FB * UPP)

                @block.gpsimd
                def _(g):
                    pool_low(g, sp_, 2 * FB * UPP)

                @block.tensor
                def _(pe):
                    pe_norm(pe)
                    pe.wait_ge(act_ready.sem, act_ready.at(KT))
                    with pe.Fori(0, FB, 1) as fb:
                        def up_wait(n):
                            if n < 2:
                                pe.wait_ge(tile_free.sem, fb * 8 + (tile_free.base + n - 1))
                            else:
                                pe.wait_ge(hid_free.sem, fb * 8 + (hid_free.base + n - 1))

                        def down_wait(n):
                            if n < 2:
                                pe.wait_ge(hid_free.sem, fb * 8 + (hid_free.base + 8 + n - 1))
                            else:
                                pe.wait_ge(tile_free.sem, fb * 8 + (tile_free.base + n - 1))
                        pe_product(pe, sp_, "ffff", fb * 2, free_wait=up_wait)
                        pe_product(pe, sp_, "ffff", fb * 2 + 1, rhs=(h_h, h_l), ready=hid_ready, ready_at=fb * KT,
                                   free_wait=down_wait)

                @block.vector
                def _(v):
                    dve_chain.start(v)
                    dve_norm(v, x, f"mlp{layer}", sp_)
                    with v.Fori(0, FB, 1) as fb:
                        for i in range(8):
                            v.wait_ge(hid_made.sem, fb * 8 + (hid_made.base + i + 1))
                            nc.vector.tensor_copy(h_h[:, i, :], ht[:, i % 2, :]).then_inc(hid_high.sem, 1)
                            v.wait_ge(hid_high.sem, fb * 8 + (hid_high.base + i + 1))
                            nc.vector.tensor_tensor(h_l[:, i, :], ht[:, i % 2, :], h_h[:, i, :].bitcast(F32), ALU.subtract)\
                                .then_inc(hid_ready.sem, 1)
                        for i in range(8):
                            wait_tile(v, i, fb * 2 + 1)
                            add_residual(v, 0, i)
                    dve_chain.close()

                @block.scalar
                def _(a):
                    act_high(a, sp_, 0)
                    act_high(a, sp_, 1)
                    act_norm(a, x)
                    act_norm_high(a, sp_)

                    def up(i, fb):
                        wait_tile(a, i, fb * 2)
                        nc.scalar.activation(sq[:, i % 2, :], banks(2 * (i % 2)), ACT.Relu).then_inc(hid_free.sem, 1)
                        a.wait_ge(hid_free.sem, fb * 8 + (hid_free.base + i + 1))
                        if fb * 8 + i >= 2:
                            a.wait_ge(hid_ready.sem, fb * 8 + (hid_ready.base + i - 1))
                        nc.scalar.activation(ht[:, i % 2, :], sq[:, i % 2, :], ACT.Square).then_inc(hid_made.sem, 1)

                    for fb in range(FB):
                        for u in range(2 * UPP):
                            n = 2 * UPP * fb + u + 1
                            if 2 <= n < 2 * UPP * FB:
                                act_high(a, sp_, n)
                            if u < UPP:
                                up(2 * u, fb)
                                up(2 * u + 1, fb)
                    act_chain.close()
            close_norm()
            act_ready.base += KT
            close_products(2 * FB, FB)
            hid_free.base += 8 * FB
            hid_ready.base += KT * FB
            hid_made.base += KT * FB
            hid_high.base += KT * FB
            local.close()

        def cross(layer):
            local, l_mem = ExitStack(), ExitStack()
            km = sb(f"km{layer}", [P, KT, M], on=local)
            vm = sb(f"vm{layer}", [P, 4, D], on=local)
            mem = sb(f"mem{layer}", [P, KT, M], on=l_mem)
            ld = dma["dma0"]
            mem_halves = (ld, dma["dma1"])

            def load_mem(sp):
                for i, s_ in enumerate(mem_halves):
                    sp.dma_start(mem[:, 4 * i:4 * i + 4, :], mem_in[512 * i:512 * i + 512].rearrange("(k p) t -> p k t", p=P))\
                        .then_inc(s_.sem, 16)

            def evac_mem(a, g, i):
                if g == 0:
                    free(nc.scalar.activation(km[:, i, :], ps[:, 2 * (i % 2), :], ACT.Copy))
                else:
                    s, half = i // 2, i % 2
                    free(nc.scalar.activation(vm[:, 2 * half:2 * half + 2, s * UC:(s + 1) * UC],
                                              ps[:, 2 * half, :].rearrange("p (j n) -> p j n", j=2), ACT.Copy))
            product_stage(mem, ["ffff", "tttt"], evac_mem, norm=f"mem{layer}", cols=M, evac_engine="scalar",
                          heads=(1, 2, ones, 256, lambda n: km[:, n, :], lambda n: pcol(f"xk{layer}", n % 2, 1)),
                          loads=(load_mem, {4 * i: (s_.sem, s_.at(16)) for i, s_ in enumerate(mem_halves)}))
            for s_ in mem_halves:
                s_.base += 16
            l_mem.close()

            def evac_q(a, g, i):
                free(nc.scalar.activation(qx[:, i, :], banks(2 * (i % 2)), ACT.Copy))
            qx = sb(f"qx{layer}", [P, KT, T], on=local)
            product_stage(x, ["ffff"], evac_q, norm=f"cross{layer}", evac_engine="scalar",
                          heads=(1, 2, ones, 256, lambda n: qx[:, n, :],
                                 lambda n: gains[:, 2 + 2 * layer + n % 2:3 + 2 * layer + n % 2]))
            att = ExitStack()
            s_sb = sb(f"xs{layer}", [P, 2, TT, 256], on=att)
            pt = sb(f"xpt{layer}", [P, 2, T], on=att)
            st = sb(f"xst{layer}", [P, 2, 4, TT], on=att)
            sc_done, neg_ready, exp_done, p_ready, tr_done, pt_ready, o_done, o_free = (ev[f"ev{i}"] for i in range(8))
            with nc.Block() as block:
                @block.tensor
                def _(pe):

                    def scores(h):
                        if h >= 1:
                            pe.wait_ge(exp_done.sem, exp_done.at(h))
                        for q in range(TT):
                            mo = 0 if q < 4 else 256
                            dst = ps[:, q // 2, (q % 2) * 256:(q % 2) * 256 + 256]
                            for j in range(2):
                                last = nc.tensor.matmul(dst, qx[:, 2 * h + j, q * P:(q + 1) * P], km[:, 2 * h + j, mo:mo + 256],
                                                        start=(j == 0), stop=(j == 1))
                        last.then_inc(sc_done.sem, 1)
                    scores(0)
                    for h in range(XH):
                        if h + 1 < XH:
                            scores(h + 1)
                        pe.wait_ge(p_ready.sem, p_ready.at(h + 1))
                        if h >= 1:
                            pe.wait_ge(pt_ready.sem, pt_ready.at(h))
                        for q in range(TT):
                            for j in range(2):
                                c = (q * 2 + j) * P
                                last = nc.tensor.transpose(ps[:, 4 + c // 512, c % 512:c % 512 + P],
                                                           s_sb[:, h % 2, q, j * P:(j + 1) * P], ident)
                        last.then_inc(tr_done.sem, 1)
                        pe.wait_ge(pt_ready.sem, pt_ready.at(h + 1))
                        for j in range(2):
                            n = 2 * h + j
                            if n >= 1:
                                pe.wait_ge(o_free.sem, o_free.at(n))
                            for kt in range(2):
                                lhs = vm[:, kt, (2 * h + j) * P:(2 * h + j + 1) * P]
                                nc.tensor.matmul(ps[:, 7, :], lhs, pt[:, kt, 0:512], start=(kt == 0), stop=(kt == 1))
                            for kt in range(2):
                                lhs = vm[:, 2 + kt, (2 * h + j) * P:(2 * h + j + 1) * P]
                                last = nc.tensor.matmul(ps[:, 3, 0:256], lhs, pt[:, kt, 512:T], start=(kt == 0), stop=(kt == 1))
                            last.then_inc(o_done.sem, 1)

                @block.vector
                def _(v):
                    dve_chain.start(v)

                    def maxima(h):
                        v.wait_ge(sc_done.sem, sc_done.at(h + 1))
                        sc = ps[:, 0:3, :].rearrange("p b (q n) -> p (b q) n", q=2)
                        dve_chain(nc.vector.tensor_reduce(st[:, h % 2, 0, :], sc, AX.X, ALU.max))
                        nc.vector.tensor_scalar(st[:, h % 2, 1, :], st[:, h % 2, 0, :], -1.0, None, ALU.mult)\
                            .then_inc(neg_ready.sem, 1)
                    maxima(0)
                    for h in range(XH):
                        s_ = st[:, h % 2]
                        v.wait_ge(exp_done.sem, exp_done.at(h + 1))
                        dve_chain(nc.vector.reciprocal(s_[:, 3, :], s_[:, 2, :]))
                        nc.vector.tensor_tensor(s_sb[:, h % 2, :, :], s_sb[:, h % 2, :, :],
                                                s_[:, 3, :].unsqueeze(2).to_broadcast([P, TT, 256]), ALU.mult)\
                            .then_inc(p_ready.sem, 1)
                        if h + 1 < XH:
                            maxima(h + 1)
                        for j in range(2):
                            n = 2 * h + j
                            v.wait_ge(o_done.sem, o_done.at(n + 1))
                            nc.vector.tensor_copy(qx[:, n, 0:512], ps[:, 7, :])
                            nc.vector.tensor_copy(qx[:, n, 512:T], ps[:, 3, 0:256]).then_inc(o_free.sem, 1)
                    dve_chain.close()

                @block.scalar
                def _(a):

                    def exps(h):
                        a.wait_ge(neg_ready.sem, neg_ready.at(h + 1))
                        if h >= 2:
                            a.wait_ge(tr_done.sem, tr_done.at(h - 1))
                        for q in range(TT):
                            last = nc.scalar.activation(s_sb[:, h % 2, q, :], ps[:, q // 2, (q % 2) * 256:(q % 2) * 256 + 256],
                                                        ACT.Exp, bias=st[:, h % 2, 1, q:q + 1],
                                                        accum_out=st[:, h % 2, 2, q:q + 1])
                        last.then_inc(exp_done.sem, 1)
                    exps(0)
                    for h in range(XH):
                        if h + 1 < XH:
                            exps(h + 1)
                        a.wait_ge(tr_done.sem, tr_done.at(h + 1))
                        if h >= 1:
                            a.wait_ge(o_done.sem, o_done.at(2 * h))
                        tr = ps[:, 4:7, :].rearrange("p b n -> p (b n)").rearrange("p (q j n) -> p j q n", j=2, n=P)
                        nc.scalar.activation(pt[:, 0, :].rearrange("p (q n) -> p q n", n=P), tr[:, 0], ACT.Copy)
                        nc.scalar.activation(pt[:, 1, :].rearrange("p (q n) -> p q n", n=P), tr[:, 1], ACT.Copy)\
                            .then_inc(pt_ready.sem, 1)
            for s_ in (sc_done, neg_ready, exp_done, p_ready, tr_done, pt_ready):
                s_.base += XH
            o_done.base += 2 * XH
            o_free.base += 2 * XH
            att.close()
            product_stage(qx, ["ffff"], add_residual)
            local.close()

        def diff_attention():
            qkv, local = ExitStack(), ExitStack()
            b1, b2, b3 = (sb(n, [P, KT, T], on=qkv) for n in ("dq_sb", "dk_sb", "dv_sb"))

            def evac(a, g, i):
                if g < 2:
                    free(nc.scalar.activation((b1, b2)[g][:, i, :], banks(2 * (i % 2)), ACT.Copy))
                else:
                    s, half = i // 2, i % 2
                    src = banks(2 * half).rearrange("p (j n) -> p j n", j=3)
                    free(nc.scalar.activation(vtok[:, 3 * half:3 * half + 3, s * UC:(s + 1) * UC], src, ACT.Copy))
            vtok = b3[:, :, :].rearrange("p k t -> p (k t)").rearrange("p (j n) -> p j n", j=TT)
            product_stage(x, ["ffff", "ffff", "tttt"], evac, norm="mix1", evac_engine="scalar",
                          heads=(2, 1, ones64, 64, lambda n: (b1, b2)[n // 8][:, n % 8, :],
                                 lambda n: gains[:, 0:1] if n < 8 else pcol("dk")))

            sc = sb("dsc", [P, 2, 2, 512], on=local)
            bias = sb("dbias", [P, 2, DIST], on=local)
            at = sb("dat", [P, 2, 512], on=local)
            st = sb("dst", [P, 2, 8], on=local)
            dist = sb("dist", [P, DIST], on=local)
            lam = sb("dlam", [P, 8], on=local)
            sc_done, neg_ready, exp_done, a_ready, tr_done, at_ready, o_done, o_free, bias_ready, bias_used, lam_a, lam_b, e0_ready = (
                ev[f"ev{i}"] for i in range(13))
            items = [(h, q) for h in range(DH) for q in range(TT)]
            with nc.Block() as block:
                @block.sync
                def _(sp):
                    sp.dma_start(dist[:, :], tab_in[:, TAB["dist"][0]:TAB["dist"][0] + DIST]).then_inc(dma["dma0"].sem, 16)

                @block.vector
                def _(v):
                    dve_chain.start(v)
                    nc.vector.tensor_tensor(lam[:, 0:2], pcol("lq"), pcol("lk"), ALU.mult).then_inc(lam_a.sem, 1)
                    v.wait_ge(lam_a.sem, lam_a.at(3))
                    dve_chain(nc.vector.tensor_tensor(lam[:, 4:5], lam[:, 3:4], lam[:, 2:3], ALU.subtract))
                    dve_chain(nc.vector.tensor_scalar(lam[:, 5:6], lam[:, 4:5], -LAMBDA_INIT, None, ALU.add))

                    def biased(n):
                        h, q = items[n]
                        keys = 512 if q < 4 else 256
                        b = n % 2
                        off = 384 - P * (q if q < 4 else q - 4)
                        if q == 0:
                            v.wait_ge(bias_ready.sem, bias_ready.at(h + 1))
                        v.wait_ge(sc_done.sem, sc_done.at(n + 1))
                        if n >= 2:
                            v.wait_ge(tr_done.sem, tr_done.at(n - 1))
                        for z in range(2):
                            nc.vector.tensor_tensor_reduce(
                                out=sc[:, b, z, 0:keys], in0=ps[:, 2 * b + z, 0:keys], in1=bias[:, h % 2, off:off + keys],
                                scale=1.0, scalar=-3.0e38, op0=ALU.add, op1=ALU.max, accum_out=st[:, b, z:z + 1])\
                                .then_inc(dchain.sem, 1)
                            dve_chain.n += 1
                        v.wait_ge(dchain.sem, dchain.base + dve_chain.n)
                        nc.vector.tensor_scalar(st[:, b, 2:4], st[:, b, 0:2], -1.0, None, ALU.mult).then_inc(neg_ready.sem, 1)

                    def combined(n):
                        h, q = items[n]
                        keys = 512 if q < 4 else 256
                        b = n % 2
                        v.wait_ge(exp_done.sem, exp_done.at(n + 1))
                        dve_chain(nc.vector.reciprocal(st[:, b, 6:8], st[:, b, 4:6]))
                        nc.vector.tensor_scalar(sc[:, b, 0, 0:keys], sc[:, b, 0, 0:keys], st[:, b, 6:7], None, ALU.mult)
                        dve_chain(nc.vector.tensor_tensor(st[:, b, 7:8], st[:, b, 7:8], lam[:, 5:6], ALU.mult))
                        nc.vector.scalar_tensor_tensor(sc[:, b, 0, 0:keys], sc[:, b, 1, 0:keys], st[:, b, 7:8],
                                                       sc[:, b, 0, 0:keys], ALU.mult, ALU.add).then_inc(a_ready.sem, 1)
                    biased(0)
                    for n in range(len(items)):
                        if n + 1 < len(items):
                            biased(n + 1)
                        combined(n)
                    dve_chain.close()

                @block.gpsimd
                def _(g):
                    g.wait_ge(dma["dma0"].sem, dma["dma0"].at(16))
                    for h in range(DH):
                        if h >= 2:
                            g.wait_ge(neg_ready.sem, neg_ready.at(TT * (h - 1)))
                        nc.gpsimd.tensor_scalar(bias[:, h % 2, :], dist[:, :], -float(2.0 ** -(h + 1)), None, ALU.mult)\
                            .then_inc(bias_ready.sem, 1)

                @block.scalar
                def _(a):
                    a.wait_ge(lam_a.sem, lam_a.at(2))
                    nc.scalar.activation(lam[:, 2:4], ps[:, 7, 0:2], ACT.Exp).then_inc(lam_a.sem, 1)

                    def after(n):
                        h, q = items[n]
                        nk = 4 if q < 4 else 2
                        a.wait_ge(tr_done.sem, tr_done.at(n + 1))
                        if n >= 2:
                            a.wait_ge(o_done.sem, o_done.at(n - 1))
                        nc.scalar.activation(at[:, n % 2, 0:nk * P], ps[:, 4 + n % 2, 0:nk * P], ACT.Copy).then_inc(at_ready.sem, 1)
                        if q == TT - 1:
                            a.wait_ge(o_done.sem, o_done.at(n + 1))
                            nc.scalar.activation(b1[:, h, :], banks(6), ACT.Copy).then_inc(o_free.sem, 1)
                    for n, (h, q) in enumerate(items):
                        keys = 512 if q < 4 else 256
                        b = n % 2
                        a.wait_ge(neg_ready.sem, neg_ready.at(n + 1))
                        for z in range(2):
                            last = nc.scalar.activation(sc[:, b, z, 0:keys], sc[:, b, z, 0:keys], ACT.Exp,
                                                        bias=st[:, b, 2 + z:3 + z], accum_out=st[:, b, 4 + z:5 + z])
                        last.then_inc(exp_done.sem, 1)
                        if n >= 1:
                            after(n - 1)
                    after(len(items) - 1)

                @block.tensor
                def _(pe):
                    pe.wait_ge(lam_a.sem, lam_a.at(1))
                    nc.tensor.matmul(ps[:, 7, 0:2], ones, lam[:, 0:2], start=True, stop=True).then_inc(lam_a.sem, 1)

                    def scores(n):
                        h, q = items[n]
                        keys, k0 = (512, 0) if q < 4 else (256, 512)
                        if n >= 2:
                            pe.wait_ge(neg_ready.sem, neg_ready.at(n - 1))
                        for z in range(2):
                            rows = slice(64 * z, 64 * z + 64)
                            last = nc.tensor.matmul(ps[:, 2 * (n % 2) + z, 0:keys], b1[rows, h, q * P:(q + 1) * P],
                                                    b2[rows, h, k0:k0 + keys], start=True, stop=True)
                        last.then_inc(sc_done.sem, 1)

                    def values(n):
                        h, q = items[n]
                        nk, t0 = (4, 0) if q < 4 else (2, 4)
                        pe.wait_ge(a_ready.sem, a_ready.at(n + 1))
                        if n >= 2:
                            pe.wait_ge(at_ready.sem, at_ready.at(n - 1))
                        for j in range(nk):
                            last = nc.tensor.transpose(ps[:, 4 + n % 2, j * P:(j + 1) * P], sc[:, n % 2, 0, j * P:(j + 1) * P], ident)
                        last.then_inc(tr_done.sem, 1)

                    def outputs(n):
                        h, q = items[n]
                        nk, t0 = (4, 0) if q < 4 else (2, 4)
                        pe.wait_ge(at_ready.sem, at_ready.at(n + 1))
                        if q == 0 and h >= 1:
                            pe.wait_ge(o_free.sem, o_free.at(h))
                        if n == 0:
                            pe.wait_ge(lam_a.sem, lam_a.at(3))
                        for j in range(nk):
                            last = nc.tensor.matmul(banks(6)[:, q * P:(q + 1) * P], vtok[:, t0 + j, h * P:(h + 1) * P],
                                                    at[:, n % 2, j * P:(j + 1) * P], start=(j == 0), stop=(j == nk - 1))
                        last.then_inc(o_done.sem, 1)
                    scores(0)
                    scores(1)
                    for n in range(len(items)):
                        if n + 2 < len(items):
                            scores(n + 2)
                        values(n)
                        if n >= 1:
                            outputs(n - 1)
                    outputs(len(items) - 1)
            ni = len(items)
            for s_ in (sc_done, neg_ready, exp_done, a_ready, tr_done, at_ready, o_done):
                s_.base += ni
            o_free.base += DH
            bias_ready.base += DH
            lam_a.base += 3
            dma["dma0"].base += 16
            local.close()
            head_norm_stage([([b1[:, h, :]], [gains[:, 1:2]], [b1[:, h, :]]) for h in range(DH)], ones, 128)
            product_stage(b1, ["ffff"], add_residual)
            qkv.close()

        def s5_gla():
            outer, local, prep, s5mem = ExitStack(), ExitStack(), ExitStack(), ExitStack()
            b1 = sb("uqk", [P, KT, T], on=outer)
            b2 = sb("vog", [P, KT, T], on=outer)
            lr = sb("lr", [32, T], on=outer)
            sm = sb("s5small", [P, 32, G], on=local)
            names = ["step", "zr", "zi", "kk", "r", "rh", "sin", "sinh", "cos", "mag", "r8", "lbr", "lbi", "nr", "den", "cr",
                     "ci", "t0", "t1", "t2", "t3", "p2r", "p2i", "p4r", "p4i"]
            S = {n: sm[:, i, :] for i, n in enumerate(names)}
            bbar = sb("bbar", [P, 2, G, GC], on=local)
            cc = sb("cc", [P, 2, G, GC], on=local)
            qf = sb("qf", [P, 2, POS, G], on=local)
            qr = sb("qr", [P, 2, SC, G], on=local)
            pw = sb("pw", [P, 2, SC + 1, G], on=prep)
            wglr = sb("wglr_sb", [P, KT, 32], on=prep)
            bin_ = sb("bin", [P, 2, G, GC], on=prep)
            pc_in, pc_out = ev["ev0"], ev["ev1"]
            ld = dma["dma0"]

            def tt(o, a, b, op):
                dve_chain(nc.vector.tensor_tensor(o, a, b, op))

            def ts(o, a, s1, s2, op0, op1=None):
                dve_chain(nc.vector.tensor_scalar(o, a, s1, s2, op0, op1) if op1 is not None
                          else nc.vector.tensor_scalar(o, a, s1, s2, op0))

            def cmul(dr, di, ar, ai, br, bi, t, conj=False, done=None):
                nc.vector.tensor_tensor(t[0], ar, br, ALU.mult)
                nc.vector.tensor_tensor(t[1], ai, bi, ALU.mult)
                nc.vector.tensor_tensor(t[2], ar, bi, ALU.mult)
                dve_chain(nc.vector.tensor_tensor(t[3], ai, br, ALU.mult))
                nc.vector.tensor_tensor(dr, t[0], t[1], ALU.add if conj else ALU.subtract)
                if conj:
                    last = nc.vector.tensor_tensor(di, t[3], t[2], ALU.subtract)
                else:
                    last = nc.vector.tensor_tensor(di, t[3], t[2], ALU.add)
                if done is None:
                    dve_chain(last)
                else:
                    last.then_inc(done.sem, 1)

            def bc_g(a, n):
                return a.unsqueeze(2).to_broadcast([P, a.shape[1], n])

            def dve_pre(v):
                v.wait_ge(pc_in.sem, pc_in.at(1))
                tt(S["zr"], pcol("lre"), S["step"], ALU.mult)
                tt(S["zi"], pcol("lim"), S["step"], ALU.mult)
                ts(S["kk"], S["zi"], 1.0 / (2 * math.pi), MAGIC, ALU.mult, ALU.add)
                ts(S["kk"], S["kk"], -MAGIC, None, ALU.add)
                dve_chain(nc.vector.scalar_tensor_tensor(S["r"], S["kk"], -TWO_PI_HI, S["zi"], ALU.mult, ALU.add))
                dve_chain(nc.vector.scalar_tensor_tensor(S["r"], S["kk"], -TWO_PI_LO, S["r"], ALU.mult, ALU.add))
                nc.vector.tensor_scalar(S["r"], S["r"], 3.1415925, -3.1415925, ALU.min, ALU.max).then_inc(pc_out.sem, 1)

            def act_pre(a):
                nc.scalar.activation(S["step"], pcol("lstep"), ACT.Exp).then_inc(pc_in.sem, 1)
                a.wait_ge(pc_out.sem, pc_out.at(1))
                nc.scalar.activation(S["mag"], S["zr"], ACT.Exp)
                nc.scalar.activation(S["r8"], S["zr"], ACT.Exp, scale=float(SC))
                nc.scalar.activation(S["sin"], S["r"], ACT.Sin)
                nc.scalar.activation(S["sinh"], S["r"], ACT.Sin, scale=0.5).then_inc(pc_in.sem, 1)

            def dve_post(v):
                v.wait_ge(pc_in.sem, pc_in.at(2))
                tmp = [S[f"t{i}"] for i in range(4)]
                tt(S["t0"], S["sinh"], S["sinh"], ALU.mult)
                ts(S["cos"], S["t0"], -2.0, 1.0, ALU.mult, ALU.add)
                tt(S["lbr"], S["mag"], S["cos"], ALU.mult)
                tt(S["lbi"], S["mag"], S["sin"], ALU.mult)
                ts(S["nr"], S["lbr"], -1.0, None, ALU.add)
                tt(S["t0"], pcol("lre"), pcol("lre"), ALU.mult)
                tt(S["t1"], pcol("lim"), pcol("lim"), ALU.mult)
                tt(S["den"], S["t0"], S["t1"], ALU.add)
                dve_chain(nc.vector.reciprocal(S["den"], S["den"]))
                cmul(S["cr"], S["ci"], S["nr"], S["lbi"], pcol("lre"), pcol("lim"), tmp, conj=True)
                tt(S["cr"], S["cr"], S["den"], ALU.mult)
                tt(S["ci"], S["ci"], S["den"], ALU.mult)
                v.wait_ge(ld.sem, ld.at(48))
                t3 = [sq[:, i // 2, (i % 2) * 384:(i % 2) * 384 + 256].rearrange("p (g c) -> p g c", c=GC) for i in range(4)]
                for h in range(2):
                    gs = slice(16 * h, 16 * h + 16)
                    cmul(bbar[:, 0, gs, :], bbar[:, 1, gs, :], bin_[:, 0, gs, :], bin_[:, 1, gs, :],
                         bc_g(S["cr"][:, gs], GC), bc_g(S["ci"][:, gs], GC), t3)
                nc.vector.memset(pw[:, 0, 0, :], 1.0)
                nc.vector.memset(pw[:, 1, 0, :], 0.0)
                nc.vector.tensor_copy(pw[:, 0, 1, :], S["lbr"])
                dve_chain(nc.vector.tensor_copy(pw[:, 1, 1, :], S["lbi"]))
                t4 = [sq[:, i // 2, (i % 2) * 384:(i % 2) * 384 + 4 * G].rearrange("p (n g) -> p n g", g=G) for i in range(4)]
                for n in (1, 2, 4):
                    by = [pw[:, i, n:n + 1, :].to_broadcast([P, n, G]) for i in range(2)]
                    cmul(pw[:, 0, n + 1:2 * n + 1, :], pw[:, 1, n + 1:2 * n + 1, :], pw[:, 0, 1:n + 1, :], pw[:, 1, 1:n + 1, :],
                         by[0], by[1], [q[:, 0:n, :] for q in t4])
                for i in range(2):
                    nc.vector.memset(qf[0:NS, i, SC + 1, :], 0.0)
                    nc.vector.memset(qf[NS:P, i, 0, :], 0.0)
                    nc.vector.tensor_copy(qf[0:NS, i, 0:SC + 1, :], pw[0:NS, i, :, :])
                    for pos in range(1, POS):
                        nc.vector.tensor_copy(qf[NS:P, i, pos, :], pw[NS:P, i, SC + 1 - pos, :])
                    nc.vector.tensor_copy(qr[NS:P, i, :, :], pw[NS:P, i, 0:SC, :])
                    for s in range(SC):
                        last = nc.vector.tensor_copy(qr[0:NS, i, s, :], pw[0:NS, i, SC - 1 - s, :])
                dve_chain(last)
                dve_chain(nc.vector.tensor_scalar(qf[:, 1, :, :], qf[:, 1, :, :], -1.0, None, ALU.mult))
                cmul(S["p2r"], S["p2i"], S["cos"], S["sin"], S["cos"], S["sin"], tmp)
                cmul(S["p4r"], S["p4i"], S["p2r"], S["p2i"], S["p2r"], S["p2i"], tmp)
                cmul(S["p2r"], S["p2i"], S["p4r"], S["p4i"], S["p4r"], S["p4i"], tmp)
                dve_chain(nc.vector.tensor_scalar(S["p2i"][NS:P], S["p2i"][NS:P], -1.0, None, ALU.mult))

            with nc.Block() as block:
                @block.sync
                def _(sp):
                    sp.dma_start(bin_[:, :, :, :], bc_in[0:2].rearrange("i p (g c) -> p i g c", c=GC)).then_inc(ld.sem, 16)
                    sp.dma_start(cc[:, :, :, :], bc_in[2:4].rearrange("i p (g c) -> p i g c", c=GC)).then_inc(ld.sem, 16)
                    sp.dma_start(wglr[:, :, :], wglr_in).then_inc(ld.sem, 16)

            def evac(a, g, i):
                if g == 0 and i < 4:
                    free(nc.scalar.activation(b1[:, i, :].rearrange("p (s j) -> p s j", s=SC),
                                              banks(2 * (i % 2)).rearrange("p (j s) -> p s j", s=SC), ACT.Copy))
                elif g == 0:
                    free(nc.scalar.activation(b1[:, i, :], banks(2 * (i % 2)), ACT.Copy, scale=float(DK ** -0.5) if i < 6 else 1.0))
                elif i < 4:
                    s, half = i // 2, i % 2
                    free(nc.scalar.activation(vt[:, 3 * half:3 * half + 3, s * UC:(s + 1) * UC],
                                              banks(2 * half).rearrange("p (j n) -> p j n", j=3), ACT.Copy))
                else:
                    free(nc.scalar.activation(b2[:, i, :], banks(2 * (i % 2)), ACT.Copy))
            def low_rank(pe, sp_):
                for k in range(KT):
                    for j, part in enumerate((sp_.in_h, sp_.in_l)):
                        st, en = k == 0 and j == 0, k == KT - 1 and j == 1
                        nc.tensor.matmul(ps[0:32, 4, :], wglr[:, k, :], part[:, k, 0:512].bitcast(F32), start=st, stop=en)
                        last = nc.tensor.matmul(ps[0:32, 5, 0:TS], wglr[:, k, :], part[:, k, 512:T].bitcast(F32), start=st, stop=en)
                last.then_inc(pc_in.sem, 1)
            vt = b2[:, 0:4, :].rearrange("p k t -> p (k t)").rearrange("p (j n) -> p j n", n=GH * DV)
            product_stage(x, ["ffff", "ttff"], evac, norm="mix0", evac_engine="scalar", dve_pre=dve_pre,
                          act_pre=act_pre, dve_post=dve_post, pe_post=low_rank)
            ld.base += 48
            pc_in.base += 3
            pc_out.base += 1
            prep.close()
            act = sb("s5act", [P, KT, T], on=local)
            rot = [sb(n, [P, G, NCH], on=s5mem) for n in ("rot_re", "rot_im")]
            dd = sb("dd", [GC, G, GC], on=s5mem)
            chunkmask = sb("chunkmask", [P, NCH], on=s5mem)

            ud, yd = dma["dma1"], dma["dma2"]
            s5 = ExitStack()
            u2b = sb("u_second", [P, T], on=s5)
            u2s = [a_.rearrange("p (g j) -> p g j", j=NCH) for a_ in (u2b[:, :], act[:, 0, :])]
            cls = [sb(f"cl{i}", [P, 2, GB, POS, GC], on=s5) for i in range(2)]
            pool_tmp = sb("pool_tmp", [P, 2, POS, GC], on=s5)
            vv = sb("vv", [P, 2, GB, P], on=s5)
            b1f = b1[:, 0:4, :].rearrange("p k t -> p (k t)")
            vT = b1f[:, 0:2 * GB * P].rearrange("p (i g c) -> p i g c", i=2, g=GB)
            mt = b1f[:, 2 * GB * P:3 * GB * P].rearrange("p (g c) -> p g c", g=GB)
            rt = act[0:GC, 2:5, :].rearrange("p k t -> p (k t)")[:, 0:GB * LAG * GC]\
                .rearrange("p (g n c) -> p g n c", g=GB, n=LAG)
            dec = act[:, 1, :]
            bp = [act[:, 2 + i, :] for i in range(2)]
            sp_ = [act[:, 4 + i, :] for i in range(2)]
            so = [act[:, 6 + i, :] for i in range(2)]
            tmpA = [rstd[:, :]] + [vv[:, 0, :, :].rearrange("p g c -> p (g c)")[:, 0:T],
                                   vv[:, 1, :, :].rearrange("p g c -> p (g c)")[:, 0:T], sq[:, 0, :]]
            ysb, yg = sq[:, 1, :], rstd[:, :]
            cl_ready = ev["ev14"]
            (t_v, vt_done, vt_ready, lag_done, rt_ready, m_loaded, bu_done, bu_read, st_ready, y_done, y_ready, y_e, y_e2,
             yg_ready) = (ev[f"ev{i}"] for i in range(14))

            def g3(a):
                return a.rearrange("p (g j) -> p g j", j=NCH)

            def dve_prep(v, b):
                tc = [vT[:, i, :, :].rearrange("p g c -> p (g c)") for i in range(2)]
                for h in range(2):
                    hs = slice(GB * b + 4 * h, GB * b + 4 * h + 4)
                    bb = [bbar[:, i, hs, :].unsqueeze(2).to_broadcast([P, 4, SC, GC]) for i in range(2)]
                    qq = [qr[:, i, :, hs].rearrange("p n g -> p g n").unsqueeze(3).to_broadcast([P, 4, SC, GC])
                          for i in range(2)]
                    ta = [t_[:, 512 * j:512 * j + 4 * P].rearrange("p (g n c) -> p g n c", g=4, n=SC)
                          for t_ in tc for j in range(2)]
                    o = [vv[:, i, 4 * h:4 * h + 4, :].rearrange("p g (n c) -> p g n c", n=SC) for i in range(2)]
                    cmul(o[0], o[1], bb[0], bb[1], qq[0], qq[1], ta, done=t_v if h else None)

            def pool_prep(b):
                for q in range(0, GB, 2):
                    cb = [cc[:, i, GB * b + q:GB * b + q + 2, :].unsqueeze(2).to_broadcast([P, 2, POS, GC]) for i in range(2)]
                    qb = [qf[:, i, :, GB * b + q:GB * b + q + 2].rearrange("p n g -> p g n").unsqueeze(3)
                          .to_broadcast([P, 2, POS, GC]) for i in range(2)]
                    o = [cls[b % 2][:, i, q:q + 2] for i in range(2)]
                    for i, op in ((0, ALU.add), (1, ALU.subtract)):
                        nc.gpsimd.tensor_tensor(o[i], cb[0], qb[i], ALU.mult)
                        pool_chain(nc.gpsimd.tensor_tensor(pool_tmp[:, :, :, :], cb[1], qb[1 - i], ALU.mult))
                        last = nc.gpsimd.tensor_tensor(o[i], o[i], pool_tmp[:, :, :, :], op)
                        if q == GB - 2 and i == 1:
                            last.then_inc(cl_ready.sem, 1)
                        else:
                            pool_chain(last)

            def pe_prep(pe, b, y_left):
                pe.wait_ge(t_v.sem, t_v.at(1))
                for i in range(2):
                    for g in range(GB):
                        last = nc.tensor.transpose(banks(2 * i, 1024)[:, g * P:(g + 1) * P], vv[:, i, g, :], ident)
                last.then_inc(vt_done.sem, 1)
                pe.wait_ge(cl_ready.sem, cl_ready.at(1))
                if y_left:
                    pe.wait_ge(y_ready.sem, y_ready.at(1))
                for g in range(GB):
                    for z in range(2):
                        rows = slice(NS * z, NS * z + NS)
                        lo = 0 if z == 0 else 2
                        for i in range(2):
                            last = nc.tensor.matmul(banks(4 + 2 * z, 1024)[0:GC, g * P:(g + 1) * P],
                                                    bbar[rows, i, GB * b + g, :],
                                                    cls[b % 2][rows, i, g, lo:lo + SC, :].rearrange("p n c -> p (n c)"),
                                                    start=(i == 0), stop=(i == 1))

            def act_prep(a):
                a.wait_ge(vt_done.sem, vt_done.at(1))
                for i in range(2):
                    nc.scalar.activation(vT[:, i, :, :].rearrange("p g c -> p (g c)"), banks(2 * i, 1024), ACT.Copy)

            def load_u(sp, b):
                src = u_dram[P * b:P * b + P].rearrange("(g c) s j -> s c g j", c=GC)
                for s in range(SC):
                    sp.dma_start(u2s[b % 2][GC * s:GC * s + GC], src[s]).then_inc(ld.sem, 16)

            def close_prep():
                for s_ in (t_v, vt_done, cl_ready):
                    s_.base += 1
                ld.base += 16 * SC

            with nc.Block() as block:
                @block.sync
                def _(sp):
                    sp.dma_start(u_dram.rearrange("(k p) s j -> p k (s j)", p=P), b1[:, 0:4, :]).then_inc(ud.sem, 16)
                    lo = TAB["chunkmask"][0]
                    sp.dma_start(chunkmask[:, :], tab_in[:, lo:lo + NCH]).then_inc(ld.sem, 16)
                    sp.wait_ge(ud.sem, ud.at(16))
                    sp.wait_ge(ld.sem, ld.at(16))
                    ld.base += 16
                    load_u(sp, 0)
                    sp.wait_ge(ld.sem, ld.at(16 * SC))

                @block.scalar
                def _(a):
                    nc.scalar.activation(lr[:, :], banks(4)[0:32], ACT.Copy).then_inc(y_ready.sem, 1)
                    act_prep(a)

                @block.tensor
                def _(pe):
                    pe_prep(pe, 0, True)

                @block.gpsimd
                def _(g):
                    pool_chain.start(g)
                    pool_prep(0)
                    pool_chain.close()

                @block.vector
                def _(v):
                    dve_chain.start(v)
                    tmp = [S[f"t{i}"] for i in range(4)]
                    nc.vector.memset(rot[0][:, :, 0:1], 1.0)
                    dve_chain(nc.vector.memset(rot[1][:, :, 0:1], 0.0))
                    n, pr, pi, nr_, ni_ = 1, S["p2r"], S["p2i"], S["p4r"], S["p4i"]
                    while n < NCH:
                        m = min(n, NCH - n)
                        tw = [act[:, 2 * i:2 * i + 2, :].rearrange("p k t -> p (k t)")[:, 0:G * m]
                              .rearrange("p (g j) -> p g j", g=G) for i in range(4)]
                        cmul(rot[0][:, :, n:n + m], rot[1][:, :, n:n + m], rot[0][:, :, 0:m], rot[1][:, :, 0:m],
                             bc_g(pr, m), bc_g(pi, m), tw)
                        cmul(nr_, ni_, pr, pi, pr, pi, tmp)
                        pr, pi, nr_, ni_ = nr_, ni_, pr, pi
                        n *= 2
                    nc.vector.tensor_tensor(dd[:, :, :], pcol("s5d")[0:GC].unsqueeze(2).to_broadcast([GC, G, GC]),
                                            ident[0:GC, 0:GC].unsqueeze(1).to_broadcast([GC, G, GC]), ALU.mult)
                    nc.vector.memset(so[0], 0.0)
                    nc.vector.memset(so[1], 0.0)
                    v.wait_ge(ud.sem, ud.at(16))
                    dve_prep(v, 0)
                    dve_chain.close()
            ud.base += 16
            y_ready.base += 1
            close_prep()


            for b in range(NB):
                gs = slice(GB * b, GB * b + GB)
                u2, cl = u2s[b % 2], cls[b % 2]
                more = b + 1 < NB
                with nc.Block() as block:
                    @block.sync
                    def _(sp):
                        sp.wait_ge(rt_ready.sem, rt_ready.at(1))
                        for s in range(SC):
                            sp.dma_start(mt[GC * s:GC * s + GC, :, :],
                                         rt[:, :, SC - 1 - s:2 * SC - 1 - s, :].rearrange("c g t d -> c g (t d)"))\
                                .then_inc(m_loaded.sem, 16)
                        if more:
                            load_u(sp, b + 1)
                        sp.wait_ge(yg_ready.sem, yg_ready.at(1))
                        dst = y_dram[P * b:P * b + P].rearrange("(g c) t j -> t c g j", c=GC)
                        for s in range(SC):
                            sp.dma_start(dst[s], g3(yg)[GC * s:GC * s + GC]).then_inc(yd.sem, 16)
                        sp.wait_ge(yd.sem, yd.at(16 * SC))
                        if more:
                            sp.wait_ge(ld.sem, ld.at(16 * SC))

                    @block.gpsimd
                    def _(g):
                        if more:
                            pool_chain.start(g)
                            pool_prep(b + 1)
                            pool_chain.close()

                    @block.vector
                    def _(v):
                        dve_chain.start(v)
                        lagf = banks(4, 1024)[0:GC].rearrange("c (g n d) -> c g n d", g=GB, n=SC)
                        lagb = banks(6, 1024)[0:GC].rearrange("c (g n d) -> c g n d", g=GB, n=SC)
                        nc.vector.tensor_copy(rt[:, :, SC:LAG, :], lagf[:, :, 1:SC, :])
                        dve_chain(nc.vector.tensor_copy(rt[:, :, 0:SC, :], lagb))
                        dve_chain(nc.vector.tensor_tensor(rt[:, :, SC - 1, :], rt[:, :, SC - 1, :], lagf[:, :, 0, :], ALU.add))
                        nc.vector.tensor_tensor(rt[:, :, SC - 1, :], rt[:, :, SC - 1, :], dd[:, gs, :], ALU.add).then_inc(rt_ready.sem, 1)
                        dve_chain(nc.vector.tensor_tensor(g3(dec), bc_g(S["r8"][:, gs], NCH),
                                                          chunkmask[:, :].unsqueeze(1).to_broadcast([P, GB, NCH]), ALU.mult))
                        v.wait_ge(bu_done.sem, bu_done.at(1))
                        bur = banks(0, 1024).rearrange("p (g j) -> p g j", j=P)[:, :, 0:NCH]
                        bui = banks(2, 1024).rearrange("p (g j) -> p g j", j=P)[:, :, 0:NCH]
                        er, ei = rot[0][:, gs, :], rot[1][:, gs, :]
                        v.wait_ge(m_loaded.sem, m_loaded.at(16 * SC))
                        cmul(g3(bp[0]), g3(bp[1]), bur, bui, er, ei, [g3(t_) for t_ in tmpA], conj=True)
                        for i in range(2):
                            nc.vector.tensor_tensor_scan(out=sp_[i][0:NS], data0=dec[0:NS], data1=bp[i][0:NS], initial=0.0,
                                                         op0=ALU.mult, op1=ALU.add)
                            ins = nc.vector.tensor_tensor_scan(out=sp_[i][NS:P, ::-1], data0=dec[NS:P, ::-1],
                                                               data1=bp[i][NS:P, ::-1], initial=0.0, op0=ALU.mult, op1=ALU.add)
                        dve_chain(ins)
                        nc.vector.tensor_tensor(g3(tmpA[0]), g3(sp_[0]), er, ALU.mult)
                        nc.vector.tensor_tensor(g3(tmpA[1]), g3(sp_[1]), ei, ALU.mult)
                        nc.vector.tensor_tensor(g3(tmpA[2]), g3(sp_[0]), ei, ALU.mult)
                        dve_chain(nc.vector.tensor_tensor(g3(tmpA[3]), g3(sp_[1]), er, ALU.mult))
                        for i, op in ((0, ALU.subtract), (1, ALU.add)):
                            o, a_, b_ = g3(so[i]), g3(tmpA[2 * i]), g3(tmpA[2 * i + 1])
                            nc.vector.tensor_tensor(o[0:NS, :, 1:NCH], a_[0:NS, :, 0:NCH - 1], b_[0:NS, :, 0:NCH - 1], op)
                            dve_chain(nc.vector.tensor_tensor(o[NS:P, :, 0:NCH - 1], a_[NS:P, :, 1:NCH], b_[NS:P, :, 1:NCH], op))
                            nc.vector.memset(o[0:NS, :, TP // SC:TP // SC + 1], 0.0)
                            last = nc.vector.memset(o[NS:P, :, TP // SC - 1:TP // SC], 0.0)
                        last.then_inc(st_ready.sem, 1)
                        if more:
                            dve_prep(v, b + 1)
                        v.wait_ge(y_ready.sem, y_ready.at(1))
                        t_ = tmpA[3]
                        tt(t_, ysb, ysb, ALU.mult)
                        ts(t_, t_, 0.044715, 1.0, ALU.mult, ALU.add)
                        nc.vector.tensor_tensor(t_, t_, ysb, ALU.mult).then_inc(y_e.sem, 1)
                        v.wait_ge(y_e2.sem, y_e2.at(1))
                        ts(t_, t_, 0.5, 0.5, ALU.mult, ALU.add)
                        nc.vector.tensor_tensor(yg, t_, ysb, ALU.mult).then_inc(yg_ready.sem, 1)
                        dve_chain.close()

                    @block.tensor
                    def _(pe):
                        for i in range(2):
                            for g in range(GB):
                                last = nc.tensor.matmul(banks(2 * i, 1024)[:, g * P:g * P + NCH], vT[:, i, g, :], u2[:, g, :],
                                                        start=True, stop=True)
                        last.then_inc(bu_done.sem, 1)
                        pe.wait_ge(m_loaded.sem, m_loaded.at(16 * SC))
                        pe.wait_ge(st_ready.sem, st_ready.at(1))
                        for g in range(GB):
                            o = banks(4, 1024)[:, g * P:g * P + NCH]
                            nc.tensor.matmul(o, mt[:, g, :], u2[:, g, :], start=True, stop=False)
                            for i in range(2):
                                last = nc.tensor.matmul(o, cl[:, i, g, 1:SC + 1, :].rearrange("p n c -> p (n c)"),
                                                        g3(so[i])[:, g, :], start=False, stop=(i == 1))
                        last.then_inc(y_done.sem, 1)
                        if more:
                            pe_prep(pe, b + 1, True)

                    @block.scalar
                    def _(a):
                        a.wait_ge(y_done.sem, y_done.at(1))
                        nc.scalar.activation(g3(ysb), banks(4, 1024).rearrange("p (g j) -> p g j", j=P)[:, :, 0:NCH], ACT.Copy)\
                            .then_inc(y_ready.sem, 1)
                        a.wait_ge(y_e.sem, y_e.at(1))
                        nc.scalar.activation(tmpA[3], tmpA[3], ACT.Tanh, scale=math.sqrt(2.0 / math.pi)).then_inc(y_e2.sem, 1)
                        if more:
                            act_prep(a)
                for s_ in (rt_ready, bu_done, st_ready, y_done, y_ready, y_e, y_e2, yg_ready):
                    s_.base += 1
                m_loaded.base += 16 * SC
                yd.base += 16 * SC
                if more:
                    close_prep()
            s5.close()

            glu = ExitStack()
            wglu = sb("wglu_sb", [P, 4, 512], on=glu)
            et = sb("glu_t", [P, 2, T], on=glu)
            with nc.Block() as block:
                @block.sync
                def _(sp):
                    sp.dma_start(b1[:, 0:4, :], y_dram.rearrange("(k p) s j -> p k (s j)", p=P)).then_inc(ld.sem, 16)
                    sp.dma_start(wglu[:, :, :], wglu_in).then_inc(ld.sem, 16)

                @block.tensor
                def _(pe):
                    pe.wait_ge(ld.sem, ld.at(32))
                    for o in range(4):
                        if o >= 2:
                            pe.wait_ge(vt_ready.sem, vt_ready.at(o - 1))
                        for k in range(4):
                            nc.tensor.matmul(ps[:, 2 * (o % 2), :], wglu[:, k, o * P:(o + 1) * P], b1[:, k, 0:512],
                                             start=(k == 0), stop=(k == 3))
                            last = nc.tensor.matmul(ps[:, 2 * (o % 2) + 1, 0:TS], wglu[:, k, o * P:(o + 1) * P], b1[:, k, 512:T],
                                                    start=(k == 0), stop=(k == 3))
                        last.then_inc(vt_done.sem, 1)

                @block.scalar
                def _(a):
                    for o in range(4):
                        a.wait_ge(vt_done.sem, vt_done.at(o + 1))
                        if o >= 2:
                            a.wait_ge(st_ready.sem, st_ready.at(o - 1))
                        nc.scalar.activation(et[:, o % 2, :], banks(2 * (o % 2)), ACT.Tanh, scale=0.5).then_inc(vt_ready.sem, 1)

                @block.vector
                def _(v):
                    dve_chain.start(v)
                    for o in range(4):
                        v.wait_ge(vt_ready.sem, vt_ready.at(o + 1))
                        e_ = et[:, o % 2, :]
                        ts(e_, e_, 0.5, 0.5, ALU.mult, ALU.add)
                        nc.vector.tensor_tensor(act[:, o, :].rearrange("p (j s) -> p s j", s=SC),
                                                e_.rearrange("p (s j) -> p s j", s=SC),
                                                b1[:, o, :].rearrange("p (s j) -> p s j", s=SC), ALU.mult).then_inc(st_ready.sem, 1)
                    v.wait_ge(st_ready.sem, st_ready.at(4))
                    dve_chain.close()
            ld.base += 32
            for s_ in (vt_done, vt_ready, st_ready):
                s_.base += 4
            glu.close()
            s5mem.close()

            gl = ExitStack()
            b3 = sb("gl_b3", [P, KT, T], on=gl)
            masks = sb("masks", [P, 2 * P], on=gl)
            wg = sb("wg", [32, 2, 256], on=gl)
            gm = sb("gm", [P, 2, T], on=gl)
            gt = b1[:, 0:4, :]
            gt2 = sb("gl_gt2", [P, T], on=gl)
            gts = [[gt[:, i, :] for i in range(4)], [sq[:, 0, :], sq[:, 1, :], rstd[:, :], gt2[:, :]]]
            qrel = b3[:, 5:7, :]
            krel = sb("krel", [P, 2, T], on=gl)
            ko2 = sb("gl_ko2", [P, 2, T], on=gl)
            ko = [b3[:, 7, :], ko2[:, 0, :]]
            koT = [a_.rearrange("p (j d) -> p j d", d=P) for a_ in (b3[:, 4, :], ko2[:, 1, :])]
            qout = sb("qout", [P, 2, T], on=gl)
            sprev = [b3[:, 2 * z:2 * z + 2, :].rearrange("p k t -> p (k t)").rearrange("p (c d) -> p c d", d=DV) for z in range(2)]
            scT = sb("scT", [P, 2, T], on=gl)
            decay = sb("decay", [P, 2, NC12], on=gl)
            (z_done, z_read, e_in, e_out, l_out, d_in, d_out, ko_ready, kt_done, kt_ready, kv_done, s_ready, sc_done, sc_ready,
             oo_done, oo_read) = (ev[f"ev{i}"] for i in range(16))

            def kv_ps(z, c):
                i = z * (NC12 // 2) + c // 2
                b = 2 + 3 * (c % 2) + i // 4
                return ps[:, b, (i % 4) * DV:(i % 4) * DV + DV]

            def c3(a):
                return a.rearrange("p (c i) -> p c i", i=CH)
            with nc.Block() as block:
                @block.sync
                def _(sp):
                    sp.dma_start(wg[:, :, :], wgate_in).then_inc(ld.sem, 16)
                    lo = TAB["masks"][0]
                    sp.dma_start(masks[:, :], tab_in[:, lo:lo + 2 * P]).then_inc(ld.sem, 16)
                    sp.wait_ge(ld.sem, ld.at(32))

                @block.scalar
                def _(a):
                    nc.scalar.preload_act_table_set("natural_log_exp_and_others")

                @block.gpsimd
                def _(g):
                    nc.gpsimd.memset(gm[:, :, :], 1.0).then_inc(pchain.sem, 1)
                    g.wait_ge(pchain.sem, pchain.at(1))
                    nc.gpsimd.memset(c3(gm[:, 0, :])[:, :, 0:1], 0.0)
                    nc.gpsimd.memset(c3(gm[:, 1, :])[:, :, CH - 1:CH], 0.0)
                    for z in range(2):
                        nc.gpsimd.memset(sprev[z][:, 0 if z == 0 else TP // CH - 1, :], 0.0)
                        nc.gpsimd.memset(sprev[z][:, TP // CH if z == 0 else NC12 - 1, :], 0.0)
                    nc.gpsimd.memset(scT[:, :, :], 0.0).then_inc(pchain.sem, 1)
                    g.wait_ge(pchain.sem, pchain.at(2))
            pchain.base += 2
            ld.base += 32
            for t in range(2):
                with nc.Block() as block:
                    @block.tensor
                    def _(pe):
                        for z in range(2):
                            nc.tensor.matmul(ps[:, 2 * z, :], wg[:, z, t * P:(t + 1) * P], lr[:, 0:512], start=True, stop=True)
                            nc.tensor.matmul(ps[:, 2 * z + 1, 0:TS], wg[:, z, t * P:(t + 1) * P], lr[:, 512:T], start=True, stop=True)\
                                .then_inc(z_done.sem, 1)
                        for z in range(2):
                            pe.wait_ge(ko_ready.sem, ko_ready.at(z + 1))
                            if z == 1:
                                pe.wait_ge(kt_ready.sem, kt_ready.at(1))
                            for j in range(TT):
                                last = nc.tensor.transpose(banks(0)[:, j * P:(j + 1) * P], ko[z][:, j * P:(j + 1) * P], ident)
                            last.then_inc(kt_done.sem, 1)
                        for z in range(2):
                            pe.wait_ge(kt_ready.sem, kt_ready.at(z + 1))
                            for c in range(NC12):
                                rows = slice(CH * (c % 2), CH * (c % 2) + CH)
                                for hh in range(2):
                                    h = 2 * t + hh
                                    last = nc.tensor.matmul(kv_ps(z, c)[DK * hh:DK * hh + DK],
                                                            koT[z][rows, c // 2, DK * hh:DK * hh + DK],
                                                            vt[rows, c // 2, h * DV:(h + 1) * DV], start=True, stop=True)
                        last.then_inc(kv_done.sem, 1)

                    @block.vector
                    def _(v):
                        dve_chain.start(v)
                        for z in range(2):
                            g_, cum, ta, tb = gts[z]
                            v.wait_ge(z_done.sem, z_done.at(z + 1))
                            col = COLS["bgate"][0] + 2 * z + t
                            dve_chain(nc.vector.tensor_scalar(g_, banks(2 * z), par[:, col:col + 1], None, ALU.add))
                            ts(ta, g_, -1.0, None, ALU.mult)
                            nc.vector.tensor_tensor(ta, ta, g_, ALU.min).then_inc(e_in.sem, 1)
                        for z in range(2):
                            g_, cum, ta, tb = gts[z]
                            v.wait_ge(e_out.sem, e_out.at(z + 1))
                            dve_chain(nc.vector.scalar_tensor_tensor(g_, g_, 0.0, ta, ALU.min, ALU.subtract))
                            o = slice(None, None, 1 if z == 0 else -1)
                            dve_chain(nc.vector.tensor_tensor_scan(out=cum[:, o], data0=gm[:, z, o], data1=g_[:, o], initial=0.0,
                                                                   op0=ALU.mult, op1=ALU.add))
                            ref = CH // 2 - 1 if z == 0 else CH // 2
                            end = CH - 1 if z == 0 else 0
                            refs = c3(cum)[:, :, ref:ref + 1].to_broadcast([P, NC12, CH])
                            ends = c3(cum)[:, :, end:end + 1].to_broadcast([P, NC12, CH])
                            nc.vector.tensor_tensor(c3(ta), c3(cum), refs, ALU.subtract)
                            nc.vector.tensor_tensor(c3(tb), ends, c3(cum), ALU.subtract).then_inc(d_in.sem, 1)
                        for z in range(2):
                            v.wait_ge(d_out.sem, d_out.at(z + 1))
                            nc.vector.tensor_tensor(ko[z], b1[:, 6 + t, :], gts[z][3], ALU.mult).then_inc(ko_ready.sem, 1)
                            nc.vector.tensor_tensor(krel[:, z, :], b1[:, 6 + t, :], gts[z][0], ALU.mult)
                        v.wait_ge(kv_done.sem, kv_done.at(1))
                        runs = []
                        for lo, hi in ((0, TP // CH), (TP // CH, NC12)):
                            for z in range(2):
                                cs = list(range(lo, hi))[::1 if z == 0 else -1]
                                runs.append([(z, c, nx) for c, nx in zip(cs[:-1], cs[1:])])
                        for n in range(max(map(len, runs))):
                            for z, c, nx in [r[n] for r in runs if n < len(r)]:
                                last = nc.vector.scalar_tensor_tensor(
                                    sprev[z][:, nx, :], sprev[z][:, c, :], decay[:, z, c:c + 1],
                                    kv_ps(z, c), ALU.mult, ALU.add)
                            dve_chain(last)
                        dve_chain.close()

                    @block.gpsimd
                    def _(g):
                        for z in range(2):
                            g.wait_ge(d_out.sem, d_out.at(z + 1))
                            nc.gpsimd.tensor_tensor(qout[:, z, :], b1[:, 4 + t, :], gts[z][1], ALU.mult)
                            nc.gpsimd.tensor_tensor(qrel[:, z, :], b1[:, 4 + t, :], gts[z][2], ALU.mult)

                    @block.scalar
                    def _(a):
                        for z in range(2):
                            a.wait_ge(e_in.sem, e_in.at(z + 1))
                            nc.scalar.activation(gts[z][2], gts[z][2], ACT.Exp).then_inc(achain.sem, 1)
                        for z in range(2):
                            a.wait_ge(achain.sem, achain.at(z + 1))
                            nc.scalar.activation(gts[z][2], gts[z][2], ACT.Ln, bias=pcol("one")).then_inc(e_out.sem, 1)
                        for z in range(2):
                            g_, cum, ta, tb = gts[z]
                            a.wait_ge(d_in.sem, d_in.at(z + 1))
                            cumends = c3(cum)[:, :, CH - 1 if z == 0 else 0]
                            nc.scalar.activation(decay[:, z, :], cumends, ACT.Exp, scale=1.0 / 16)
                            nc.scalar.activation(g_, ta, ACT.Exp, scale=-1.0 / 16).then_inc(achain.sem, 1)
                            nc.scalar.activation(tb, tb, ACT.Exp, scale=1.0 / 16)
                            a.wait_ge(achain.sem, achain.at(3 + z))
                            nc.scalar.activation(ta, ta, ACT.Exp, scale=1.0 / 16)
                            nc.scalar.activation(cum, cum, ACT.Exp, scale=1.0 / 16).then_inc(d_out.sem, 1)
                        for z in range(2):
                            a.wait_ge(kt_done.sem, kt_done.at(z + 1))
                            nc.scalar.activation(koT[z].rearrange("p j d -> p (j d)"), banks(0), ACT.Copy).then_inc(kt_ready.sem, 1)
                for s_ in (z_done, e_in, e_out, d_in, d_out, ko_ready, kt_done, kt_ready):
                    s_.base += 2
                kv_done.base += 1
                achain.base += 4
                with nc.Block() as block:
                    @block.tensor
                    def _(pe):
                        for hh in range(2):
                            h = 2 * t + hh
                            rows = slice(DK * hh, DK * hh + DK)
                            if hh == 1:
                                pe.wait_ge(sc_ready.sem, sc_ready.at(1))
                            for z in range(2):
                                for j in range(TT):
                                    js = slice(j * P, (j + 1) * P)
                                    last = nc.tensor.matmul(banks(2 * z)[:, js], krel[rows, z, js], qrel[rows, z, js],
                                                            start=True, stop=True)
                            last.then_inc(sc_done.sem, 1)
                            pe.wait_ge(sc_ready.sem, sc_ready.at(hh + 1))
                            ob = banks(4 + 2 * hh)
                            for j in range(TT):
                                js = slice(j * P, (j + 1) * P)
                                for z in range(2):
                                    nc.tensor.matmul(ob[:, js], vt[:, j, h * DV:(h + 1) * DV], scT[:, z, js],
                                                     start=(z == 0), stop=False, skip_group_check=True)
                                for z in range(2):
                                    for c in (2 * j, 2 * j + 1):
                                        cs = slice(CH * c, CH * c + CH)
                                        last = nc.tensor.matmul(ob[:, cs], sprev[z][rows, c, :], qout[rows, z, cs],
                                                                start=False, stop=(z == 1), skip_group_check=True)
                            last.then_inc(oo_done.sem, 1)

                    @block.vector
                    def _(v):
                        for hh in range(2):
                            v.wait_ge(sc_done.sem, sc_done.at(hh + 1))
                            if hh == 1:
                                v.wait_ge(oo_done.sem, oo_done.at(1))
                            for z in range(2):
                                mk = masks[:, P * z:P * z + P].bitcast(mybir.dt.uint32).unsqueeze(1).to_broadcast([P, TT, P])
                                last = nc.vector.copy_predicated(scT[:, z, :].rearrange("p (j i) -> p j i", i=P), mk,
                                                                 banks(2 * z).rearrange("p (j i) -> p j i", i=P))
                            last.then_inc(sc_ready.sem, 1)

                    @block.scalar
                    def _(a):
                        for hh in range(2):
                            a.wait_ge(oo_done.sem, oo_done.at(hh + 1))
                            nc.scalar.activation(act[:, 4 + 2 * t + hh, :], banks(4 + 2 * hh), ACT.Copy)
                for s_ in (sc_done, sc_ready, oo_done):
                    s_.base += 2
            with nc.Block() as block:
                @block.scalar
                def _(a):
                    for h in range(GH):
                        nc.scalar.activation(gt[:, h, :], b2[:, 4 + h, :], ACT.Tanh, scale=0.5).then_inc(e_in.sem, 1)

                @block.vector
                def _(v):
                    dve_chain.start(v)
                    for h in range(GH):
                        v.wait_ge(e_in.sem, e_in.at(h + 1))
                        ts(gt[:, h, :], gt[:, h, :], 0.5, 0.5, ALU.mult, ALU.add)
                        tt(b2[:, 4 + h, :], b2[:, 4 + h, :], gt[:, h, :], ALU.mult)
                    dve_chain.close()
            e_in.base += GH

            def gate(v, h):
                v.wait_ge(normed.sem, normed.at(h + 1))
                nc.vector.tensor_tensor(b1[:, 4 + h, :], b1[:, 4 + h, :], b2[:, 4 + h, :], ALU.mult)
            with nc.Block() as block:
                @block.scalar
                def _(a):
                    nc.scalar.preload_act_table_set("natural_log_exp_and_others")
                    for k in range(4):
                        nc.scalar.activation(b1[:, k, :], act[:, k, :], ACT.Copy)
            gl.close()
            head_norm_stage([([act[:, 4 + h, :]], [pcol("gnorm")], [b1[:, 4 + h, :]]) for h in range(GH)], ones, DV, extra=gate)
            local.close()
            product_stage(b1, ["ffff"], add_residual)
            outer.close()
        s5_gla()
        cross(0)
        mlp(0)
        diff_attention()
        cross(1)
        mlp(1)

        with nc.Block() as block:
            @block.sync
            def _(sp):
                sp.dma_start(out.rearrange("(k p) t -> p k t", p=P), x[:, :, :]).then_inc(dma["dma1"].sem, 16)
                sp.wait_ge(dma["dma1"].sem, dma["dma1"].at(16))


def kernel(**inputs):
    import numpy as _np
    import concourse.bacc as _bacc
    from concourse import mybir as _mybir
    from concourse.bass_utils import run_bass_kernel_spmd as _run

    w = {k: _np.asarray(v) for k, v in inputs.items()}

    def cols(v):
        return v.reshape(-1, P).T

    par = _np.zeros((P, NPAR), _np.float32)

    def put(name, v):
        a, n = COLS[name]
        par[:v.shape[0], a:a + n] = v

    for layer in range(DEPTH):
        for short, name in (("mix", "norm_mix"), ("cross", "norm_cross"), ("mem", "norm_mem"), ("mlp", "norm_mlp"),
                            ("xq", "x_q_norm"), ("xk", "x_k_norm")):
            put(f"{short}{layer}", cols(w[name][layer]))
    for name, src in (("dq", "diff_q_norm"), ("dk", "diff_k_norm")):
        put(name, _np.concatenate([w[src][0], w[src][0]])[:, None])
    put("dnorm", w["diff_norm"][0][:, None])
    put("gnorm", w["gla_norm"][0][:, None])
    put("lq", _np.stack([w["diff_lambda_q1"][0], w["diff_lambda_q2"][0]], 1))
    put("lk", _np.stack([w["diff_lambda_k1"][0], w["diff_lambda_k2"][0]], 1))
    put("bgate", w["gla_b_gate"][0].reshape(2, 2, P).transpose(2, 0, 1).reshape(P, 4))
    put("lre", w["s5_lambda_re"][0].transpose(0, 2, 1).reshape(P, G))
    put("lim", w["s5_lambda_im"][0].transpose(0, 2, 1).reshape(P, G))
    put("lstep", _np.repeat(w["s5_log_step"][0], NS, axis=0))
    put("s5d", w["s5_d"][0].T)
    put("eps", _np.full((P, 1), EPS, _np.float32))
    put("one", _np.ones((P, 1), _np.float32))
    mask = _np.ones((P, NCH), _np.float32)
    mask[:NS, [0, TP // SC]] = 0
    mask[NS:, [TP // SC - 1, NCH - 1]] = 0
    put("ident", _np.eye(P, dtype=_np.float32))
    put("ones", _np.ones((P, P), _np.float32))
    put("ones64", _np.kron(_np.eye(2, dtype=_np.float32), _np.ones((64, 64), _np.float32)))
    dist = (_np.abs(_np.arange(P)[:, None] + 384 - _np.arange(DIST)[None, :]).astype(_np.float32))

    b_ri = [w[n][0].transpose(0, 2, 1, 3).reshape(P, G * GC) for n in ("s5_b_re", "s5_b_im")]
    c_ri = [w[n][0].transpose(0, 3, 1, 2).reshape(P, G * GC) for n in ("s5_c_re", "s5_c_im")]
    bc = _np.stack(b_ri + c_ri)

    def units(a):
        n = a.shape[1] // UC
        return a.reshape(KT, P, n, UC).transpose(2, 1, 0, 3).reshape(n, P, KT * UC)

    ev = w["ev_w_in"][0]
    u_, q_, k_, v_, og_, glr_ = _np.split(ev, [512, 768, 1024, 1536, 2048], axis=1)
    parts = [units(_np.concatenate([u_, q_, k_], 1)), units(_np.concatenate([v_, og_], 1)), units(w["ev_w_out"][0])]

    def tail(layer):
        r = [units(w["x_w_kv"][layer]), units(w["x_w_q"][layer]), units(w["x_w_o"][layer])]
        for fb in range(FB):
            r.append(units(w["mlp_w1"][layer][:, fb * 1024:(fb + 1) * 1024]))
            r.append(units(w["mlp_w2"][layer][fb * 1024:(fb + 1) * 1024]))
        return r

    parts += tail(0) + [units(w["od_w_in"][0]), units(w["od_w_out"][0])] + tail(1)
    wgate = _np.zeros((2 * 16, 2, 256), _np.float32)
    for z in range(2):
        wgate[16 * z:16 * z + 16, z] = w["gla_w_gate"][0][z]
    j, i = _np.arange(P)[:, None], _np.arange(P)[None, :]
    same = j // CH == i // CH
    tri = _np.concatenate([same & (j <= i), same & (j >= i)], 1).astype(_np.float32)

    arrays = {
        "params": par,
        "x_in": _np.concatenate([w["x_prompt"][0], w["x_sample"][0]], 0).T,
        "mem_in": _np.concatenate([w["mem_prompt"][0], w["mem_sample"][0]], 0).T,
        "wstream": _np.concatenate(parts, 0),
        "wglr": glr_.reshape(KT, P, 32).transpose(1, 0, 2),
        "wglu": w["s5_w_glu"][0].reshape(4, P, 512).transpose(1, 0, 2),
        "wgate": wgate,
        "bc": bc,
        "tab": _np.concatenate([dist, tri, mask], 1),
    }
    arrays = {k: _np.ascontiguousarray(v) for k, v in arrays.items()}
    nc = _bacc.Bacc("TRN2", target_bir_lowering=False, num_devices=1)
    args = [nc.dram_tensor(k, a.shape, _mybir.dt.from_np(a.dtype), kind="ExternalInput").ap() for k, a in arrays.items()]
    scratch = [nc.dram_tensor(n, (512, SC, NCH), F32, kind="Internal").ap() for n in ("u_scratch", "y_scratch")]
    out = nc.dram_tensor("y_out", (D, T), F32, kind="ExternalOutput").ap()
    build(nc, *args, *scratch, out)
    r = _run(nc, [arrays], core_ids=[0])
    y = r.results[0]["y_out"].T
    return (y[None, :TP], y[None, TP:])
```
